# Optimizing a Trainium2 kernel written in Bass

```python
import jax, jax.numpy as jnp
from jax import lax
import numpy as np
import math

D_MODEL = 1024
BATCH = 1
SEQ = 512
DEPTH = 2

N_A_LAYERS = DEPTH // 2
N_B_LAYERS = DEPTH - N_A_LAYERS
EPS = 1e-6

CHUNK = 128
A_WIDTH = 2 * D_MODEL
A_GROUP_WIDTH = 256
A_GROUPS = A_WIDTH // A_GROUP_WIDTH

HEAD_DIM = 128
DILATED_GROUPS = ((128, 1), (512, 4), (2048, 16))
N_GROUPS = len(DILATED_GROUPS)
Q_HEADS_PER_GROUP = D_MODEL // HEAD_DIM
KV_HEADS_PER_GROUP = 2
Q_PER_KV = Q_HEADS_PER_GROUP // KV_HEADS_PER_GROUP
N_Q_HEADS = N_GROUPS * Q_HEADS_PER_GROUP
N_KV_HEADS = N_GROUPS * KV_HEADS_PER_GROUP
B_WIDTH = Q_HEADS_PER_GROUP * HEAD_DIM
BAND = 128


def rms_norm(x, g):
    xf = x.astype(jnp.float32)
    y = xf * lax.rsqrt(jnp.mean(xf * xf, axis=-1, keepdims=True) + EPS)
    return (y * g.astype(jnp.float32)).astype(x.dtype)

def ada_mod(c, w, b, n):
    h = jax.nn.silu(c) @ w + b
    return jnp.split(h[:, None, :], n, axis=-1)

def alibi_slopes():
    h = jnp.arange(1, N_Q_HEADS + 1, dtype=jnp.float32)
    return jnp.exp2(-8.0 * h / N_Q_HEADS)

def to_dilated(t, d):
    b, s = t.shape[:2]
    rest = t.shape[2:]
    span = d * BAND
    sp = -(-s // span) * span
    t = jnp.pad(t, [(0, 0), (0, sp - s)] + [(0, 0)] * len(rest))
    t = t.reshape((b, sp // d, d) + rest)
    t = jnp.swapaxes(t, 1, 2)
    return t.reshape((b, d, sp // span, BAND) + rest)

def from_dilated(t, s):
    b, d, nb = t.shape[:3]
    rest = t.shape[4:]
    t = t.reshape((b, d, nb * BAND) + rest)
    t = jnp.swapaxes(t, 1, 2)
    return t.reshape((b, nb * BAND * d) + rest)[:, :s]

def band_keys(t):
    prev = jnp.pad(t[:, :, :-1], [(0, 0), (0, 0), (1, 0)] + [(0, 0)] * 3)
    return jnp.concatenate([prev, t], axis=3)

def gmlp_layer(x, c, ada_w, ada_b, norm_g, w_in, sgu_g, w_s, b_s, w_out):
    bsz, s, _ = x.shape
    shift, scale, gate = ada_mod(c, ada_w, ada_b, 3)
    h = rms_norm(x, norm_g) * (1 + scale) + shift
    u, v, z = jnp.split(h @ w_in, 3, axis=-1)
    u = jax.nn.gelu(u)
    v = rms_norm(jax.nn.gelu(v), sgu_g)
    v = v.reshape(bsz, s // CHUNK, CHUNK, A_GROUPS, A_GROUP_WIDTH)
    w_causal = jnp.tril(w_s)
    mixed = jnp.einsum('gts,bcsge->bctge', w_causal, v) + b_s.T[None, None, :, :, None]
    y = u * mixed.reshape(bsz, s, A_WIDTH) * jax.nn.silu(z)
    return x + gate * (y @ w_out)

def shared_kv(x, c, ada_w, ada_b, norm_g, w_kv, k_norm_g):
    bsz, s, _ = x.shape
    shift, scale = ada_mod(c, ada_w, ada_b, 2)
    h = rms_norm(x, norm_g) * (1 + scale) + shift
    k, v = jnp.split(h @ w_kv, 2, axis=-1)
    k = rms_norm(k.reshape(bsz, s, N_KV_HEADS, HEAD_DIM), k_norm_g)
    v = v.reshape(bsz, s, N_KV_HEADS, HEAD_DIM)
    groups = []
    for g, (window, d) in enumerate(DILATED_GROUPS):
        hs = slice(g * KV_HEADS_PER_GROUP, (g + 1) * KV_HEADS_PER_GROUP)
        groups.append((band_keys(to_dilated(k[:, :, hs], d)),
                       band_keys(to_dilated(v[:, :, hs], d))))
    return groups

def dilated_group_attn(q, kb, vb, slopes, window, d):
    s = q.shape[1]
    ql = to_dilated(q, d)
    bsz, _, nb = ql.shape[:3]
    ql = ql.reshape(bsz, d, nb, BAND, KV_HEADS_PER_GROUP, Q_PER_KV, HEAD_DIM)
    sc = jnp.einsum('brnikgh,brnjkh->brnkgij', ql, kb, preferred_element_type=jnp.float32)
    i = jnp.arange(BAND)[:, None]
    j = jnp.arange(2 * BAND)[None, :]
    dq = BAND + i - j
    key_idx = (jnp.arange(nb)[:, None, None] - 1) * BAND + j
    valid = (dq >= 0) & (dq <= window // d) & (key_idx >= 0)
    bias = -slopes.astype(jnp.float32).reshape(KV_HEADS_PER_GROUP, Q_PER_KV)[:, :, None, None] \
        * (d * dq).astype(jnp.float32)
    sc = jnp.where(valid[:, None, None], sc + bias, -jnp.inf)
    m = jnp.max(sc, axis=-1, keepdims=True)
    p = jnp.exp(sc - m)
    l = jnp.sum(p, axis=-1, keepdims=True)
    o = jnp.einsum('brnkgij,brnjkh->brnikgh', p / l, vb.astype(jnp.float32))
    lse = jnp.moveaxis((m + jnp.log(l))[..., 0], -1, 3)
    o = from_dilated(o.reshape(bsz, d, nb, BAND, Q_HEADS_PER_GROUP, HEAD_DIM), s)
    lse = from_dilated(lse.reshape(bsz, d, nb, BAND, Q_HEADS_PER_GROUP), s)
    return o, lse

def dilated_layer(x, c, kv_groups, ada_w, ada_b, norm_g, w_in, q_norm_g, w_out):
    bsz, s, _ = x.shape
    shift, scale, gate = ada_mod(c, ada_w, ada_b, 3)
    h = rms_norm(x, norm_g) * (1 + scale) + shift
    qz = h @ w_in
    q = qz[..., :N_Q_HEADS * HEAD_DIM].reshape(bsz, s, N_Q_HEADS, HEAD_DIM)
    z = qz[..., N_Q_HEADS * HEAD_DIM:]
    q = rms_norm(q, q_norm_g) * (HEAD_DIM ** -0.5)
    slopes = alibi_slopes()
    outs, lses = [], []
    for g, (window, d) in enumerate(DILATED_GROUPS):
        hs = slice(g * Q_HEADS_PER_GROUP, (g + 1) * Q_HEADS_PER_GROUP)
        kb, vb = kv_groups[g]
        o, lse = dilated_group_attn(q[:, :, hs], kb, vb, slopes[hs], window, d)
        outs.append(o)
        lses.append(lse)
    alpha = jax.nn.softmax(jnp.stack(lses), axis=0)
    o = jnp.sum(alpha[..., None] * jnp.stack(outs), axis=0).astype(x.dtype)
    y = o.reshape(bsz, s, B_WIDTH) * jax.nn.silu(z)
    return x + gate * (y @ w_out)

def first_inputs(seed: int = 0) -> dict:
    key = jax.random.key(seed)
    ks = jax.random.split(key, 24)
    nrm = lambda k, shape, sc: jax.random.normal(k, shape, jnp.float32) * sc
    D = D_MODEL
    return {
        "x": nrm(ks[0], (BATCH, SEQ, D), 1.0),
        "c": nrm(ks[1], (BATCH, D), 1.0),
        "a_ada_w": nrm(ks[2], (N_A_LAYERS, D, 3 * D), 0.5 * D ** -0.5),
        "a_ada_b": nrm(ks[3], (N_A_LAYERS, 3 * D), 0.01),
        "a_norm_g": 1.0 + nrm(ks[4], (N_A_LAYERS, D), 0.05),
        "a_w_in": nrm(ks[5], (N_A_LAYERS, D, 3 * A_WIDTH), D ** -0.5),
        "a_sgu_g": 1.0 + nrm(ks[6], (N_A_LAYERS, A_WIDTH), 0.05),
        "a_w_spatial": nrm(ks[7], (N_A_LAYERS, A_GROUPS, CHUNK, CHUNK), 0.5 * CHUNK ** -0.5),
        "a_b_spatial": 1.0 + nrm(ks[8], (N_A_LAYERS, A_GROUPS, CHUNK), 0.01),
        "a_w_out": nrm(ks[9], (N_A_LAYERS, A_WIDTH, D), A_WIDTH ** -0.5),
        "kv_ada_w": nrm(ks[10], (D, 2 * D), 0.5 * D ** -0.5),
        "kv_ada_b": nrm(ks[11], (2 * D,), 0.01),
        "kv_norm_g": 1.0 + nrm(ks[12], (D,), 0.05),
        "w_kv": nrm(ks[13], (D, 2 * N_KV_HEADS * HEAD_DIM), D ** -0.5),
        "k_norm_g": 1.0 + nrm(ks[14], (HEAD_DIM,), 0.05),
        "b_ada_w": nrm(ks[15], (N_B_LAYERS, D, 3 * D), 0.5 * D ** -0.5),
        "b_ada_b": nrm(ks[16], (N_B_LAYERS, 3 * D), 0.01),
        "b_norm_g": 1.0 + nrm(ks[17], (N_B_LAYERS, D), 0.05),
        "b_w_in": nrm(ks[18], (N_B_LAYERS, D, N_Q_HEADS * HEAD_DIM + B_WIDTH), D ** -0.5),
        "b_q_norm_g": 1.0 + nrm(ks[19], (N_B_LAYERS, HEAD_DIM), 0.05),
        "b_w_out": nrm(ks[20], (N_B_LAYERS, B_WIDTH, D), B_WIDTH ** -0.5),
    }

def first_block(x, c, a_ada_w, a_ada_b, a_norm_g, a_w_in, a_sgu_g, a_w_spatial, a_b_spatial,
              a_w_out, kv_ada_w, kv_ada_b, kv_norm_g, w_kv, k_norm_g, b_ada_w, b_ada_b,
              b_norm_g, b_w_in, b_q_norm_g, b_w_out):
    kv_groups = None
    for layer in range(DEPTH):
        if layer < N_A_LAYERS:
            x = gmlp_layer(x, c, a_ada_w[layer], a_ada_b[layer], a_norm_g[layer], a_w_in[layer],
                           a_sgu_g[layer], a_w_spatial[layer], a_b_spatial[layer], a_w_out[layer])
        else:
            if layer == N_A_LAYERS:
                kv_groups = shared_kv(x, c, kv_ada_w, kv_ada_b, kv_norm_g, w_kv, k_norm_g)
            lb = layer - N_A_LAYERS
            x = dilated_layer(x, c, kv_groups, b_ada_w[lb], b_ada_b[lb], b_norm_g[lb], b_w_in[lb],
                              b_q_norm_g[lb], b_w_out[lb])
    return x


DEPTH_2 = 1

HEAD_DIM_2 = 64
FOX_HEADS = 8
DIFF_HEADS = 4
FOX_WIDTH = FOX_HEADS * HEAD_DIM_2
DIFF_WIDTH = DIFF_HEADS * 2 * HEAD_DIM_2
MIX_WIDTH = FOX_WIDTH + DIFF_WIDTH
IN_WIDTH = 3 * FOX_WIDTH + FOX_HEADS + 3 * DIFF_WIDTH
D_FF = ((8 * D_MODEL // 3 + 255) // 256) * 256
BLOCK_Q = 128


def _rms(x, g):
    xf = x.astype(jnp.float32)
    y = xf * lax.rsqrt(jnp.mean(xf * xf, axis=-1, keepdims=True) + EPS)
    return (y * g.astype(jnp.float32)).astype(x.dtype)

def _to_blocks(t):
    b, h, s = t.shape[:3]
    nb = s // BLOCK_Q
    t = t.reshape((b, h, nb, BLOCK_Q) + t.shape[3:])
    return jnp.moveaxis(t, 2, 0)

def _from_blocks(t):
    nb, b, h, bq, d = t.shape
    return jnp.moveaxis(t, 0, 2).reshape(b, h, nb * bq, d)

def _fox_attention(q, k, v, log_f):
    s_len = q.shape[2]
    scale = 1.0 / math.sqrt(q.shape[-1])
    cum = jnp.cumsum(log_f, axis=-1)
    key_pos = jnp.arange(s_len)
    starts = jnp.arange(s_len // BLOCK_Q) * BLOCK_Q

    def one_block(args):
        qi, ci, st = args
        s = jnp.einsum('bhqd,bhkd->bhqk', qi, k, preferred_element_type=jnp.float32) * scale
        s = s + ci[..., :, None] - cum[..., None, :]
        qpos = st + jnp.arange(BLOCK_Q)
        mask = key_pos[None, :] <= qpos[:, None]
        p = jax.nn.softmax(jnp.where(mask, s, -jnp.inf), axis=-1)
        return jnp.einsum('bhqk,bhkd->bhqd', p.astype(v.dtype), v)

    out = lax.map(one_block, (_to_blocks(q), _to_blocks(cum), starts))
    return _from_blocks(out)

def _diff_attention(q1, q2, k1, k2, v, lam, slopes):
    s_len = q1.shape[2]
    scale = 1.0 / math.sqrt(q1.shape[-1])
    key_pos = jnp.arange(s_len)
    starts = jnp.arange(s_len // BLOCK_Q) * BLOCK_Q

    def one_block(args):
        q1i, q2i, st = args
        qpos = st + jnp.arange(BLOCK_Q)
        dist = (qpos[:, None] - key_pos[None, :]).astype(jnp.float32)
        alibi = -slopes[:, None, None] * dist
        mask = dist >= 0
        s1 = jnp.einsum('bhqd,bhkd->bhqk', q1i, k1, preferred_element_type=jnp.float32) * scale + alibi
        s2 = jnp.einsum('bhqd,bhkd->bhqk', q2i, k2, preferred_element_type=jnp.float32) * scale + alibi
        p = (jax.nn.softmax(jnp.where(mask, s1, -jnp.inf), axis=-1)
             - lam * jax.nn.softmax(jnp.where(mask, s2, -jnp.inf), axis=-1))
        return jnp.einsum('bhqk,bhkd->bhqd', p.astype(v.dtype), v)

    out = lax.map(one_block, (_to_blocks(q1), _to_blocks(q2), starts))
    return _from_blocks(out)

def _modulate(x, g, shift, scale):
    return _rms(x, g) * (1.0 + scale[:, None, :]) + shift[:, None, :]

def second_inputs(seed: int = 0) -> dict:
    key = jax.random.key(seed)
    ks = jax.random.split(key, 20)
    f32 = jnp.float32
    nrm = lambda k, shape, s: jax.random.normal(k, shape, f32) * s
    d = D_MODEL
    return {
        "x": nrm(ks[0], (BATCH, SEQ, d), 1.0),
        "c": nrm(ks[1], (BATCH, d), 1.0),
        "ln1_g": 1.0 + nrm(ks[2], (DEPTH_2, d), 0.02),
        "ln2_g": 1.0 + nrm(ks[3], (DEPTH_2, d), 0.02),
        "w_ada": nrm(ks[4], (DEPTH_2, d, 6 * d), 0.5 * d ** -0.5),
        "b_ada": nrm(ks[5], (DEPTH_2, 6 * d), 0.02),
        "w_in": nrm(ks[6], (DEPTH_2, d, IN_WIDTH), d ** -0.5),
        "b_f": 1.5 + nrm(ks[7], (DEPTH_2, FOX_HEADS), 0.1),
        "fox_qk_g": 1.0 + nrm(ks[8], (DEPTH_2, 2, HEAD_DIM_2), 0.02),
        "diff_qk_g": 1.0 + nrm(ks[9], (DEPTH_2, 2, HEAD_DIM_2), 0.02),
        "diff_lam": nrm(ks[10], (DEPTH_2, 4, HEAD_DIM_2), 0.1),
        "diff_norm_g": 1.0 + nrm(ks[11], (DEPTH_2, 2 * HEAD_DIM_2), 0.02),
        "w_out": nrm(ks[12], (DEPTH_2, MIX_WIDTH, d), MIX_WIDTH ** -0.5),
        "w_gate": nrm(ks[13], (DEPTH_2, d, D_FF), d ** -0.5),
        "w_up": nrm(ks[14], (DEPTH_2, d, D_FF), d ** -0.5),
        "w_down": nrm(ks[15], (DEPTH_2, D_FF, d), D_FF ** -0.5),
    }

def second_block(x, c, ln1_g, ln2_g, w_ada, b_ada, w_in, b_f, fox_qk_g, diff_qk_g,
              diff_lam, diff_norm_g, w_out, w_gate, w_up, w_down):
    b, s, d = x.shape
    cond = jax.nn.silu(c)
    slopes = 2.0 ** (-8.0 * jnp.arange(1, DIFF_HEADS + 1, dtype=jnp.float32) / DIFF_HEADS)
    splits = np.cumsum([FOX_WIDTH, FOX_WIDTH, FOX_WIDTH, FOX_HEADS,
                        DIFF_WIDTH, DIFF_WIDTH]).tolist()

    for l in range(DEPTH_2):
        mod = cond @ w_ada[l] + b_ada[l]
        sh1, sc1, g1, sh2, sc2, g2 = jnp.split(mod, 6, axis=-1)

        h = _modulate(x, ln1_g[l], sh1, sc1)
        u = h @ w_in[l]
        fq, fk, fv, fg, dq, dk, dv = jnp.split(u, splits, axis=-1)

        heads = lambda t, n, hd: t.reshape(b, s, n, hd).transpose(0, 2, 1, 3)
        fq = _rms(heads(fq, FOX_HEADS, HEAD_DIM_2), fox_qk_g[l, 0])
        fk = _rms(heads(fk, FOX_HEADS, HEAD_DIM_2), fox_qk_g[l, 1])
        fv = heads(fv, FOX_HEADS, HEAD_DIM_2)
        log_f = jax.nn.log_sigmoid(fg.astype(jnp.float32) + b_f[l].astype(jnp.float32))
        log_f = log_f.transpose(0, 2, 1)
        fox_out = _fox_attention(fq, fk, fv, log_f)

        dq = dq.reshape(b, s, DIFF_HEADS, 2, HEAD_DIM_2).transpose(0, 2, 3, 1, 4)
        dk = dk.reshape(b, s, DIFF_HEADS, 2, HEAD_DIM_2).transpose(0, 2, 3, 1, 4)
        dq = _rms(dq, diff_qk_g[l, 0])
        dk = _rms(dk, diff_qk_g[l, 1])
        dv = heads(dv, DIFF_HEADS, 2 * HEAD_DIM_2)
        lam_init = 0.8 - 0.6 * math.exp(-0.3 * l)
        lv = diff_lam[l].astype(jnp.float32)
        lam = jnp.exp(jnp.sum(lv[0] * lv[1])) - jnp.exp(jnp.sum(lv[2] * lv[3])) + lam_init
        diff_out = _diff_attention(dq[:, :, 0], dq[:, :, 1], dk[:, :, 0], dk[:, :, 1], dv, lam, slopes)
        diff_out = _rms(diff_out, diff_norm_g[l]) * (1.0 - lam_init)

        mixed = jnp.concatenate([
            fox_out.transpose(0, 2, 1, 3).reshape(b, s, FOX_WIDTH),
            diff_out.transpose(0, 2, 1, 3).reshape(b, s, DIFF_WIDTH)], axis=-1)
        x = x + g1[:, None, :] * (mixed @ w_out[l])

        h2 = _modulate(x, ln2_g[l], sh2, sc2)
        y = (jax.nn.silu(h2 @ w_gate[l]) * (h2 @ w_up[l])) @ w_down[l]
        x = x + g2[:, None, :] * y
    return x


def setup_inputs(seed=0):
    out = dict(first_inputs(seed))
    for name, value in second_inputs(seed + 1).items():
        if name != "x":
            out[name + "_2"] = value
    return out


def reference(
    x, c, a_ada_w, a_ada_b, a_norm_g, a_w_in, a_sgu_g, a_w_spatial, a_b_spatial, a_w_out,
    kv_ada_w, kv_ada_b, kv_norm_g, w_kv, k_norm_g, b_ada_w, b_ada_b, b_norm_g, b_w_in,
    b_q_norm_g, b_w_out, c_2, ln1_g_2, ln2_g_2, w_ada_2, b_ada_2, w_in_2, b_f_2, fox_qk_g_2,
    diff_qk_g_2, diff_lam_2, diff_norm_g_2, w_out_2, w_gate_2, w_up_2, w_down_2,
):
    x = first_block(
        x, c, a_ada_w, a_ada_b, a_norm_g, a_w_in, a_sgu_g, a_w_spatial, a_b_spatial, a_w_out,
        kv_ada_w, kv_ada_b, kv_norm_g, w_kv, k_norm_g, b_ada_w, b_ada_b, b_norm_g, b_w_in,
        b_q_norm_g, b_w_out,
    )
    return second_block(
        x, c_2, ln1_g_2, ln2_g_2, w_ada_2, b_ada_2, w_in_2, b_f_2, fox_qk_g_2, diff_qk_g_2,
        diff_lam_2, diff_norm_g_2, w_out_2, w_gate_2, w_up_2, w_down_2,
    )


_drawn_inputs = setup_inputs


def setup_inputs(seed=0):
    import zlib

    import numpy as np

    out = dict(_drawn_inputs(seed))
    spreads = {}
    factors = {'a_ada_b': 8.0,
     'a_norm_g': 4.894,
     'a_sgu_g': 8.0,
     'a_b_spatial': 8.0,
     'kv_ada_b': 8.0,
     'kv_norm_g': 8.0,
     'k_norm_g': 8.0,
     'b_ada_b': 8.0,
     'b_norm_g': 8.0,
     'b_q_norm_g': 8.0,
     'ln1_g_2': 42.424,
     'ln2_g_2': 42.761,
     'b_f_2': 192.487,
     'fox_qk_g_2': 59.235,
     'diff_qk_g_2': 64.0,
     'diff_lam_2': 3.196,
     'diff_norm_g_2': 200.0}
    for name, (base, spread) in spreads.items():
        noise = np.random.default_rng([zlib.crc32(name.encode()), seed]).standard_normal(out[name].shape)
        drawn = base * np.exp(spread * noise) if base else spread * noise
        out[name] = __import__('jax').numpy.asarray(drawn.astype(out[name].dtype))
    for name, factor in factors.items():
        out[name] = (out[name] * factor).astype(out[name].dtype)
    return out
```

```python
import math

import numpy as np

import concourse.bass as bass
from concourse import mybir
from concourse.alu_op_type import AluOpType as ALU

F32 = mybir.dt.float32
F32R = mybir.dt.float32r
ACT = mybir.ActivationFunctionType
AX = mybir.AxisListType.X

P = 128
TOK = 512
TB = TOK // P
DM = 1024
KT = DM // P
EPS = 1e-6
AW = 2 * DM
AT = AW // P
GROUPS = 8
QH = DM // P
NKV = 6
SLOPES_B = [2.0 ** (-8.0 * h / 24) for h in range(1, 25)]
SLOPES_D = [2.0 ** (-8.0 * h / 4) for h in range(1, 5)]
FF = 2816
FF1, FF2 = 16, 6
LAM_INIT = 0.8 - 0.6 * math.exp(0.0)
FAR = 1e30

W_V = 0
W_UZ = W_V + 8
W_OUTA = W_UZ + 16
W_KV = W_OUTA + 8
W_B = W_KV + 6
W_OUTB = W_B + 16
W_Q2 = W_OUTB + 4
W_OUT2 = W_Q2 + 12
W_GU1 = W_OUT2 + 4
W_DN1 = W_GU1 + FF1
W_GU2 = W_DN1 + 8
W_DN2 = W_GU2 + FF2
W_END = W_DN2 + 4

MODS = [("a", 0, 8), ("kv", 0, 8), ("b", 0, 12), ("a", 8, 4), ("2", 0, 24)]
S_A, S_KV, S_B, S_AG, S_2 = 0, 8, 16, 28, 32
SHIFT_A, SCALE_A, SHIFT_KV, SCALE_KV = 0, 8, 16, 24
SHIFT_B, SCALE_B, GATE_B, GATE_A = 32, 40, 48, 56
SHIFT_1, SCALE_1, GATE_1, SHIFT_2, SCALE_2, GATE_2 = 64, 72, 80, 88, 96, 104
NMOD = 112

C_1, C_2, G_A, G_KV, G_B, G_LN1, G_LN2, G_SGU = 0, 8, 16, 24, 32, 40, 48, 56
G_K, G_QB, G_DN, G_FQ, G_FK, G_DQ, G_DK = 72, 73, 74, 75, 76, 77, 78
NVEC = 79


def constants():
    i, j = np.arange(P)[:, None], np.arange(P)[None, :]
    ident = np.eye(P)
    ones = np.ones((P, P))
    half = np.kron(np.eye(2), np.ones((64, 64)))
    causal_t = (i <= j) * 1.0
    blocks = []
    for shift in range(3, -4, -1):
        d = 4 * (i - j) + shift
        blocks.append(np.where((d >= 0) & (d <= P), d, FAR))
    d4 = 4 * (i - j)
    blocks.append(np.where(d4 >= 0, d4, FAR))
    blocks.append(np.where((d4 >= 0) & (d4 % 16 == 0), d4, FAR))
    x = np.arange(TOK)[None, :]
    d = i + TOK - P - x
    slopes = np.broadcast_to(-np.array(SLOPES_B, np.float32), (P, 24))
    last = np.broadcast_to(np.array([EPS, 0.0, 0.0, 0.0]), (P, 4))
    tiles = [ident, ones, half, causal_t, np.where(d >= 0, d, FAR), np.where(i >= j, 0.0, -FAR), slopes, last]
    return [np.concatenate(part, axis=1).astype(np.float32) for part in (tiles, blocks)]


K_ID, K_ONE, K_HALF, K_TRI, K_DIST, K_MASK = 0, P, 2 * P, 3 * P, 4 * P, 4 * P + TOK
K_SLOPE = K_MASK + P
K_EPS = K_SLOPE + 24
NCONST = K_EPS + 4


def program(nc, d):
    base = 16512
    top = [base]

    def at(name, shape, off, dt=F32):
        return nc.alloc_sbuf_tensor_at(name, shape, dt, offset=off)

    def take(nbytes):
        off = top[0]
        top[0] += (nbytes + 63) // 64 * 64
        return off

    KB = 1024
    x = at("x", [P, KT, TOK], take(16 * KB))
    h_hi = at("h_hi", [P, KT, TOK], take(16 * KB), F32R)
    off_hlo = take(16 * KB)
    h_lo = at("h_lo", [P, KT, TOK], off_hlo, F32R)
    w_raw = [at(f"w_raw{s}", [P, 2048], take(8 * KB)) for s in range(2)]
    w_hi = [at(f"w_hi{s}", [P, 2048], take(8 * KB), F32R) for s in range(2)]
    w_lo = [at(f"w_lo{s}", [P, 2048], take(8 * KB), F32R) for s in range(2)]
    off_ada = take(8 * KB)
    ada_raw = at("ada_raw", [P, KT, 256], off_ada)
    consts = at("consts", [P, NCONST], take(4 * NCONST))
    vecs = at("vecs", [P, NVEC], take(4 * NVEC))
    mods = at("mods", [P, NMOD], take(4 * NMOD))
    mod_bias = at("mod_bias", [P, NMOD], take(4 * NMOD))
    silu_c = at("silu_c", [P, 16], take(64))
    gains = at("gains", [P, 8], take(32))
    gscale = at("gscale", [P, 8], take(32))
    ada_acc = at("ada_acc", [P, 256], take(KB))
    x_rstd = at("x_rstd", [P, TOK], take(2 * KB))
    v_sums = at("v_sums", [P, TB, GROUPS], take(128))
    v_stat = at("v_stat", [P, 8, TB], take(128))
    row_stat = at("row_stat", [P, 3, 4], take(64))
    stat2 = at("stat2", [P, 3, 2, 2], take(64))
    lam_inv = at("lam_inv", [P, 2], take(8))
    lam_two = at("lam_two", [P, 2], take(8))
    neg_lam = at("neg_lam", [P, 1], take(4))
    c_col = at("c_col", [P, TB, 8], take(128))
    bf_col = at("bf_col", [8, 1], take(4))
    wf_raw = at("wf_raw", [P, KT, 8], take(256))
    ident, ones, half_ones = consts[:, K_ID:K_ID + P], consts[:, K_ONE:K_ONE + P], consts[:, K_HALF:K_HALF + P]
    tmp0 = take(18 * KB)
    T = [tmp0 + 2 * KB * s for s in range(9)]
    sq = [at(f"sq{s}", [P, TOK], T[s]) for s in range(2)]
    sq_first = [at(f"sq_first{s}", [P, TOK], T[s]) for s in range(8)]
    ln_s = at("ln_s", [P, TOK], T[2])
    y0 = at("y0", [P, TOK], T[3])
    y0_half = at("y0_half", [P, TOK], T[4])
    newton = at("newton", [P, TOK], T[5])
    rstd = at("rstd", [P, TOK], T[6])
    hx = [at(f"hx{s}", [P, TOK], T[7 + s]) for s in range(2)]
    off_blocks = take(4 * 9 * P)
    big = top[0]

    x_tok = at("x_tok", [P, TB, DM], big)
    rows_mod = at("rows_mod", [NMOD, P], big + 16 * KB)
    rows_vec = at("rows_vec", [NVEC, P], big + 16 * KB + 512)
    v = at("v", [P, TB, AW], big)
    y_lo = at("y_lo", [P, TB, AW], big, F32R)
    y_hi = at("y_hi", [P, AT, TOK], big + 32 * KB, F32R)
    ada_up = [at(f"ada_up{s}", [P, KT, 256], big + 32 * KB + 8 * KB * s) for s in range(4)]
    ws_t = at("ws_t", [P, GROUPS, P], big + 64 * KB)
    b_sp = at("b_sp", [P, GROUPS, P], off_blocks)
    ws_raw = at("ws_raw", [P, GROUPS, P], big + 20 * KB)
    gelu_u = [at(f"gelu_u{s}", [P, TOK], T[2 + s]) for s in range(2)]
    tanh_z = at("tanh_z", [P, TOK], T[4])
    mixed = [at(f"mixed{s}", [P, TOK], T[5 + s]) for s in range(2)]
    v_stage = [at(f"v_stage{s}", [P, TB, P], T[7 + s]) for s in range(2)]
    v_sq = at("v_sq", [P, TB, 256], T[2])

    k_t = at("k_t", [P, NKV, TOK], big)
    v_b = at("v_b", [P, TB, NKV * P], big + 12 * KB)
    yb_hi = at("yb_hi", [P, QH, TOK], big + 24 * KB, F32R)
    yb_lo = at("yb_lo", [P, QH, TOK], big + 40 * KB, F32R)
    q_n = [at("q_n0", [P, 3, TOK], off_ada), at("q_n1", [P, 3, TOK], big + 56 * KB)]
    s_b = at("s_b", [P, 768], big + 62 * KB)
    p_t = at("p_t", [P, 768], big + 65 * KB)
    z_b = at("z_b", [P, TOK], big + 68 * KB)
    z_t = at("z_t", [P, TOK], T[7])
    yb = at("yb", [P, TOK], T[8])
    blocks = at("blocks", [P, 9, P], off_blocks)

    qk = [[at(f"qk{s}_{n}", [P, TOK], big + (4 * s + n) * 2 * KB) for n in range(4)] for s in range(2)]
    v_2 = [[at(f"v2{s}_{n}", [P, TB, P], big + 16 * KB + (2 * s + n) * 2 * KB) for n in range(2)] for s in range(2)]
    m_hi = at("m_hi", [P, KT, TOK], big + 24 * KB, F32R)
    m_lo = at("m_lo", [P, KT, TOK], big + 40 * KB, F32R)
    s_2 = [at(f"s_2{s}", [P, 2, TOK], big + 56 * KB + 4 * KB * s) for s in range(2)]
    pt_2 = [at(f"pt_2{s}", [P, TOK], big + 64 * KB + 2 * KB * s) for s in range(2)]
    c_row = [at("c_row0", [P, TOK], big + 68 * KB), at("c_row1", [P, TOK], off_blocks)]
    lam_rows = at("lam_rows", [P, 256], big + 24 * KB)
    lam_prod = at("lam_prod", [P, 128], big + 25 * KB)
    wf_hi = at("wf_hi", [P, KT, P], big + 56 * KB, F32R)
    wf_lo = at("wf_lo", [P, KT, P], big + 60 * KB, F32R)
    gate_abs = at("gate_abs", [8, TOK], T[2])
    gate_exp = at("gate_exp", [8, TOK], T[3])
    gate_ln = at("gate_ln", [8, TOK], T[4])
    gate_min = at("gate_min", [8, TOK], T[5])
    gate_log = at("gate_log", [8, TOK], T[6])
    gate_one = at("gate_one", [8, TOK], T[0])
    cum = at("cum", [8, TOK], T[8])
    d_out = at("d_out", [P, TOK], T[7])
    assert big + 70 * KB <= 229344, big

    gu_hi = at("gu_hi", [P, FF1, TOK], big, F32R)
    gu_lo = at("gu_lo", [P, FF1, TOK], big + 32 * KB, F32R)
    tanh_g = [at(f"tanh_g{s}", [P, TOK], T[2 + s]) for s in range(2)]
    gu = [at(f"gu{s}", [P, TOK], T[4 + s]) for s in range(2)]
    out_tok = at("out_tok", [P, TB, DM], off_hlo)

    G = [nc.alloc_psum_tensor(f"acc{n}", [P, TOK], F32) for n in range(4)]
    T0 = nc.alloc_psum_tensor("turn0", [P, TOK], F32)
    T1 = nc.alloc_psum_tensor("turn1", [P, TOK], F32)
    NB = nc.alloc_psum_tensor("norm", [P, TOK], F32)
    AD = nc.alloc_psum_tensor("ada", [P, TOK], F32)


    def sem(name):
        return nc.alloc_semaphore(name)

    rows_loaded, consts_loaded, x_loaded, ws_loaded = sem("rows_loaded"), sem("consts_loaded"), sem("x_loaded"), sem("ws_loaded")
    small_loaded, blocks_loaded, stored = sem("small_loaded"), sem("blocks_loaded"), sem("stored")
    w_loaded = [sem("w_loaded0"), sem("w_loaded1")]
    ada_loaded, ada_up_loaded = sem("ada_loaded"), [sem(f"ada_up_loaded{s}") for s in range(4)]
    hi_done, lo_done = sem("hi_done"), sem("lo_done")
    mm_done, acc_freed, v_gelu_done = sem("mm_done"), sem("acc_freed"), sem("v_gelu_done")
    ada_sum, ada_mm_done, ada_out = sem("ada_sum"), sem("ada_mm_done"), sem("ada_out")
    rows_turned, vecs_ready, silu_ready, gains_ready = sem("rows_turned"), sem("vecs_ready"), sem("silu_ready"), sem("gains_ready")
    ws_turned, ws_ready, x_turned, x_copied = sem("ws_turned"), sem("ws_ready"), sem("x_turned"), sem("x_copied")
    lam_part, lam_exp, lam_ready = sem("lam_part"), sem("lam_exp"), sem("lam_ready")
    sq_ready, qsq_ready = sem("sq_ready"), sem("qsq_ready")
    sum_done, ln_done, y0_done, half_done = sem("sum_done"), sem("ln_done"), sem("y0_done"), sem("half_done")
    newton_done, rstd_done = sem("newton_done"), sem("rstd_done")
    gs_done, hx_done, hhi_done, hlo_done = sem("gs_done"), sem("hx_done"), sem("hhi_done"), sem("hlo_done")
    v_sums_done, v_stat_dve, v_stat_act = sem("v_sums_done"), sem("v_stat_dve"), sem("v_stat_act")
    v_staged, mix_done, mix_freed = sem("v_staged"), sem("mix_done"), sem("mix_freed")
    gelu_done, tanh_done, uz_done = sem("gelu_done"), sem("tanh_done"), sem("uz_done")
    y_done, yhi_done, ylo_done = sem("y_done"), sem("yhi_done"), sem("ylo_done")
    qk_done, s_freed, max_done, exp_done = sem("qk_done"), sem("s_freed"), sem("max_done"), sem("exp_done")
    inv_done, p_ready, turn_done = sem("inv_done"), sem("p_ready"), sem("turn_done")
    pt_act, pt_dve, pv_done = sem("pt_act"), sem("pt_dve"), sem("pv_done")
    tanhz_done = sem("tanhz_done")
    head_out, ybhi_done, yblo_done = sem("head_out"), sem("ybhi_done"), sem("yblo_done")
    wf_zeroed, wfhi_done, wflo_done, fg_done = sem("wf_zeroed"), sem("wfhi_done"), sem("wflo_done"), sem("fg_done")
    fgate_act, fgate_dve, c_turned, c_col_ready = sem("fgate_act"), sem("fgate_dve"), sem("c_turned"), sem("c_col_ready")
    c_spread, c_row_ready = sem("c_spread"), sem("c_row_ready")
    qk2_done, s2_freed, bias2_done, max2_done, exp2_done = sem("qk2_done"), sem("s2_freed"), sem("bias2_done"), sem("max2_done"), sem("exp2_done")
    inv2_done, p2_ready, turn2_done, pt2_done, pv2_done = sem("inv2_done"), sem("p2_ready"), sem("turn2_done"), sem("pt2_done"), sem("pv2_done")
    d_done, mhi_done, mlo_done = sem("d_done"), sem("mhi_done"), sem("mlo_done")
    tanhg_done, gz_done, guhi_done, gulo_done = sem("tanhg_done"), sem("gz_done"), sem("guhi_done"), sem("gulo_done")
    o_turned, o_copied = sem("o_turned"), sem("o_copied")

    N_X0, N_X1, N_K, N_Q, N_X2, N_2 = 0, 1, 2, 8, 32, 33
    N_X3 = N_2 + 20
    SQ1, SQ2, SQ3 = 8, 17, 26

    def norm2(t, mi):
        return N_2 + 4 * t + max(0, t - 1) + (mi if t < 4 else 0)

    def ge(eng, semaphore, value):
        if not isinstance(value, int) or value > 0:
            eng.wait_ge(semaphore, value)

    def next_chunk(u, par):
        return (u, 1) if par == 0 else (u + 1, 0)

    def dilated(tile):
        return tile.rearrange("p (i r) -> p r i", r=4)

    def four(tile):
        return tile.rearrange("p (r i) -> p r i", r=4)

    def units2(t):
        return [(kind, qb) for qb in range(TB) for kind in range(3)]

    def s_reads(u):
        before = sum(1 if n % 3 < 2 else 2 for n in range(u))
        return before, before % 2

    block = nc.Block()
    with block:

        @block.sync
        def _(sp):
            def load(u, par, halves):
                for _, src in halves:
                    sp.lower_ap_dma(src)
                ge(sp, lo_done, 2 * u + par - 1)
                for dst, src in halves:
                    sp.dma_start(dst, src).then_inc(w_loaded[par], 16)

            def ada_load(name, col, s):
                src = ada_w[name][:, :, bass.ds(col, 256)]
                sp.lower_ap_dma(src)
                sp.wait_ge(ada_sum, 8 * s)
                sp.dma_start(ada_raw[:, :, :], src).then_inc(ada_loaded, 16)

            def kn(w):
                return w.rearrange("(k p) n -> p k n", p=P)

            ada_w = {"a": kn(d["a_ada_w"][0]), "kv": kn(d["kv_ada_w"]), "b": kn(d["b_ada_w"][0]), "2": kn(d["w_ada_2"][0])}
            w_in_a, w_out_a, w_kv = kn(d["a_w_in"][0]), kn(d["a_w_out"][0]), kn(d["w_kv"])
            w_in_b, w_out_b = kn(d["b_w_in"][0]), kn(d["b_w_out"][0])
            w_in_2, w_out_2 = kn(d["w_in_2"][0]), kn(d["w_out_2"][0])
            w_gate, w_up = kn(d["w_gate_2"][0]), kn(d["w_up_2"][0])
            w_dn1, w_dn2 = kn(d["w_down_2"][0][0:FF1 * P, :]), kn(d["w_down_2"][0][FF1 * P:FF, :])

            def pair(par, wa, a, wb, b):
                dst = w_raw[par][:, :].rearrange("p (k n) -> p k n", k=KT)
                return [(dst[:, :, 0:P], wa[:, :, bass.ds(a, P)]), (dst[:, :, P:2 * P], wb[:, :, bass.ds(b, P)])]

            def span(par, w, col, kts):
                n = 256 if kts <= KT else P
                dst = w_raw[par][:, 0:kts * n].rearrange("p (k n) -> p k n", k=kts)
                cut = kts // 2
                return [(dst[:, 0:cut, :], w[:, 0:cut, bass.ds(col, n)]), (dst[:, cut:kts, :], w[:, cut:kts, bass.ds(col, n)])]

            sp.dma_start(consts[:, :], d["tiles"]).then_inc(consts_loaded, 16)
            sp.dma_start(x_tok[:, :, :], d["x"][0].rearrange("(t p) n -> p t n", p=P)).then_inc(x_loaded, 16)
            for s in range(8):
                if s >= 4:
                    sp.wait_ge(ada_sum, 8 * (s - 3))
                sp.dma_start(ada_up[s % 4][:, :, :], ada_w["a"][:, :, 256 * s:256 * s + 256]).then_inc(ada_up_loaded[s % 4], 16)
                if s == 4:
                    load(W_V // 2, 0, span(0, w_in_a, AW, KT))
            load(W_V // 2, 1, span(1, w_in_a, AW + 256, KT))

            def v_pair(u):
                n = 2 * (u - W_V // 2)
                for par in range(2):
                    if not (isinstance(u, int) and u == 0):
                        load(u, par, span(par, w_in_a, AW + 256 * (n + par), KT))
                    ada_load("kv", 256 * (n + par), S_KV + n + par)

            v_pair(0)
            with sp.Fori(1, W_UZ // 2) as u:
                v_pair(u)

            def uz_pair(u, name, c0, s0):
                j = 2 * (u - W_UZ // 2)
                for par in range(2):
                    load(u, par, pair(par, w_in_a, P * (j + par), w_in_a, 2 * AW + P * (j + par)))
                    ada_load(name, 256 * (j + par) + c0, s0 + j + par)

            with sp.Fori(W_UZ // 2, W_UZ // 2 + 6) as u:
                uz_pair(u, "b", 0, S_B)
            with sp.Fori(W_UZ // 2 + 6, W_OUTA // 2) as u:
                uz_pair(u, "a", 256 * (8 - 12), S_B)
            with sp.Fori(W_OUTA // 2, W_KV // 2) as u:
                m = 2 * (u - W_OUTA // 2)
                for par in range(2):
                    load(u, par, span(par, w_out_a, P * (m + par), AT))
                    ada_load("2", 256 * (m + par), S_2 + m + par)
            sp.wait_ge(mix_freed, AT)
            sp.dma_start(blocks[:, :, :], d["blocks"].rearrange("p (b n) -> p b n", n=P)).then_inc(blocks_loaded, 16)
            with sp.Fori(W_KV // 2, W_B // 2) as u:
                j = 2 * (u - W_KV // 2)
                for par in range(2):
                    load(u, par, pair(par, w_kv, P * (j + par), w_kv, NKV * P + P * (j + par)))
                    ada_load("2", 256 * (j + par + 8), S_2 + 8 + j + par)
            with sp.Fori(0, QH // 2) as i:
                for kv in range(2):
                    u = i * 2 + kv + W_B // 2
                    col = P * i + 4 * P * kv
                    load(u, 0, pair(0, w_in_b, col, w_in_b, col + DM))
                    load(u, 1, pair(1, w_in_b, col + 2 * DM, w_in_b, col + 3 * DM))
            with sp.Fori(W_OUTB // 2, W_Q2 // 2) as u:
                c = u - W_OUTB // 2
                for par in range(2):
                    load(u, par, span(par, w_out_b, 512 * c + 256 * par, KT))
                sp.wait_ge(pv_done, 4 * QH)
                for e in range(3):
                    ada_load("2", 256 * (3 * c + e + 14), S_2 + 14 + 3 * c + e)
            for t in range(4):
                fox, dif = P * t, 1544 + P * t
                for n, (a, b) in enumerate(((fox, fox + 512), (dif, dif + 512), (fox + 1024, dif + 1024))):
                    w = W_Q2 + 3 * t + n
                    load(w // 2, w % 2, pair(w % 2, w_in_2, a, w_in_2, b))
            with sp.Fori(W_OUT2 // 2, W_GU1 // 2) as u:
                c = u - W_OUT2 // 2
                for par in range(2):
                    load(u, par, span(par, w_out_2, 512 * c + 256 * par, KT))
                    ada_load("2", 256 * (2 * c + par + 20), S_2 + 20 + 2 * c + par)

            def gate_up(u, col):
                for par in range(2):
                    load(u, par, pair(par, w_gate, col + P * par, w_up, col + P * par))

            with sp.Fori(W_GU1 // 2, W_DN1 // 2) as u:
                gate_up(u, 2 * P * (u - W_GU1 // 2))
            with sp.Fori(W_DN1 // 2, W_GU2 // 2) as u:
                for par in range(2):
                    load(u, par, span(par, w_dn1, 2 * P * (u - W_DN1 // 2) + P * par, FF1))
            with sp.Fori(W_GU2 // 2, W_DN2 // 2) as u:
                gate_up(u, 2 * P * (u - W_GU2 // 2) + FF1 * P)
            with sp.Fori(W_DN2 // 2, W_END // 2) as u:
                for par in range(2):
                    load(u, par, span(par, w_dn2, 512 * (u - W_DN2 // 2) + 256 * par, FF2))
            out = d["out"][0].rearrange("(t p) n -> p t n", p=P)
            for half in range(2):
                sp.wait_ge(o_copied, 4 * half + 4)
                sp.dma_start(out[:, :, 512 * half:512 * half + 512], out_tok[:, :, 512 * half:512 * half + 512]).then_inc(stored, 16)
            sp.wait_ge(stored, 32)

        @block.gpsimd
        def _(pool):
            def stage(j, par):
                ge(pool, mix_done, j - 1)
                nc.gpsimd.tensor_tensor(v_stage[par][:, :, :], v[:, :, bass.ds(j * P, P)],
                                        v_stat[:, 5, :].unsqueeze(2).broadcast_to([P, TB, P]), ALU.mult).then_inc(v_staged, 1)

            pool.wait_ge(v_stat_dve, 3)
            stage(0, 0)
            stage(1, 1)
            with pool.Fori(1, AT // 2) as i:
                for par in range(2):
                    stage(2 * i + par, par)
            pool.wait_ge(pv_done, 4 * QH)
            nc.gpsimd.memset(wf_hi[:, :, :].bitcast(F32), 0.0).then_inc(wf_zeroed, 1)
            nc.gpsimd.memset(wf_lo[:, :, :].bitcast(F32), 0.0).then_inc(wf_zeroed, 1)

        @block.scalar
        def _(act):
            eps_col = consts[:, K_EPS:K_EPS + 1]

            def to_hi(u, par):
                act.wait_ge(w_loaded[par], 32 * u + 32)
                ge(act, mm_done, 4 * u + 2 * par - 2)
                nc.scalar.activation(w_hi[par][:, :], w_raw[par][:, :], ACT.Copy).then_inc(hi_done, 1)

            def rstd_start(k, total, count):
                act.wait_ge(sum_done, k + 1)
                nc.scalar.activation(ln_s[:, :], total, ACT.Ln, scale=1.0 / count, bias=eps_col).then_inc(ln_done, 1)
                act.wait_ge(ln_done, k + 1)
                ge(act, rstd_done, k)
                nc.scalar.activation(y0[:, :], ln_s[:, :], ACT.Exp, scale=-0.5).then_inc(y0_done, 1)
                act.wait_ge(y0_done, k + 1)
                nc.scalar.activation(y0_half[:, :], y0[:, :], ACT.Square, scale=math.sqrt(0.5 / count)).then_inc(half_done, 1)

            def h_round(e, shift, dilate):
                for kt in range(KT):
                    act.wait_ge(hx_done, 8 * e + kt + 1)
                    src, dst = hx[kt % 2][:, :], h_hi[:, kt, :]
                    nc.scalar.activation(four(dst) if dilate else dst, dilated(src) if dilate else src, ACT.Identity,
                                         bias=mods[:, shift + kt:shift + kt + 1]).then_inc(hhi_done, 1)

            def square_x(m, slot, count, seen):
                act.wait_ge(acc_freed, seen)
                nc.scalar.activation(sq[slot][:, :], x[:, m, :], ACT.Square).then_inc(sq_ready, 1)

            def square_zero(after):
                act.wait_ge(newton_done, after + 1)
                nc.scalar.activation(sq[1][:, :], x[:, 0, :], ACT.Copy, scale=0.0).then_inc(sq_ready, 1)

            at_row = 0
            for name, lo, n in MODS:
                src = d[{"a": "a_ada_b", "kv": "kv_ada_b", "b": "b_ada_b", "2": "b_ada_2"}[name]]
                src = (src if name == "kv" else src[0]).rearrange("(r p) -> r p", p=P)
                act.dma_start(rows_mod[at_row:at_row + 2 * n, :], src[2 * lo:2 * lo + 2 * n, :]).then_inc(rows_loaded, 16)
                at_row += 2 * n
            for name, col, n in (("c", C_1, 8), ("c_2", C_2, 8), ("a_norm_g", G_A, 8), ("kv_norm_g", G_KV, 8), ("b_norm_g", G_B, 8),
                                 ("ln1_g_2", G_LN1, 8), ("ln2_g_2", G_LN2, 8), ("a_sgu_g", G_SGU, 16), ("k_norm_g", G_K, 1),
                                 ("b_q_norm_g", G_QB, 1), ("diff_norm_g_2", G_DN, 1)):
                src = d[name] if len(d[name].shape) == 1 else d[name][0]
                act.dma_start(rows_vec[col:col + n, :], src.rearrange("(r p) -> r p", p=P)).then_inc(rows_loaded, 16)
            for name, col in (("fox_qk_g_2", G_FQ), ("diff_qk_g_2", G_DQ)):
                for half in range(2):
                    act.dma_start(rows_vec[col:col + 2, 64 * half:64 * half + 64], d[name][0]).then_inc(rows_loaded, 16)
            act.dma_start(ws_raw[:, :, :], d["a_w_spatial"][0].rearrange("g t s -> t g s")).then_inc(ws_loaded, 16)
            act.dma_start(b_sp[:, :, :], d["a_b_spatial"][0].rearrange("g t -> (g t)").partition_broadcast(P)
                          .rearrange("p (g t) -> p g t", g=GROUPS)).then_inc(small_loaded, 16)
            act.dma_start(lam_rows[:, :], d["diff_lam_2"][0].rearrange("a b -> (a b)").partition_broadcast(P)).then_inc(small_loaded, 16)
            act.dma_start(bf_col[:, :], d["b_f_2"].rearrange("a h -> h a")).then_inc(small_loaded, 16)
            act.dma_start(wf_raw[:, :, :], d["w_in_2"][0].rearrange("(k p) n -> p k n", p=P)[:, :, 1536:1544]).then_inc(small_loaded, 16)

            act.wait_ge(vecs_ready, 2)
            nc.scalar.activation(silu_c[:, :], vecs[:, C_1:C_1 + 16], ACT.Silu).then_inc(silu_ready, 1)
            for kt in range(KT):
                act.wait_ge(x_turned, kt + 1)
                nc.scalar.activation(x[:, kt, :], G[kt % 4][:, :], ACT.Copy).then_inc(x_copied, 1)
                act.wait_ge(x_copied, kt + 1)
                nc.scalar.activation(sq_first[kt][:, :], x[:, kt, :], ACT.Square).then_inc(sq_ready, 1)
            rstd_start(N_X0, NB[:, :], DM)
            act.wait_ge(lam_part, 2)
            nc.scalar.activation(lam_two[:, :], lam_two[:, :], ACT.Exp).then_inc(lam_exp, 1)
            to_hi(0, 0)
            h_round(0, SHIFT_A, False)

            def v_pair(u):
                n = 2 * u - W_V
                for par in range(2):
                    to_hi(*next_chunk(u, par))
                    for hb in range(2):
                        act.wait_ge(mm_done, 4 * u + 2 * par + hb + 1)
                        nc.scalar.activation(v[:, 2 * hb:2 * hb + 2, bass.ds(256 * n + 256 * par, 256)],
                                             G[2 * par + hb][:, :].rearrange("p (t n) -> p t n", t=2),
                                             ACT.Gelu_apprx_tanh).then_inc(v_gelu_done, 1)

            v_pair(0)
            with act.Fori(1, W_UZ // 2) as u:
                v_pair(u)
            act.wait_ge(v_stat_dve, 1)
            nc.scalar.activation(v_stat[:, 1, :], v_stat[:, 0, :], ACT.Ln, scale=1.0 / AW, bias=eps_col).then_inc(v_stat_act, 1)
            act.wait_ge(v_stat_act, 1)
            nc.scalar.activation(v_stat[:, 2, :], v_stat[:, 1, :], ACT.Exp, scale=-0.5).then_inc(v_stat_act, 1)
            act.wait_ge(v_stat_act, 2)
            nc.scalar.activation(v_stat[:, 3, :], v_stat[:, 2, :], ACT.Square, scale=math.sqrt(0.5 / AW)).then_inc(v_stat_act, 1)

            def uz_pair(u):
                j = 2 * u - W_UZ
                for par in range(2):
                    to_hi(*next_chunk(u, par))
                    act.wait_ge(mm_done, 4 * u + 2 * par + 1)
                    ge(act, uz_done, j + par - 1)
                    nc.scalar.activation(gelu_u[par][:, :], G[2 * par][:, :], ACT.Gelu_apprx_tanh).then_inc(gelu_done, 1)
                    act.wait_ge(mm_done, 4 * u + 2 * par + 2)
                    ge(act, uz_done, j + par)
                    nc.scalar.activation(tanh_z[:, :], G[2 * par + 1][:, :], ACT.Tanh, scale=0.5).then_inc(tanh_done, 1)
                    act.wait_ge(y_done, j + par + 1)
                    nc.scalar.activation(y_hi[:, j + par, :], mixed[par][:, :], ACT.Copy).then_inc(yhi_done, 1)

            uz_pair(W_UZ // 2)
            with act.Fori(W_UZ // 2 + 1, W_OUTA // 2) as u:
                uz_pair(u)

            square_zero(N_X0)
            with act.Fori(W_OUTA // 2, W_KV // 2) as u:
                m = 2 * u - W_OUTA
                for par in range(2):
                    to_hi(*next_chunk(u, par))
                    square_x(m + par, par, SQ1, 4 * u + 2 * par - 14)
            rstd_start(N_X1, NB[:, :], DM)
            h_round(1, SHIFT_KV, True)

            with act.Fori(W_KV // 2, W_B // 2) as u:
                j = 2 * u - W_KV
                for par in range(2):
                    to_hi(*next_chunk(u, par))
                    act.wait_ge(mm_done, 4 * u + 2 * par + 1)
                    nc.scalar.activation(sq[par][:, :], G[2 * par][:, :], ACT.Square).then_inc(qsq_ready, 1)
                    rstd_start(N_K + j + par, NB[:, :], P)
            act.wait_ge(mm_done, 2 * W_B)
            h_round(2, SHIFT_B, True)

            def head(n, p, mh, attend, project):
                m, q = n - 1, 1 - p
                w0 = 2 * n + W_B
                k = 3 * n + N_Q

                def exps(r):
                    act.wait_ge(max_done, 4 * m + r + 1)
                    nc.scalar.activation(s_b[:, :], s_b[:, :], ACT.Exp, bias=row_stat[:, 0, r:r + 1],
                                         accum_out=row_stat[:, 1, r:r + 1]).then_inc(exp_done, 1)

                def turn_copy(r):
                    act.wait_ge(turn_done, 4 * m + r + 1)
                    nc.scalar.activation(p_t[:, 0:TOK], T0[:, :], ACT.Copy).then_inc(pt_act, 1)

                def squares(mi):
                    act.wait_ge(mm_done, 2 * w0 + mi + 1)
                    act.wait_ge(sum_done, k + mi - 1)
                    nc.scalar.activation(sq[(mi + p) % 2][:, :], G[mi % 2][:, :], ACT.Square).then_inc(qsq_ready, 1)

                u0 = n + W_B // 2
                if project:
                    to_hi(u0, 1)
                if attend:
                    exps(0)
                if project:
                    squares(0)
                if attend:
                    turn_copy(0)
                    exps(1)
                if project:
                    rstd_start(k, NB[:, :], P)
                    squares(1)
                    to_hi(u0 + 1, 0)
                if attend:
                    turn_copy(1)
                    exps(2)
                if project:
                    rstd_start(k + 1, NB[:, :], P)
                    squares(2)
                if attend:
                    turn_copy(2)
                    exps(3)
                if project:
                    rstd_start(k + 2, NB[:, :], P)
                if attend:
                    turn_copy(3)
                    act.wait_ge(head_out, m + 1)
                    nc.scalar.activation(yb_hi[:, mh + 4 * q, :], yb[:, :], ACT.Copy).then_inc(ybhi_done, 1)
                if project:
                    act.wait_ge(mm_done, 2 * w0 + 4)
                    act.wait_ge(acc_freed, 2 * w0 - 16)
                    nc.scalar.activation(z_t[:, :], G[1][:, :], ACT.Tanh, scale=0.5).then_inc(tanhz_done, 1)

            head(0, 0, 0, False, True)
            with act.Fori(1, QH // 2) as i:
                head(2 * i - 1, 1, i - 1, True, True)
                head(2 * i, 0, i - 1, True, True)
            head(QH - 1, 1, QH // 2 - 1, True, True)
            head(QH, 0, QH // 2 - 1, True, False)

            square_zero(N_X2 - 1)
            with act.Fori(W_OUTB // 2, W_Q2 // 2) as u:
                for par in range(2):
                    to_hi(*next_chunk(u, par))
                    for half in range(2):
                        square_x(4 * (u - W_OUTB // 2) + 2 * par + half, half, SQ2, 4 * u + 2 * par + half - 15)
            rstd_start(N_X2, NB[:, :], DM)
            act.wait_ge(wf_zeroed, 2)
            act.wait_ge(small_loaded, 64)
            nc.scalar.activation(wf_hi[:, :, 0:8], wf_raw[:, :, :], ACT.Copy).then_inc(wfhi_done, 1)
            h_round(3, SHIFT_1, False)

            act.wait_ge(fg_done, 1)
            nc.scalar.activation(gate_abs[:, :], T0[0:8, :], ACT.Abs, bias=bf_col[:, :]).then_inc(fgate_act, 1)
            act.wait_ge(fgate_act, 1)
            nc.scalar.activation(gate_exp[:, :], gate_abs[:, :], ACT.Exp, scale=-1.0).then_inc(fgate_act, 1)
            act.wait_ge(fgate_act, 2)
            nc.scalar.activation(gate_ln[:, :], gate_exp[:, :], ACT.Ln, bias=ones[0:8, 0:1]).then_inc(fgate_act, 1)

            for t in range(5):
                w0 = W_Q2 + 3 * t
                a = t - 1
                attend, project = t >= 1, t < 4
                units = units2(a)
                if attend:
                    for n, bank in enumerate((T0, T1)):
                        act.wait_ge(c_spread, 2 * a + n + 1)
                        if a >= 1:
                            act.wait_ge(pv2_done, 12 * a)
                        nc.scalar.activation(c_row[n][:, :], bank[:, :], ACT.Copy).then_inc(c_row_ready, 1)
                for u in range(13):
                    if project and u in (0, 4, 8):
                        to_hi(*divmod(w0 + u // 4 + 1, 2))
                    if attend and u >= 1:
                        act.wait_ge(turn2_done, 12 * a + u)
                        width = (units[u - 1][1] + 1) * P
                        nc.scalar.activation(pt_2[(u - 1) % 2][:, 0:width], T0[:, 0:width], ACT.Copy).then_inc(pt2_done, 1)
                    if attend and u < 12:
                        kind, qb = units[u]
                        width = (qb + 1) * P
                        act.wait_ge(max2_done, 12 * a + u + 1)
                        for n in range(2 if kind == 2 else 1):
                            ex = nc.scalar.activation(s_2[u % 2][:, n, 0:width], s_2[u % 2][:, n, 0:width], ACT.Exp,
                                                      bias=stat2[:, 0, u % 2, n:n + 1], accum_out=stat2[:, 1, u % 2, n:n + 1])
                        ex.then_inc(exp2_done, 1)
                    if project and u in (1, 3, 5, 7):
                        mi = u // 2
                        k = norm2(t, mi)
                        act.wait_ge(mm_done, 2 * w0 + mi + 1)
                        act.wait_ge(sum_done, k - 1)
                        nc.scalar.activation(sq[k % 2][:, :], G[mi % 2][:, :], ACT.Square).then_inc(qsq_ready, 1)
                    if project and u in (2, 4, 6, 8):
                        rstd_start(norm2(t, u // 2 - 1), NB[:, :], 64)
                if attend:
                    k = norm2(t, 4)
                    act.wait_ge(pv2_done, 12 * a + 12)
                    nc.scalar.activation(m_hi[:, a, :], AD[:, :], ACT.Copy).then_inc(mhi_done, 1)
                    nc.scalar.activation(sq[k % 2][:, :], T1[:, :], ACT.Square).then_inc(qsq_ready, 1)
                    rstd_start(k, NB[:, :], P)
                    act.wait_ge(d_done, a + 1)
                    nc.scalar.activation(m_hi[:, 4 + a, :], d_out[:, :], ACT.Copy).then_inc(mhi_done, 1)

            square_zero(N_X3 - 1)
            with act.Fori(W_OUT2 // 2, W_GU1 // 2) as u:
                for par in range(2):
                    to_hi(*next_chunk(u, par))
                    for half in range(2):
                        square_x(4 * (u - W_OUT2 // 2) + 2 * par + half, half, SQ3, 4 * u + 2 * par + half - 15)
            rstd_start(N_X3, NB[:, :], DM)
            h_round(4, SHIFT_2, False)

            def gate_up(u, f, par, first):
                to_hi(*next_chunk(u, par))
                act.wait_ge(mm_done, 4 * u + 2 * par + 1)
                ge(act, gulo_done, f + first - 1)
                nc.scalar.activation(tanh_g[par][:, :], G[2 * par][:, :], ACT.Tanh, scale=0.5).then_inc(tanhg_done, 1)
                act.wait_ge(acc_freed, 4 * u + 2 * par - 14)
                nc.scalar.activation(gu_hi[:, f, :], gu[par][:, :], ACT.Copy).then_inc(guhi_done, 1)

            for par in range(2):
                gate_up(W_GU1 // 2, par, par, 0)
            with act.Fori(W_GU1 // 2 + 1, W_DN1 // 2) as u:
                for par in range(2):
                    gate_up(u, 2 * (u - W_GU1 // 2) + par, par, 0)
            with act.Fori(W_DN1 // 2, W_GU2 // 2) as u:
                for par in range(2):
                    to_hi(*next_chunk(u, par))
            with act.Fori(W_GU2 // 2, W_DN2 // 2) as u:
                for par in range(2):
                    gate_up(u, 2 * (u - W_GU2 // 2) + par, par, FF1)

            def result(m):
                act.wait_ge(o_turned, m + 1)
                nc.scalar.activation(out_tok[:, :, bass.ds(P * m, P)], (T0, T1)[m % 2][:, :].rearrange("p (t n) -> p t n", t=TB),
                                     ACT.Copy).then_inc(o_copied, 1)

            for c in range(4):
                if c < 3:
                    to_hi(*divmod(W_DN2 + c + 1, 2))
                if c >= 1:
                    result(2 * c - 2)
                    result(2 * c - 1)
            result(6)
            result(7)

        @block.vector
        def _(dve):
            def f32(tile):
                return tile.bitcast(F32)

            def stt(out, in0, scalar, in1, op0, op1, **more):
                return nc.vector.scalar_tensor_tensor(out, in0, scalar, in1, op0, op1, **more)

            def to_lo(u, par):
                dve.wait_ge(hi_done, 2 * u + par + 1)
                nc.vector.tensor_tensor(w_lo[par][:, :], w_raw[par][:, :], f32(w_hi[par][:, :]), ALU.subtract).then_inc(lo_done, 1)

            def ada_step(s, raw, cond):
                nc.vector.tensor_scalar(ada_acc[:, :], raw[:, 0, :], silu_c[:, cond:cond + 1], None, ALU.mult).then_inc(ada_sum, 1)
                for kt in range(1, KT):
                    dve.wait_ge(ada_sum, 8 * s + kt)
                    stt(ada_acc[:, :], raw[:, kt, :], silu_c[:, cond + kt:cond + kt + 1], ada_acc[:, :], ALU.mult, ALU.add)\
                        .then_inc(ada_sum, 1)

            def ada(s, cond):
                dve.wait_ge(ada_loaded, 16 * (s - 7))
                ada_step(s, ada_raw, cond)

            def ada_end(s):
                dve.wait_ge(ada_mm_done, s + 1)
                nc.vector.tensor_tensor(mods[:, bass.ds(2 * s, 2)], AD[:, 0:2], mod_bias[:, bass.ds(2 * s, 2)], ALU.add).then_inc(ada_out, 1)

            def gain(e, scale, g, have):
                dve.wait_ge(ada_out, have)
                stt(gscale[:, :], mods[:, scale:scale + 8], 1.0, vecs[:, g:g + 8], ALU.add, ALU.mult).then_inc(gs_done, 1)
                dve.wait_ge(gs_done, e + 1)

            def rstd_end(k, total, count, rstd=rstd):
                dve.wait_ge(half_done, k + 1)
                stt(newton[:, :], total, count * EPS, y0_half[:, :], ALU.add, ALU.mult).then_inc(newton_done, 1)
                dve.wait_ge(newton_done, k + 1)
                stt(rstd[:, :], newton[:, :], 1.5, y0[:, :], ALU.subtract, ALU.mult, reverse0=True).then_inc(rstd_done, 1)
                dve.wait_ge(rstd_done, k + 1)

            def h_split(e, shift, dilate):
                def scaled(kt):
                    stt(hx[kt % 2][:, :], x[:, kt, :], gscale[:, kt:kt + 1], x_rstd[:, :], ALU.mult, ALU.mult).then_inc(hx_done, 1)

                scaled(0)
                scaled(1)
                for kt in range(KT):
                    dve.wait_ge(hhi_done, 8 * e + kt + 1)
                    src, hi, lo = hx[kt % 2][:, :], f32(h_hi[:, kt, :]), h_lo[:, kt, :]
                    if dilate:
                        src, hi, lo = dilated(src), four(hi), four(lo)
                    stt(lo, src, mods[:, shift + kt:shift + kt + 1], hi, ALU.add, ALU.subtract).then_inc(hlo_done, 1)
                    if kt + 2 < KT:
                        dve.wait_ge(hlo_done, 8 * e + kt + 1)
                        scaled(kt + 2)

            def update_x(m, acc, gate, mm, n, dilate=False):
                dve.wait_ge(mm_done, mm)
                xm = dilated(x[:, m, :]) if dilate else x[:, m, :]
                stt(xm, four(acc) if dilate else acc, mods[:, bass.ds(m + gate, 1)], xm, ALU.mult, ALU.add).then_inc(acc_freed, n)

            dve.wait_ge(rows_turned, 1)
            nc.vector.tensor_copy(vecs[:, :], AD[:, 0:NVEC]).then_inc(vecs_ready, 1)
            nc.vector.tensor_copy(mod_bias[:, :], AD[:, 128:128 + NMOD]).then_inc(vecs_ready, 1)
            dve.wait_ge(vecs_ready, 2)
            nc.vector.tensor_scalar(gains[:, 0:1], vecs[:, G_QB:G_QB + 1], P ** -0.5, None, ALU.mult)
            nc.vector.tensor_scalar(gains[:, 1:2], vecs[:, G_FQ:G_FQ + 1], 0.125, None, ALU.mult)
            nc.vector.tensor_copy(gains[:, 2:3], vecs[:, G_FK:G_FK + 1])
            nc.vector.tensor_scalar(gains[:, 3:4], vecs[:, G_DQ:G_DQ + 1], 0.125, None, ALU.mult)
            nc.vector.tensor_copy(gains[:, 4:5], vecs[:, G_DK:G_DK + 1])
            nc.vector.tensor_scalar(gains[:, 5:6], vecs[:, G_DN:G_DN + 1], 1.0 - LAM_INIT, None, ALU.mult).then_inc(gains_ready, 1)
            dve.wait_ge(ws_turned, 1)
            tri = consts[:, K_TRI:K_TRI + P].unsqueeze(1).broadcast_to([P, 4, P])
            for n, bank in enumerate((T0, T1)):
                nc.vector.tensor_tensor(ws_t[:, 4 * n:4 * n + 4, :], bank[:, :].rearrange("p (g t) -> p g t", g=4), tri, ALU.mult)\
                    .then_inc(ws_ready, 1)
            dve.wait_ge(small_loaded, 64)
            for n in range(2):
                stt(lam_prod[:, 64 * n:64 * n + 64], lam_rows[:, 128 * n:128 * n + 64], 1.0, lam_rows[:, 128 * n + 64:128 * n + 128],
                    ALU.mult, ALU.mult, accum_out=lam_two[:, n:n + 1]).then_inc(lam_part, 1)
            dve.wait_ge(silu_ready, 1)
            for s in range(8):
                dve.wait_ge(ada_up_loaded[s % 4], 16 * (s // 4 + 1))
                if s >= 1:
                    dve.wait_ge(ada_mm_done, s)
                ada_step(s, ada_up[s % 4], 0)
                ada_end(s)
            dve.wait_ge(lam_exp, 1)
            stt(neg_lam[:, :], lam_two[:, 1:2], -LAM_INIT, lam_two[:, 0:1], ALU.add, ALU.subtract).then_inc(lam_ready, 1)
            gain(0, SCALE_A, G_A, 8)
            rstd_end(N_X0, NB[:, :], DM, x_rstd)
            h_split(0, SHIFT_A, False)
            to_lo(0, 0)

            def v_pair(u):
                n = 2 * u - W_V
                for par in range(2):
                    to_lo(*next_chunk(u, par))
                    ada(n + par + S_KV, 0)
                    dve.wait_ge(v_gelu_done, 4 * u + 2 * par + 2)
                    ge(dve, v_sums_done, n + par)
                    for t in range(TB):
                        vt = v[:, t, bass.ds(256 * n + 256 * par, 256)]
                        last = stt(v_sq[:, t, :], vt, 1.0, vt, ALU.mult, ALU.mult, accum_out=v_sums[:, t, bass.ds(n + par, 1)])
                    last.then_inc(v_sums_done, 1)
                    ada_end(n + par + S_KV)

            v_pair(0)
            with dve.Fori(1, W_UZ // 2) as u:
                v_pair(u)
            dve.wait_ge(v_sums_done, GROUPS)
            nc.vector.tensor_reduce(v_stat[:, 0, :], v_sums[:, :, :], AX, ALU.add).then_inc(v_stat_dve, 1)
            dve.wait_ge(v_stat_act, 3)
            dve.wait_ge(v_stat_dve, 1)
            stt(v_stat[:, 4, :], v_stat[:, 0, :], AW * EPS, v_stat[:, 3, :], ALU.add, ALU.mult).then_inc(v_stat_dve, 1)
            dve.wait_ge(v_stat_dve, 2)
            stt(v_stat[:, 5, :], v_stat[:, 4, :], 1.5, v_stat[:, 2, :], ALU.subtract, ALU.mult, reverse0=True).then_inc(v_stat_dve, 1)

            def uz_pair(u):
                jj = 2 * u - W_UZ
                g = u - W_UZ // 2
                for par in range(2):
                    j = jj + par
                    to_lo(*next_chunk(u, par))
                    ada(j + S_B, 0)
                    dve.wait_ge(gelu_done, j + 1)
                    dve.wait_ge(tanh_done, j + 1)
                    stt(tanh_z[:, :], tanh_z[:, :], 1.0, G[2 * par + 1][:, :], ALU.add, ALU.mult).then_inc(acc_freed, 2)
                    dve.wait_ge(acc_freed, 2 * j + 2)
                    stt(gelu_u[par][:, :], tanh_z[:, :], 0.5, gelu_u[par][:, :], ALU.mult, ALU.mult).then_inc(uz_done, 1)
                    dve.wait_ge(mix_done, j + 1)
                    mix = mixed[par][:, :].rearrange("p (c t) -> p c t", c=TB)
                    stt(mix, (T0, T1)[par][:, :].rearrange("p (c t) -> p c t", c=TB), vecs[:, bass.ds(j + G_SGU, 1)],
                        b_sp[:, bass.ds(g, 1), :].broadcast_to([P, TB, P]), ALU.mult, ALU.add).then_inc(mix_freed, 1)
                    dve.wait_ge(mix_freed, j + 1)
                    dve.wait_ge(uz_done, j + 1)
                    nc.vector.tensor_tensor(mixed[par][:, :], mixed[par][:, :], gelu_u[par][:, :], ALU.mult).then_inc(y_done, 1)
                    dve.wait_ge(yhi_done, j + 1)
                    nc.vector.tensor_tensor(y_lo[:, :, bass.ds(j * P, P)], mix,
                                            f32(y_hi[:, j, :]).rearrange("p (c t) -> p c t", c=TB),
                                            ALU.subtract).then_inc(ylo_done, 1)
                    ada_end(j + S_B)

            dve.wait_ge(small_loaded, 64)
            uz_pair(W_UZ // 2)
            with dve.Fori(W_UZ // 2 + 1, W_OUTA // 2) as u:
                uz_pair(u)

            with dve.Fori(W_OUTA // 2, W_KV // 2) as u:
                for par in range(2):
                    m = 2 * u - W_OUTA + par
                    to_lo(*next_chunk(u, par))
                    ada(m + S_2, 8)
                    update_x(m, G[2 * par][:, :], GATE_A, 4 * u + 2 * par + 2, 2)
                    ada_end(m + S_2)
            gain(1, SCALE_KV, G_KV, S_KV + 8)
            rstd_end(N_X1, NB[:, :], DM, x_rstd)
            h_split(1, SHIFT_KV, True)

            with dve.Fori(W_KV // 2, W_B // 2) as u:
                for par in range(2):
                    j = 2 * u - W_KV + par
                    to_lo(*next_chunk(u, par))
                    ada(j + S_2 + 8, 8)
                    rstd_end(N_K + j, NB[:, :], P)
                    stt(k_t[:, j, :], G[2 * par][:, :], vecs[:, G_K:G_K + 1], rstd[:, :],
                        ALU.mult, ALU.mult).then_inc(acc_freed, 1)
                    dve.wait_ge(mm_done, 4 * u + 2 * par + 2)
                    nc.vector.tensor_copy(v_b[:, :, bass.ds(j * P, P)], G[2 * par + 1][:, :].rearrange("p (t n) -> p t n", t=TB))\
                        .then_inc(acc_freed, 1)
                    ada_end(j + S_2 + 8)
            gain(2, SCALE_B, G_B, S_B + 12)
            h_split(2, SHIFT_B, True)

            dve.wait_ge(gains_ready, 1)
            dve.wait_ge(blocks_loaded, 16)

            def head(n, p, mh, attend, project):
                m, q = n - 1, 1 - p
                u0 = n + W_B // 2
                k = 3 * n + N_Q

                def slope(g):
                    return consts[:, bass.ds(mh + (K_SLOPE + 8 * g + 4 * q), 1)]

                def weights(r):
                    dve.wait_ge(qk_done, 4 * m + r + 1)
                    stt(s_b[:, 0:TOK], blocks[:, 3 - r:7 - r, :].rearrange("p b n -> p (b n)"), slope(0), G[2][:, :], ALU.mult, ALU.add)
                    for g in (1, 2):
                        last = stt(s_b[:, TOK + P * (g - 1):TOK + P * g], blocks[:, 6 + g, :], slope(g), G[3][:, P * (g - 1):P * g],
                                   ALU.mult, ALU.add)
                    last.then_inc(s_freed, 1)
                    dve.wait_ge(s_freed, 4 * m + r + 1)
                    nc.vector.tensor_reduce(row_stat[:, 0, r:r + 1], s_b[:, :], AX, ALU.max, negate=True).then_inc(max_done, 1)
                    dve.wait_ge(exp_done, 4 * m + r + 1)
                    nc.vector.reciprocal(row_stat[:, 2, r:r + 1], row_stat[:, 1, r:r + 1]).then_inc(inv_done, 1)
                    dve.wait_ge(inv_done, 4 * m + r + 1)
                    nc.vector.tensor_scalar(s_b[:, :], s_b[:, :], row_stat[:, 2, r:r + 1], None, ALU.mult).then_inc(p_ready, 1)

                def turn_copy(r):
                    dve.wait_ge(turn_done, 4 * m + r + 1)
                    nc.vector.tensor_copy(p_t[:, TOK:768], T1[:, 0:256]).then_inc(pt_dve, 1)

                def q_norm(mi):
                    rstd_end(k + mi, NB[:, :], P)
                    stt(q_n[p][:, mi, :], G[mi % 2][:, :], gains[:, 0:1], rstd[:, :], ALU.mult, ALU.mult).then_inc(acc_freed, 1)

                if project:
                    to_lo(u0, 1)
                if attend:
                    weights(0)
                    turn_copy(0)
                    weights(1)
                if project:
                    q_norm(0)
                    to_lo(u0 + 1, 0)
                if attend:
                    turn_copy(1)
                    weights(2)
                if project:
                    q_norm(1)
                if attend:
                    turn_copy(2)
                    weights(3)
                if project:
                    q_norm(2)
                if attend:
                    turn_copy(3)
                    dve.wait_ge(pv_done, 4 * m + 4)
                    dve.wait_ge(acc_freed, 2 * (2 * n + W_B) - 16)
                    stt(yb[:, :], z_b[:, :], 0.5, AD[:, :], ALU.mult, ALU.mult).then_inc(head_out, 1)
                    dve.wait_ge(ybhi_done, m + 1)
                    nc.vector.tensor_tensor(yb_lo[:, mh + 4 * q, :], yb[:, :], f32(yb_hi[:, mh + 4 * q, :]), ALU.subtract)\
                        .then_inc(yblo_done, 1)
                if project:
                    dve.wait_ge(tanhz_done, n + 1)
                    stt(z_b[:, :], z_t[:, :], 1.0, G[1][:, :], ALU.add, ALU.mult).then_inc(acc_freed, 1)

            head(0, 0, 0, False, True)
            with dve.Fori(1, QH // 2) as i:
                head(2 * i - 1, 1, i - 1, True, True)
                head(2 * i, 0, i - 1, True, True)
            head(QH - 1, 1, QH // 2 - 1, True, True)
            head(QH, 0, QH // 2 - 1, True, False)

            with dve.Fori(W_OUTB // 2, W_Q2 // 2) as u:
                c = u - W_OUTB // 2
                for par in range(2):
                    to_lo(*next_chunk(u, par))
                    for e in ((0, 1) if par == 0 else (2,)):
                        ada(3 * c + (S_2 + 14 + e), 8)
                        if e == 0:
                            ada_end(3 * c + (S_2 + 14))
                    for half in range(2):
                        update_x(4 * c + 2 * par + half, G[2 * par + half][:, :], GATE_B, 4 * u + 2 * par + half + 1, 1, True)
                    ada_end(3 * c + (S_2 + 15 + par))
            dve.wait_ge(wfhi_done, 1)
            nc.vector.tensor_tensor(wf_lo[:, :, 0:8], wf_raw[:, :, :], f32(wf_hi[:, :, 0:8]), ALU.subtract).then_inc(wflo_done, 1)
            gain(3, SCALE_1, G_LN1, S_2 + 8)
            rstd_end(N_X2, NB[:, :], DM, x_rstd)
            h_split(3, SHIFT_1, False)

            nc.vector.memset(gate_one[:, :], 1.0).then_inc(fgate_dve, 1)
            dve.wait_ge(fgate_act, 1)
            nc.vector.tensor_scalar(gate_min[:, :], T0[0:8, :], bf_col[:, :], 0.0, ALU.add, ALU.min).then_inc(fgate_dve, 1)
            dve.wait_ge(fgate_act, 3)
            dve.wait_ge(fgate_dve, 2)
            nc.vector.tensor_tensor(gate_log[:, :], gate_min[:, :], gate_ln[:, :], ALU.subtract).then_inc(fgate_dve, 1)
            dve.wait_ge(fgate_dve, 3)
            nc.vector.tensor_tensor_scan(cum[:, :], gate_one[:, :], gate_log[:, :], 0.0, ALU.mult, ALU.add).then_inc(fgate_dve, 1)
            dve.wait_ge(c_turned, 1)
            nc.vector.tensor_copy(c_col[:, :, :], T1[:, 0:32].rearrange("p (t h) -> p t h", t=TB)).then_inc(c_col_ready, 1)
            dve.wait_ge(c_col_ready, 1)

            for t in range(5):
                w0 = W_Q2 + 3 * t
                a = t - 1
                attend, project = t >= 1, t < 4
                units = units2(a)
                if attend:
                    dve.wait_ge(c_row_ready, 2 * a + 2)
                for u in range(13):
                    if project and u in (0, 4, 8):
                        to_lo(*divmod(w0 + u // 4 + 1, 2))
                    if attend and u < 12:
                        kind, qb = units[u]
                        width, n0 = (qb + 1) * P, 12 * a + u
                        before, first = s_reads(u)
                        sets = 2 if kind == 2 else 1
                        dve.wait_ge(qk2_done, n0 + 1)
                        for n in range(sets):
                            s, score = s_2[u % 2][:, n, 0:width], G[2 + (first + n) % 2][:, 0:width]
                            if kind == 2:
                                biased = stt(s, consts[:, K_DIST + TOK - width:K_DIST + TOK], -SLOPES_D[a], score, ALU.mult, ALU.add)
                            else:
                                biased = stt(s, score, c_col[:, qb, 2 * a + kind:2 * a + kind + 1], c_row[kind][:, 0:width],
                                             ALU.add, ALU.subtract)
                            biased.then_inc(s2_freed, 1)
                        dve.wait_ge(s2_freed, 16 * a + before + sets)
                        if kind < 2:
                            s = s_2[u % 2][:, 0, width - P:width]
                            nc.vector.tensor_tensor(s, s, consts[:, K_MASK:K_MASK + P], ALU.add).then_inc(bias2_done, 1)
                            dve.wait_ge(bias2_done, 8 * a + sum(1 for e in units[:u + 1] if e[0] < 2))
                        nc.vector.tensor_reduce(stat2[:, 0, u % 2, 0:sets], s_2[u % 2][:, 0:sets, 0:width], AX, ALU.max, negate=True)\
                            .then_inc(max2_done, 1)
                        dve.wait_ge(exp2_done, n0 + 1)
                        i0 = 20 * a + u + sum(2 for e in units[:u] if e[0] == 2)
                        nc.vector.reciprocal(stat2[:, 2, u % 2, 0:sets], stat2[:, 1, u % 2, 0:sets]).then_inc(inv2_done, 1)
                        dve.wait_ge(inv2_done, i0 + 1)
                        p1 = s_2[u % 2][:, 0, 0:width]
                        if kind < 2:
                            nc.vector.tensor_scalar(p1, p1, stat2[:, 2, u % 2, 0:1], None, ALU.mult).then_inc(p2_ready, 1)
                        else:
                            nc.vector.tensor_scalar(p1, p1, stat2[:, 2, u % 2, 0:1], None, ALU.mult).then_inc(inv2_done, 1)
                            nc.vector.tensor_tensor(lam_inv[:, 0:1], stat2[:, 2, u % 2, 1:2], neg_lam[:, :], ALU.mult).then_inc(inv2_done, 1)
                            dve.wait_ge(inv2_done, i0 + 3)
                            stt(p1, s_2[u % 2][:, 1, 0:width], lam_inv[:, 0:1], p1, ALU.mult, ALU.add).then_inc(p2_ready, 1)
                    if project and u in (2, 4, 6, 8):
                        mi = u // 2 - 1
                        rstd_end(norm2(t, mi), NB[:, :], 64)
                        stt(qk[t % 2][mi][:, :], G[mi % 2][:, :], gains[:, 1 + mi:2 + mi], rstd[:, :], ALU.mult, ALU.mult).then_inc(acc_freed, 1)
                    if project and u in (10, 12):
                        mi = u // 2 - 1
                        dve.wait_ge(mm_done, 2 * w0 + mi + 1)
                        nc.vector.tensor_copy(v_2[t % 2][mi - 4][:, :, :], G[mi % 2][:, :].rearrange("p (t n) -> p t n", t=TB)).then_inc(acc_freed, 1)
                if attend:
                    k = norm2(t, 4)
                    dve.wait_ge(mhi_done, 2 * a + 1)
                    nc.vector.tensor_tensor(m_lo[:, a, :], AD[:, :], f32(m_hi[:, a, :]), ALU.subtract).then_inc(mlo_done, 1)
                    rstd_end(k, NB[:, :], P)
                    stt(d_out[:, :], T1[:, :], gains[:, 5:6], rstd[:, :], ALU.mult, ALU.mult).then_inc(d_done, 1)
                    dve.wait_ge(mhi_done, 2 * a + 2)
                    nc.vector.tensor_tensor(m_lo[:, 4 + a, :], d_out[:, :], f32(m_hi[:, 4 + a, :]), ALU.subtract).then_inc(mlo_done, 1)

            with dve.Fori(W_OUT2 // 2, W_GU1 // 2) as u:
                c = u - W_OUT2 // 2
                for par in range(2):
                    to_lo(*next_chunk(u, par))
                    ada(2 * c + (S_2 + 20 + par), 8)
                    for half in range(2):
                        update_x(4 * c + 2 * par + half, G[2 * par + half][:, :], GATE_1, 4 * u + 2 * par + half + 1, 1)
                    ada_end(2 * c + (S_2 + 20 + par))
            gain(4, SCALE_2, G_LN2, S_2 + 20)
            rstd_end(N_X3, NB[:, :], DM, x_rstd)
            h_split(4, SHIFT_2, False)

            def gate_up(u, f, par, first):
                to_lo(*next_chunk(u, par))
                dve.wait_ge(tanhg_done, f + first + 1)
                stt(tanh_g[par][:, :], tanh_g[par][:, :], 1.0, G[2 * par][:, :], ALU.add, ALU.mult).then_inc(acc_freed, 1)
                dve.wait_ge(mm_done, 4 * u + 2 * par + 2)
                dve.wait_ge(acc_freed, 4 * u + 2 * par - 15)
                stt(gu[par][:, :], tanh_g[par][:, :], 0.5, G[2 * par + 1][:, :], ALU.mult, ALU.mult).then_inc(acc_freed, 1)
                dve.wait_ge(guhi_done, f + first + 1)
                nc.vector.tensor_tensor(gu_lo[:, f, :], gu[par][:, :], f32(gu_hi[:, f, :]), ALU.subtract).then_inc(gulo_done, 1)

            with dve.Fori(W_GU1 // 2, W_DN1 // 2) as u:
                for par in range(2):
                    gate_up(u, 2 * (u - W_GU1 // 2) + par, par, 0)
            with dve.Fori(W_DN1 // 2, W_GU2 // 2) as u:
                for par in range(2):
                    to_lo(*next_chunk(u, par))
                    update_x(2 * (u - W_DN1 // 2) + par, G[2 * par][:, :], GATE_2, 4 * u + 2 * par + 2, 2)
            with dve.Fori(W_GU2 // 2, W_DN2 // 2) as u:
                for par in range(2):
                    gate_up(u, 2 * (u - W_GU2 // 2) + par, par, FF1)
            for c in range(4):
                w = W_DN2 + c
                if c < 3:
                    to_lo(*divmod(w + 1, 2))
                for half in range(2):
                    update_x(2 * c + half, G[2 * (w % 2) + half][:, :], GATE_2, 2 * w + half + 1, 1)

        @block.tensor
        def _(pe):
            def mm(out, lhsT, rhs, start, stop):
                return nc.tensor.matmul(out, lhsT, rhs, start=start, stop=stop)

            def split(out, parts, n):
                for kt in range(n):
                    a_hi, a_lo, b_hi, b_lo = parts(kt)
                    mm(out, a_hi, b_hi, kt == 0, False)
                    mm(out, a_hi, b_lo, False, False)
                    last = mm(out, a_lo, b_hi, False, kt == n - 1)
                return last

            def columns(out, par, half, kts, hi, lo, lo_kt, pieces=None):
                n = 256 if kts <= KT else P
                wh = w_hi[par][:, 0:kts * n].rearrange("p (k n) -> p k n", k=kts)
                wl = w_lo[par][:, 0:kts * n].rearrange("p (k n) -> p k n", k=kts)
                for kt in pieces or range(kts):
                    a_hi, a_lo = wh[:, kt, P * half:P * half + P], wl[:, kt, P * half:P * half + P]
                    mm(out, a_hi, hi[:, kt, :], kt == 0, False)
                    mm(out, a_hi, lo_kt(kt), False, False)
                    last = mm(out, a_lo, hi[:, kt, :], False, kt == kts - 1)
                return last

            def h_lo_of(kt):
                return h_lo[:, kt, :]

            def rows(out, par, t, lo, n):
                wh = w_hi[par][:, :].rearrange("p (k n) -> p k n", k=KT)
                wl = w_lo[par][:, :].rearrange("p (k n) -> p k n", k=KT)
                s = slice(P * t, P * t + P)
                return split(out, lambda kt: (h_hi[:, kt, s], h_lo[:, kt, s], wh[:, kt, lo:lo + n], wl[:, kt, lo:lo + n]), KT)

            def chunk_ready(u, par):
                pe.wait_ge(lo_done, 2 * u + par + 1)

            def ada_sum_up(s):
                pe.wait_ge(ada_sum, 8 * s + 8)
                ge(pe, ada_out, s)
                mm(AD[:, 0:1], ada_acc[:, 0:P], ones[:, 0:1], True, True)
                mm(AD[:, 1:2], ada_acc[:, P:2 * P], ones[:, 0:1], True, True).then_inc(ada_mm_done, 1)

            def first_h(e):
                pe.wait_ge(hlo_done, 8 * e + 8)

            def open_squares(base, k):
                pe.wait_ge(sq_ready, base + 1)
                pe.wait_ge(newton_done, k)
                mm(NB[:, :], ones, sq[1][:, :], True, False)

            def add_squares(m, slot, base, last=False):
                pe.wait_ge(sq_ready, base + m + 2)
                added = mm(NB[:, :], ones, sq[slot][:, :], False, last)
                if last:
                    added.then_inc(sum_done, 1)

            pe.wait_ge(consts_loaded, 16)
            pe.wait_ge(rows_loaded, 16 * (len(MODS) + 11 + 4))
            nc.tensor.transpose(AD[:, 0:NVEC], rows_vec[:, :], ident[0:NVEC, 0:NVEC])
            nc.tensor.transpose(AD[:, P:P + NMOD], rows_mod[:, :], ident[0:NMOD, 0:NMOD]).then_inc(rows_turned, 1)
            pe.wait_ge(ws_loaded, 16)
            for g in range(GROUPS):
                turned = nc.tensor.transpose((T0, T1)[g // 4][:, P * (g % 4):P * (g % 4) + P], ws_raw[:, g, :], ident)
            turned.then_inc(ws_turned, 1)
            pe.wait_ge(x_loaded, 16)
            for kt in range(KT):
                if kt >= 4:
                    pe.wait_ge(x_copied, kt - 3)
                for t in range(TB):
                    turned = nc.tensor.transpose(G[kt % 4][:, P * t:P * t + P], x_tok[:, t, P * kt:P * kt + P], ident)
                turned.then_inc(x_turned, 1)
            for kt in range(KT):
                pe.wait_ge(sq_ready, kt + 1)
                summed = mm(NB[:, :], ones, sq_first[kt][:, :], kt == 0, kt == KT - 1)
            summed.then_inc(sum_done, 1)
            pe.wait_ge(vecs_ready, 2)
            for s in range(8):
                ada_sum_up(s)
            first_h(0)

            def v_pair(u):
                n = 2 * u - W_V
                for par in range(2):
                    chunk_ready(u, par)
                    for hb in range(2):
                        ge(pe, v_gelu_done, 4 * u + 2 * par + hb - 3)
                        for t in range(2):
                            last = rows(G[2 * par + hb][:, 256 * t:256 * t + 256], par, 2 * hb + t, 0, 256)
                        last.then_inc(mm_done, 1)
                    ada_sum_up(n + par + S_KV)

            v_pair(0)
            with pe.Fori(1, W_UZ // 2) as u:
                v_pair(u)

            def uz_pair(u):
                jj = 2 * u - W_UZ
                for par in range(2):
                    j = jj + par
                    chunk_ready(u, par)
                    if isinstance(u, int):
                        pe.wait_ge(v_gelu_done, 2 * (W_UZ - 2 + par) + 2)
                    else:
                        pe.wait_ge(acc_freed, 2 * j - 2)
                    for half in range(2):
                        columns(G[2 * par + half][:, :], par, half, KT, h_hi, h_lo, h_lo_of).then_inc(mm_done, 1)
                    pe.wait_ge(v_staged, j + 1)
                    ge(pe, mix_freed, j - 1)
                    for c in range(TB):
                        mixed_c = mm((T0, T1)[par][:, P * c:P * c + P], v_stage[par][:, c, :], ws_t[:, u - W_UZ // 2, :], True, True)
                    mixed_c.then_inc(mix_done, 1)
                    ada_sum_up(j + S_B)

            pe.wait_ge(ws_ready, 2)
            uz_pair(W_UZ // 2)
            with pe.Fori(W_UZ // 2 + 1, W_OUTA // 2) as u:
                uz_pair(u)

            pe.wait_ge(ylo_done, AT)
            open_squares(SQ1, N_X1)
            with pe.Fori(W_OUTA // 2, W_KV // 2) as u:
                for par in range(2):
                    m = 2 * u - W_OUTA + par
                    chunk_ready(u, par)
                    pe.wait_ge(acc_freed, 4 * u + 2 * par - 18)
                    columns(G[2 * par][:, :], par, 0, AT, y_hi, y_lo, lambda kt: y_lo[:, :, P * kt:P * kt + P]).then_inc(mm_done, 2)
                    add_squares(m - 1, 1 - par, SQ1)
                    ada_sum_up(m + S_2)
            add_squares(KT - 1, 1, SQ1, True)
            first_h(1)

            with pe.Fori(W_KV // 2, W_B // 2) as u:
                for par in range(2):
                    j = 2 * u - W_KV + par
                    chunk_ready(u, par)
                    pe.wait_ge(acc_freed, 4 * u + 2 * par - 18)
                    columns(G[2 * par][:, :], par, 0, KT, h_hi, h_lo, h_lo_of).then_inc(mm_done, 1)
                    for t in range(TB):
                        last = rows(G[2 * par + 1][:, P * t:P * t + P], par, t, P, P)
                    last.then_inc(mm_done, 1)
                    pe.wait_ge(qsq_ready, j + 1)
                    pe.wait_ge(newton_done, j + N_K)
                    mm(NB[:, :], ones, sq[par][:, :], True, True).then_inc(sum_done, 1)
                    ada_sum_up(j + S_2 + 8)
            first_h(2)

            def head(n, p, mh, attend, project):
                m, q = n - 1, 1 - p
                u0 = n + W_B // 2
                w0 = 2 * n + W_B
                k = 3 * n + N_Q

                def piece(mi):
                    if mi % 2 == 0:
                        chunk_ready(u0, mi // 2)
                    pe.wait_ge(acc_freed, 2 * w0 + mi - 17)
                    columns(G[mi % 2][:, :], mi // 2, mi % 2, KT, h_hi, h_lo, h_lo_of).then_inc(mm_done, 1)

                def squares(mi):
                    pe.wait_ge(qsq_ready, k + mi - N_Q + NKV + 1)
                    pe.wait_ge(newton_done, k + mi)
                    mm(NB[:, :], ones, sq[(mi + p) % 2][:, :], True, True).then_inc(sum_done, 1)

                def scores(r):
                    if r == 0:
                        pe.wait_ge(acc_freed, 2 * w0 - 17)
                    pe.wait_ge(s_freed, 4 * m + r) if not (isinstance(n, int) and n == 1 and r == 0) else None
                    s = slice(P * r, P * r + P)
                    mm(G[2][:, :], q_n[q][:, 0, s], k_t[:, q, :], True, True)
                    mm(G[3][:, 0:P], q_n[q][:, 1, s], k_t[:, 2 + q, s], True, True)
                    mm(G[3][:, P:2 * P], q_n[q][:, 2, s], k_t[:, 4 + q, s], True, True).then_inc(qk_done, 1)

                def turn(r):
                    pe.wait_ge(p_ready, 4 * m + r + 1)
                    for b in range(6):
                        bank = T0[:, P * b:P * b + P] if b < 4 else T1[:, P * (b - 4):P * (b - 3)]
                        turned = nc.tensor.transpose(bank, s_b[:, P * b:P * b + P], ident)
                    turned.then_inc(turn_done, 1)

                def values(r):
                    pe.wait_ge(pt_act, 4 * m + r + 1)
                    pe.wait_ge(pt_dve, 4 * m + r + 1)
                    if r == 0 and not (isinstance(n, int) and n == 1):
                        pe.wait_ge(head_out, m)
                    for b in range(6):
                        block_v, g = (b, 0) if b < 4 else (r, b - 3)
                        last = mm(AD[:, P * r:P * r + P], v_b[:, block_v, P * (2 * g + q):P * (2 * g + q + 1)], p_t[:, P * b:P * b + P],
                                  b == 0, b == 5)
                    last.then_inc(pv_done, 1)

                if attend:
                    scores(0)
                if project:
                    piece(0)
                for r in range(4):
                    if attend:
                        turn(r)
                        if r < 3:
                            scores(r + 1)
                        values(r)
                    if project and r < 3:
                        squares(r)
                        piece(r + 1)

            head(0, 0, 0, False, True)
            head(1, 1, 0, True, True)
            head(2, 0, 0, True, True)
            with pe.Fori(2, QH // 2) as i:
                head(2 * i - 1, 1, i - 1, True, True)
                head(2 * i, 0, i - 1, True, True)
            head(QH - 1, 1, QH // 2 - 1, True, True)
            head(QH, 0, QH // 2 - 1, True, False)

            def out_chunk(u, par, c, hi, lo, base, between):
                chunk_ready(u, par)
                for half in range(2):
                    m = 4 * c + 2 * par + half
                    pe.wait_ge(acc_freed, 4 * u + 2 * par + half - 17)
                    columns(G[2 * par + half][:, :], par, half, KT, hi, lo, lambda kt: lo[:, kt, :]).then_inc(mm_done, 1)
                    between(half)
                    add_squares(m - 1, 1 - half, base)

            pe.wait_ge(yblo_done, QH)
            pe.wait_ge(s_freed, 4 * QH)
            open_squares(SQ2, N_X2)
            with pe.Fori(W_OUTB // 2, W_Q2 // 2) as u:
                c = u - W_OUTB // 2
                for par in range(2):
                    def between(half):
                        if half == 0 and par == 0:
                            ada_sum_up(3 * c + (S_2 + 14))
                    out_chunk(u, par, c, yb_hi, yb_lo, SQ2, between)
                    ada_sum_up(3 * c + (S_2 + 15 + par))
            add_squares(KT - 1, 1, SQ2, True)
            first_h(3)

            pe.wait_ge(wflo_done, 1)
            split(T0[:, :], lambda kt: (wf_hi[:, kt, :], wf_lo[:, kt, :], h_hi[:, kt, :], h_lo[:, kt, :]), KT).then_inc(fg_done, 1)
            pe.wait_ge(fgate_dve, 4)
            for t in range(TB):
                turned = nc.tensor.transpose(T1[:, 8 * t:8 * t + 8], cum[:, P * t:P * t + P], ident[0:8, 0:8])
            turned.then_inc(c_turned, 1)

            for t in range(5):
                w0 = W_Q2 + 3 * t
                a = t - 1
                attend, project = t >= 1, t < 4
                units = units2(a)
                if attend:
                    ge(pe, mlo_done, 2 * a)
                    ge(pe, pt2_done, 12 * a)
                    pe.wait_ge(c_col_ready, 1)
                    for n, bank in enumerate((T0, T1)):
                        mm(bank[:, :], ident[0:8, 2 * a + n:2 * a + n + 1].broadcast_to([8, P]), cum[:, :], True, True).then_inc(c_spread, 1)

                def turn(u):
                    kind, qb = units[u]
                    pe.wait_ge(p2_ready, 12 * a + u + 1)
                    if u == 0:
                        pe.wait_ge(c_row_ready, 2 * a + 2)
                    ge(pe, pt2_done, 12 * a + u)
                    for b in range(qb + 1):
                        turned = nc.tensor.transpose(T0[:, P * b:P * b + P], s_2[u % 2][:, 0, P * b:P * b + P], ident)
                    turned.then_inc(turn2_done, 1)

                def values(u):
                    kind, qb = units[u]
                    pe.wait_ge(pt2_done, 12 * a + u + 1)
                    for b in range(qb + 1):
                        pt = pt_2[u % 2][:, P * b:P * b + P]
                        if kind == 2:
                            out, vt = T1[:, P * qb:P * qb + P], v_2[a % 2][1][:, b, :]
                        else:
                            out, vt = AD[64 * kind:64 * kind + 64, P * qb:P * qb + P], v_2[a % 2][0][:, b, 64 * kind:64 * kind + 64]
                        last = mm(out, vt, pt, b == 0, b == qb)
                    last.then_inc(pv2_done, 1)

                for u in range(12):
                    if attend:
                        kind, qb = units[u]
                        before, first = s_reads(u)
                        if u == 0:
                            pe.wait_ge(acc_freed, 2 * w0 - 16)
                        for n in range(2 if kind == 2 else 1):
                            if 16 * a + before + n >= 2:
                                pe.wait_ge(s2_freed, 16 * a + before + n - 1)
                            half = slice(64 * n, 64 * n + 64) if kind == 2 else slice(64 * kind, 64 * kind + 64)
                            qt, kt_ = (qk[a % 2][2], qk[a % 2][3]) if kind == 2 else (qk[a % 2][0], qk[a % 2][1])
                            score = mm(G[2 + (first + n) % 2][:, 0:(qb + 1) * P], qt[half, P * qb:P * qb + P], kt_[half, 0:(qb + 1) * P], True, True)
                        score.then_inc(qk2_done, 1)
                        if u >= 1:
                            turn(u - 1)
                        if u >= 2:
                            values(u - 2)
                    if project:
                        mi, w = u // 2, w0 + u // 4
                        par = w % 2
                        if u % 4 == 0:
                            pe.wait_ge(lo_done, w + 1)
                        if u % 2 == 0:
                            pe.wait_ge(acc_freed, 2 * w0 + mi - 17)
                        if mi < 4:
                            last = columns(G[mi % 2][:, :], par, mi % 2, KT, h_hi, h_lo, h_lo_of, range(4 * (u % 2), 4 * (u % 2) + 4))
                        else:
                            for tt in (2 * (u % 2), 2 * (u % 2) + 1):
                                last = rows(G[mi % 2][:, P * tt:P * tt + P], par, tt, P * (mi % 2), P)
                        if u % 2 == 1:
                            last.then_inc(mm_done, 1)
                        if u in (2, 4, 6, 8):
                            k = norm2(t, u // 2 - 1)
                            pe.wait_ge(qsq_ready, k - N_2 + 31)
                            pe.wait_ge(newton_done, k)
                            mm(NB[:, :], half_ones, sq[k % 2][:, :], True, True).then_inc(sum_done, 1)
                if attend:
                    turn(11)
                    values(10)
                    values(11)
                    k = norm2(t, 4)
                    pe.wait_ge(qsq_ready, k - N_2 + 31)
                    pe.wait_ge(newton_done, k)
                    mm(NB[:, :], ones, sq[k % 2][:, :], True, True).then_inc(sum_done, 1)

            pe.wait_ge(mlo_done, KT)
            open_squares(SQ3, N_X3)
            with pe.Fori(W_OUT2 // 2, W_GU1 // 2) as u:
                c = u - W_OUT2 // 2
                for par in range(2):
                    out_chunk(u, par, c, m_hi, m_lo, SQ3, lambda half: None)
                    ada_sum_up(2 * c + (S_2 + 20 + par))
            add_squares(KT - 1, 1, SQ3, True)
            first_h(4)

            def gate_up(u):
                for par in range(2):
                    chunk_ready(u, par)
                    for half in range(2):
                        pe.wait_ge(acc_freed, 4 * u + 2 * par + half - 19)
                        columns(G[2 * par + half][:, :], par, half, KT, h_hi, h_lo, h_lo_of).then_inc(mm_done, 1)

            def gu_lo_of(kt):
                return gu_lo[:, kt, :]

            with pe.Fori(W_GU1 // 2, W_DN1 // 2) as u:
                gate_up(u)
            pe.wait_ge(gulo_done, FF1)
            with pe.Fori(W_DN1 // 2, W_GU2 // 2) as u:
                for par in range(2):
                    chunk_ready(u, par)
                    pe.wait_ge(acc_freed, 4 * u + 2 * par - 18)
                    columns(G[2 * par][:, :], par, 0, FF1, gu_hi, gu_lo, gu_lo_of).then_inc(mm_done, 2)
            with pe.Fori(W_GU2 // 2, W_DN2 // 2) as u:
                gate_up(u)
            pe.wait_ge(gulo_done, FF1 + FF2)

            def result(m):
                pe.wait_ge(acc_freed, 2 * W_DN2 - 15 + m)
                ge(pe, o_copied, m - 1)
                for t in range(TB):
                    turned = nc.tensor.transpose((T0, T1)[m % 2][:, P * t:P * t + P], x[:, m, P * t:P * t + P], ident)
                turned.then_inc(o_turned, 1)

            for c in range(4):
                w = W_DN2 + c
                chunk_ready(*divmod(w, 2))
                for half in range(2):
                    pe.wait_ge(acc_freed, 2 * w + half - 19)
                    columns(G[2 * (w % 2) + half][:, :], w % 2, half, FF2, gu_hi, gu_lo, gu_lo_of).then_inc(mm_done, 1)
                if c >= 1:
                    result(2 * c - 2)
                    result(2 * c - 1)
            result(6)
            result(7)


INPUTS = ["x", "c", "a_ada_w", "a_ada_b", "a_norm_g", "a_w_in", "a_sgu_g", "a_w_spatial", "a_b_spatial", "a_w_out", "kv_ada_w",
          "kv_ada_b", "kv_norm_g", "w_kv", "k_norm_g", "b_ada_w", "b_ada_b", "b_norm_g", "b_w_in", "b_q_norm_g", "b_w_out", "c_2",
          "ln1_g_2", "ln2_g_2", "w_ada_2", "b_ada_2", "w_in_2", "b_f_2", "fox_qk_g_2", "diff_qk_g_2", "diff_lam_2", "diff_norm_g_2",
          "w_out_2", "w_gate_2", "w_up_2", "w_down_2"]


def kernel(**inputs):
    from concourse import bacc
    from concourse.bass_utils import run_bass_kernel_spmd

    nc = bacc.Bacc("TRN2", target_bir_lowering=False, num_devices=1)
    arrays = {f"in_{name}": np.ascontiguousarray(inputs[name]) for name in INPUTS}
    arrays["in_tiles"], arrays["in_blocks"] = constants()
    d = {n[3:]: nc.dram_tensor(n, a.shape, mybir.dt.from_np(a.dtype), kind="ExternalInput").ap() for n, a in arrays.items()}
    d["out"] = nc.dram_tensor("out", (1, TOK, DM), F32, kind="ExternalOutput").ap()
    program(nc, d)
    run = run_bass_kernel_spmd(nc, [arrays], core_ids=[0])
    return run.results[0]["out"]
```

```python
import math

import numpy as np

import concourse.bass as bass
from concourse import mybir
from concourse.alu_op_type import AluOpType as ALU

F32 = mybir.dt.float32
F32R = mybir.dt.float32r
ACT = mybir.ActivationFunctionType
AX = mybir.AxisListType.X

P = 128
TOK = 512
TB = TOK // P
DM = 1024
KT = DM // P
EPS = 1e-6
AW = 2 * DM
AT = AW // P
GROUPS = 8
QH = DM // P
NKV = 6
SLOPES_B = [2.0 ** (-8.0 * h / 24) for h in range(1, 25)]
SLOPES_D = [2.0 ** (-8.0 * h / 4) for h in range(1, 5)]
FF = 2816
FF1, FF2 = 16, 6
LAM_INIT = 0.8 - 0.6 * math.exp(0.0)
FAR = 1e30

W_V = 0
W_UZ = W_V + 8
W_OUTA = W_UZ + 16
W_KV = W_OUTA + 8
W_B = W_KV + 6
W_OUTB = W_B + 16
W_Q2 = W_OUTB + 4
W_OUT2 = W_Q2 + 12
W_GU1 = W_OUT2 + 4
W_DN1 = W_GU1 + FF1
W_GU2 = W_DN1 + 8
W_DN2 = W_GU2 + FF2
W_END = W_DN2 + 4

MODS = [("a", 0, 8), ("kv", 0, 8), ("b", 0, 12), ("a", 8, 4), ("2", 0, 24)]
UP = 8
S_OUTB, S_OUT2, S_END = 38, 44, 48
SHIFT_A, SCALE_A, SHIFT_KV, SCALE_KV = 0, 8, 16, 24
SHIFT_B, SCALE_B, GATE_B, GATE_A = 32, 40, 48, 56
SHIFT_1, SCALE_1, GATE_1, SHIFT_2, SCALE_2, GATE_2 = 64, 72, 80, 88, 96, 104
NMOD = 112

C_1, C_2, G_A, G_KV, G_B, G_LN1, G_LN2, G_SGU = 0, 8, 16, 24, 32, 40, 48, 56
G_K, G_QB, G_DN, G_FQ, G_FK, G_DQ, G_DK = 72, 73, 74, 75, 76, 77, 78
NVEC = 79


def constants():
    i, j = np.arange(P)[:, None], np.arange(P)[None, :]
    ident = np.eye(P)
    ones = np.ones((P, P))
    half = np.kron(np.eye(2), np.ones((64, 64)))
    causal_t = (i <= j) * 1.0
    blocks = []
    for shift in range(3, -4, -1):
        d = 4 * (i - j) + shift
        blocks.append(np.where((d >= 0) & (d <= P), d, FAR))
    d4 = 4 * (i - j)
    blocks.append(np.where(d4 >= 0, d4, FAR))
    blocks.append(np.where((d4 >= 0) & (d4 % 16 == 0), d4, FAR))
    x = np.arange(TOK)[None, :]
    d = i + TOK - P - x
    slopes = np.broadcast_to(-np.array(SLOPES_B, np.float32), (P, 24))
    last = np.broadcast_to(np.array([EPS, 0.0, 0.0, 0.0]), (P, 4))
    tiles = [ident, ones, half, causal_t, np.where(d >= 0, d, FAR), np.where(i >= j, 0.0, -FAR), slopes, last]
    return [np.concatenate(part, axis=1).astype(np.float32) for part in (tiles, blocks)]


K_ID, K_ONE, K_HALF, K_TRI, K_DIST, K_MASK = 0, P, 2 * P, 3 * P, 4 * P, 4 * P + TOK
K_SLOPE = K_MASK + P
K_EPS = K_SLOPE + 24
NCONST = K_EPS + 4


def program(nc, d):
    base = 16512
    top = [base]

    def at(name, shape, off, dt=F32):
        return nc.alloc_sbuf_tensor_at(name, shape, dt, offset=off)

    def take(nbytes):
        off = top[0]
        top[0] += (nbytes + 63) // 64 * 64
        return off

    KB = 1024
    x = at("x", [P, KT, TOK], take(16 * KB))
    h_hi = at("h_hi", [P, KT, TOK], take(16 * KB), F32R)
    off_hlo = take(16 * KB)
    h_lo = at("h_lo", [P, KT, TOK], off_hlo, F32R)
    w_raw = [at(f"w_raw{s}", [P, 2048], take(8 * KB)) for s in range(2)]
    w_hi = [at(f"w_hi{s}", [P, 2048], take(8 * KB), F32R) for s in range(2)]
    w_lo = [at(f"w_lo{s}", [P, 2048], take(8 * KB), F32R) for s in range(2)]
    off_ada = take(8 * KB)
    ada_raw = at("ada_raw", [P, KT, 256], off_ada)
    consts = at("consts", [P, NCONST], take(4 * NCONST))
    vecs = at("vecs", [P, NVEC + NMOD], take(4 * (NVEC + NMOD)))
    mod_bias = vecs[:, NVEC:NVEC + NMOD]
    mods = at("mods", [P, NMOD], take(4 * NMOD))
    silu_c = at("silu_c", [P, 16], take(64))
    gains = at("gains", [P, 8], take(32))
    gscale = at("gscale", [P, 8], take(32))
    ada_acc = at("ada_acc", [P, 256], take(KB))
    x_rstd = at("x_rstd", [P, TOK], take(2 * KB))
    v_sums = at("v_sums", [P, TB, GROUPS], take(128))
    v_stat = at("v_stat", [P, 8, TB], take(128))
    row_stat = at("row_stat", [P, 3, 4], take(64))
    stat2 = at("stat2", [P, 3, 2, 2], take(64))
    lam_inv = at("lam_inv", [P, 2], take(8))
    lam_two = at("lam_two", [P, 2], take(8))
    neg_lam = at("neg_lam", [P, 1], take(4))
    c_col = at("c_col", [P, TB, 8], take(128))
    bf_col = at("bf_col", [8, 1], take(4))
    wf_raw = at("wf_raw", [P, KT, 8], take(256))
    ident, ones, half_ones = consts[:, K_ID:K_ID + P], consts[:, K_ONE:K_ONE + P], consts[:, K_HALF:K_HALF + P]
    tmp0 = take(18 * KB)
    T = [tmp0 + 2 * KB * s for s in range(9)]
    sq = [at(f"sq{s}", [P, TOK], T[s]) for s in range(2)]
    sq_first = [at(f"sq_first{s}", [P, TOK], T[s]) for s in range(8)]
    ln_s = at("ln_s", [P, TOK], T[2])
    y0 = at("y0", [P, TOK], T[3])
    y0_half = at("y0_half", [P, TOK], T[4])
    sq_sum = at("sq_sum", [P, TOK], T[5])
    rstd = at("rstd", [P, TOK], T[6])
    hx = [at(f"hx{s}", [P, TOK], T[7 + s]) for s in range(2)]
    off_blocks = take(4 * 9 * P)
    big = top[0]

    v = at("v", [P, TB, AW], big)
    y_lo = at("y_lo", [P, TB, AW], big, F32R)
    y_hi = at("y_hi", [P, AT, TOK], big + 32 * KB, F32R)
    ada_up = [at(f"ada_up{s}", [P, KT, 256], big + 32 * KB + 8 * KB * s) for s in range(4)]
    ws_t = at("ws_t", [P, GROUPS, P], big + 64 * KB)
    b_sp = at("b_sp", [P, GROUPS, P], off_blocks)
    ws_raw = at("ws_raw", [P, GROUPS, P], big + 20 * KB)
    gelu_u = [at(f"gelu_u{s}", [P, TOK], T[2 + s]) for s in range(2)]
    tanh_z = at("tanh_z", [P, TOK], T[4])
    mixed = [at(f"mixed{s}", [P, TOK], T[5 + s]) for s in range(2)]
    v_stage = [at(f"v_stage{s}", [P, TB, P], T[7 + s]) for s in range(2)]
    v_sq = at("v_sq", [P, TB, 256], T[2])

    k_t = at("k_t", [P, NKV, TOK], big)
    v_b = at("v_b", [P, TB, NKV * P], big + 12 * KB)
    hk_hi = at("hk_hi", [P, KT, TOK], big + 24 * KB, F32R)
    hk_lo = at("hk_lo", [P, KT, TOK], big + 40 * KB, F32R)
    yb_hi = at("yb_hi", [P, QH, TOK], big + 24 * KB, F32R)
    yb_lo = at("yb_lo", [P, QH, TOK], big + 40 * KB, F32R)
    q_n = [at("q_n0", [P, 3, TOK], off_ada), at("q_n1", [P, 3, TOK], big + 56 * KB)]
    s_b = at("s_b", [P, 768], big + 62 * KB)
    p_t = at("p_t", [P, 768], big + 65 * KB)
    z_b = [at("z_b0", [P, TOK], big + 68 * KB), at("z_b1", [P, TOK], T[5])]
    z_t = at("z_t", [P, TOK], T[7])
    yb = at("yb", [P, TOK], T[8])
    blocks = at("blocks", [P, 9, P], off_blocks)

    qk = [[at(f"qk{s}_{n}", [P, TOK], big + (4 * s + n) * 2 * KB) for n in range(4)] for s in range(2)]
    v_2 = [at(f"v2{s}", [P, TB, 2 * P], big + (16 + 4 * s) * KB) for s in range(2)]
    m_hi = at("m_hi", [P, KT, TOK], big + 24 * KB, F32R)
    m_lo = at("m_lo", [P, KT, TOK], big + 40 * KB, F32R)
    c_row = [at(f"c_row{n}", [P, TOK], big + (24 + 16 * (n % 2) + n // 2 * 2) * KB) for n in range(8)]
    s_2 = [at(f"s_2{s}", [P, 2, TOK], off) for s, off in enumerate((big + 56 * KB, big + 60 * KB, off_blocks))]
    pt_2 = [at(f"pt_2{s}", [P, TOK], big + 64 * KB + 2 * KB * s) for s in range(2)]
    lam_rows = at("lam_rows", [P, 256], big + 24 * KB)
    lam_prod = at("lam_prod", [P, 128], big + 25 * KB)
    wf_hi = at("wf_hi", [P, KT, P], big + 56 * KB, F32R)
    wf_lo = at("wf_lo", [P, KT, P], big + 60 * KB, F32R)
    gate_abs = at("gate_abs", [8, TOK], T[5])
    gate_exp = at("gate_exp", [8, TOK], T[5])
    gate_ln = at("gate_ln", [8, TOK], T[5])
    gate_min = at("gate_min", [8, TOK], T[7])
    gate_log = at("gate_log", [8, TOK], T[7])
    gate_one = at("gate_one", [8, TOK], big + 68 * KB)
    cum = at("cum", [8, TOK], T[8])
    d_out = at("d_out", [P, TOK], T[7])
    assert big + 70 * KB <= 229344, big

    gu_hi = at("gu_hi", [P, FF1, TOK], big, F32R)
    gu_lo = at("gu_lo", [P, FF1, TOK], big + 32 * KB, F32R)
    tanh_g = [at(f"tanh_g{s}", [P, TOK], T[2 + s]) for s in range(2)]
    gu = [at(f"gu{s}", [P, TOK], T[4 + s]) for s in range(2)]

    G = [nc.alloc_psum_tensor(f"acc{n}", [P, TOK], F32) for n in range(4)]
    T0 = nc.alloc_psum_tensor("turn0", [P, TOK], F32)
    T1 = nc.alloc_psum_tensor("turn1", [P, TOK], F32)
    NB = nc.alloc_psum_tensor("norm", [P, TOK], F32)
    AD = nc.alloc_psum_tensor("ada", [P, TOK], F32)
    FIRST_V = (G[0], T0, G[1], T1)

    def sem(name):
        return nc.alloc_semaphore(name)

    vecs_loaded, consts_loaded, ws_loaded = sem("vecs_loaded"), sem("consts_loaded"), sem("ws_loaded")
    x_loaded = [sem("x_loaded0"), sem("x_loaded1")]
    small_loaded, blocks_loaded, stored = sem("small_loaded"), sem("blocks_loaded"), sem("stored")
    w_loaded = [sem("w_loaded0"), sem("w_loaded1")]
    ada_loaded, ada_up_loaded = sem("ada_loaded"), [sem(f"ada_up_loaded{s}") for s in range(4)]
    hi_done, lo_done = sem("hi_done"), sem("lo_done")
    mm_done, acc_freed, v_gelu_done = sem("mm_done"), sem("acc_freed"), sem("v_gelu_done")
    ada_sum, ada_mm_done, ada_out = sem("ada_sum"), sem("ada_mm_done"), sem("ada_out")
    up_sum, up_summed, up_done, up_out = sem("up_sum"), sem("up_summed"), sem("up_done"), sem("up_out")
    silu_ready, gains_ready, ws_ready = sem("silu_ready"), sem("gains_ready"), sem("ws_ready")
    lam_part, lam_exp, lam_ready = sem("lam_part"), sem("lam_exp"), sem("lam_ready")
    sq_ready, sq_added, qsq_ready = sem("sq_ready"), sem("sq_added"), sem("qsq_ready")
    sum_done, ln_done, y0_done, half_done = sem("sum_done"), sem("ln_done"), sem("y0_done"), sem("half_done")
    newton_done, rstd_done = sem("newton_done"), sem("rstd_done")
    gs_done, hx_done, hhi_done, hlo_done = sem("gs_done"), sem("hx_done"), sem("hhi_done"), sem("hlo_done")
    v_sums_done, v_stat_dve, v_stat_act = sem("v_sums_done"), sem("v_stat_dve"), sem("v_stat_act")
    v_staged, mix_done, mix_freed = sem("v_staged"), sem("mix_done"), sem("mix_freed")
    gelu_done, tanh_done, uz_done = sem("gelu_done"), sem("tanh_done"), sem("uz_done")
    y_done, yhi_done, ylo_done = sem("y_done"), sem("yhi_done"), sem("ylo_done")
    qk_done, s_freed, max_done, exp_done = sem("qk_done"), sem("s_freed"), sem("max_done"), sem("exp_done")
    inv_done, p_ready, turn_done = sem("inv_done"), sem("p_ready"), sem("turn_done")
    pt_act, pt_dve, pv_done = sem("pt_act"), sem("pt_dve"), sem("pv_done")
    z_exp, z_part = sem("z_exp"), sem("z_part")
    head_out, ybhi_done, yblo_done = sem("head_out"), sem("ybhi_done"), sem("yblo_done")
    wf_zeroed, wfhi_done, wflo_done, fg_done = sem("wf_zeroed"), sem("wfhi_done"), sem("wflo_done"), sem("fg_done")
    fgate_act, fgate_dve, c_turned, c_col_ready = sem("fgate_act"), sem("fgate_dve"), sem("c_turned"), sem("c_col_ready")
    c_spread, c_row_ready = sem("c_spread"), sem("c_row_ready")
    qk2_done, s2_freed, bias2_done, max2_done, exp2_done = sem("qk2_done"), sem("s2_freed"), sem("bias2_done"), sem("max2_done"), sem("exp2_done")
    inv2_done, p2_ready, turn2_done, pt2_done, pv2_done = sem("inv2_done"), sem("p2_ready"), sem("turn2_done"), sem("pt2_done"), sem("pv2_done")
    d_done, mhi_done, mlo_done = sem("d_done"), sem("mhi_done"), sem("mlo_done")
    tanhg_done, gz_done, guhi_done, gulo_done = sem("tanhg_done"), sem("gz_done"), sem("guhi_done"), sem("gulo_done")

    N_X0, N_X1, N_K, N_Q, N_X2, N_2 = 0, 1, 2, 8, 32, 33
    N_X3 = N_2 + 20
    SQ1, SQ2, SQ3 = 8, 16, 24

    def norm2(t, mi):
        return N_2 + 4 * t + max(0, t - 2) + mi + (1 if t >= 2 and mi >= 1 else 0)

    def norm_d(a):
        return N_2 + (9, 14, 18, 19)[a]

    UNITS2 = [(kind, qb) for qb in range(TB) for kind in range(3)]

    def ge(eng, semaphore, value):
        if not isinstance(value, int) or value > 0:
            eng.wait_ge(semaphore, value)

    def next_chunk(u, par):
        return (u, 1) if par == 0 else (u + 1, 0)

    def dilated(tile):
        return tile.rearrange("p (i r) -> p r i", r=4)

    def four(tile):
        return tile.rearrange("p (r i) -> p r i", r=4)

    def s_reads(u):
        before = sum(1 if n % 3 < 2 else 2 for n in range(u))
        return before, before % 2

    block = nc.Block()
    with block:

        @block.sync
        def _(sp):
            weights, ada_weights = d["weights"], d["ada"]

            def load(u, par, used=2048):
                src = weights[bass.ds(2 * u + par, 1), :, 0:used].rearrange("a p n -> p (a n)")
                sp.lower_ap_dma(src)
                ge(sp, lo_done, 2 * u + par - 1)
                sp.dma_start(w_raw[par][:, 0:used], src).then_inc(w_loaded[par], 16)

            def ada_load(r):
                src = ada_weights[bass.ds(r + UP, 1), :, :].rearrange("a p n -> p (a n)")
                sp.lower_ap_dma(src)
                ge(sp, ada_sum, 8 * r)
                sp.dma_start(ada_raw[:, :, :].rearrange("p k n -> p (k n)"), src).then_inc(ada_loaded, 16)

            def ada_up_load(s):
                sp.dma_start(ada_up[s % 4][:, :, :].rearrange("p k n -> p (k n)"), ada_weights[s]).then_inc(ada_up_loaded[s % 4], 16)

            sp.dma_start(vecs[:, :], d["vecs"]).then_inc(vecs_loaded, 16)
            for s in range(2):
                ada_up_load(s)
            for half in range(2):
                sp.dma_start(x[:, 4 * half:4 * half + 4, :], d["x"][:, 4 * half:4 * half + 4, :]).then_inc(x_loaded[half], 16)
            for s in range(2, UP):
                if s >= 4:
                    sp.wait_ge((up_sum, up_done)[s % 2], (8, 1)[s % 2] * ((s - 2) // 2))
                ada_up_load(s)
                if s == 5:
                    load(W_V // 2, 0)
            load(W_V // 2, 1)

            for par in range(2):
                load(1, par)
                ada_load(par)
            with sp.Fori(2, W_B // 2 + 1) as u:
                for par in range(2):
                    load(u, par)
                    ada_load(2 * u + par - 2)
            with sp.Fori(W_B // 2 + 1, W_OUTB // 2 + 1) as u:
                for par in range(2):
                    load(u, par)
            sp.wait_ge(pv_done, 4 * QH)
            for r in range(S_OUTB, S_OUT2):
                ada_load(r)
                if r < S_OUTB + 4:
                    load(*divmod(W_OUTB + 2 + r - S_OUTB, 2))
            with sp.Fori(W_Q2 // 2 + 1, W_OUT2 // 2 + 1) as u:
                for par in range(2):
                    load(u, par)
            for r in range(S_OUT2, S_END):
                ada_load(r)
                load(*divmod(W_OUT2 + 2 + r - S_OUT2, 2))
            with sp.Fori(W_GU1 // 2 + 1, W_DN2 // 2) as u:
                for par in range(2):
                    load(u, par)
            for w in range(W_DN2, W_END):
                load(*divmod(w, 2), FF2 * 256)
            for m in range(KT):
                sp.wait_ge(acc_freed, 2 * W_DN2 - 15 + m)
                sp.dma_start(d["out"][:, m, :], x[:, m, :]).then_inc(stored, 16)
            sp.wait_ge(stored, 16 * KT)

        @block.gpsimd
        def _(pool):
            def stage(j, par):
                ge(pool, mix_done, j - 1)
                nc.gpsimd.tensor_tensor(v_stage[par][:, :, :], v[:, :, bass.ds(j * P, P)],
                                        v_stat[:, 5, :].unsqueeze(2).broadcast_to([P, TB, P]), ALU.mult).then_inc(v_staged, 1)

            pool.wait_ge(v_stat_dve, 3)
            stage(0, 0)
            stage(1, 1)
            with pool.Fori(1, AT // 2) as i:
                for par in range(2):
                    stage(2 * i + par, par)

            def sum_squares(k):
                for m in range(1, KT - 1):
                    pool.wait_ge(sq_ready, 8 * k + m + 9)
                    if m > 1:
                        pool.wait_ge(sq_added, 6 * k + m - 1)
                    nc.gpsimd.tensor_tensor(sq_sum[:, :], sq[0][:, :] if m == 1 else sq_sum[:, :], sq[m % 2][:, :], ALU.add)\
                        .then_inc(sq_added, 1)

            sum_squares(0)
            pool.wait_ge(pv_done, 4 * QH)
            nc.gpsimd.memset(wf_hi[:, :, :].bitcast(F32), 0.0).then_inc(wf_zeroed, 1)
            nc.gpsimd.memset(wf_lo[:, :, :].bitcast(F32), 0.0).then_inc(wf_zeroed, 1)
            sum_squares(1)
            sum_squares(2)

        @block.scalar
        def _(act):
            eps_col = consts[:, K_EPS:K_EPS + 1]

            def to_hi(u, par, used=2048):
                act.wait_ge(w_loaded[par], 16 * u + 16)
                ge(act, mm_done, 4 * u + 2 * par - 2)
                nc.scalar.activation(w_hi[par][:, 0:used], w_raw[par][:, 0:used], ACT.Copy).then_inc(hi_done, 1)

            def rstd_start(k, total, count):
                act.wait_ge(sum_done, k + 1)
                nc.scalar.activation(ln_s[:, :], total, ACT.Ln, scale=1.0 / count, bias=eps_col).then_inc(ln_done, 1)
                act.wait_ge(ln_done, k + 1)
                ge(act, rstd_done, k)
                nc.scalar.activation(y0[:, :], ln_s[:, :], ACT.Exp, scale=-0.5).then_inc(y0_done, 1)
                act.wait_ge(y0_done, k + 1)
                nc.scalar.activation(y0_half[:, :], y0[:, :], ACT.Square, scale=math.sqrt(0.5 / count)).then_inc(half_done, 1)

            def h_round(e, shift, dilate, kts=range(KT), h=h_hi):
                for kt in kts:
                    act.wait_ge(hx_done, 8 * e + kt + 1)
                    src, dst = hx[kt % 2][:, :], h[:, kt, :]
                    nc.scalar.activation(four(dst) if dilate else dst, dilated(src) if dilate else src, ACT.Identity,
                                         bias=mods[:, shift + kt:shift + kt + 1]).then_inc(hhi_done, 1)

            def square_x(k, m, seen):
                act.wait_ge(acc_freed, seen)
                if m >= 2:
                    act.wait_ge(sq_added, 6 * k + max(1, m - 2))
                nc.scalar.activation(sq[m % 2][:, :], x[:, m, :], ACT.Square).then_inc(sq_ready, 1)

            act.dma_start(consts[:, :], d["tiles"]).then_inc(consts_loaded, 16)
            act.dma_start(ws_raw[:, :, :], d["spatial"]).then_inc(ws_loaded, 16)
            act.dma_start(b_sp[:, :, :], d["a_b_spatial"][0].rearrange("g t -> (g t)").partition_broadcast(P)
                          .rearrange("p (g t) -> p g t", g=GROUPS)).then_inc(small_loaded, 16)
            act.dma_start(lam_rows[:, :], d["diff_lam_2"][0].rearrange("a b -> (a b)").partition_broadcast(P)).then_inc(small_loaded, 16)
            act.dma_start(bf_col[:, :], d["b_f_2"].rearrange("a h -> h a")).then_inc(small_loaded, 16)
            act.dma_start(wf_raw[:, :, :], d["forget"]).then_inc(small_loaded, 16)

            act.wait_ge(vecs_loaded, 16)
            nc.scalar.activation(silu_c[:, :], vecs[:, C_1:C_1 + 16], ACT.Silu).then_inc(silu_ready, 1)
            act.preload_act_table_set("natural_log_exp_and_others")
            for kt in range(KT):
                act.wait_ge(x_loaded[kt // 4], 16)
                nc.scalar.activation(sq_first[kt][:, :], x[:, kt, :], ACT.Square).then_inc(sq_ready, 1)
            rstd_start(N_X0, NB[:, :], DM)
            act.wait_ge(lam_part, 2)
            nc.scalar.activation(lam_two[:, :], lam_two[:, :], ACT.Exp).then_inc(lam_exp, 1)
            to_hi(0, 0)
            h_round(0, SHIFT_A, False)

            def v_pair(u):
                n = 2 * u - W_V
                for par in range(2):
                    to_hi(*next_chunk(u, par))
                    for hb in range(2):
                        act.wait_ge(mm_done, 4 * u + 2 * par + hb + 1)
                        if isinstance(u, int) and par == 0:
                            nc.scalar.activation(v[:, 2 * hb, 0:256], FIRST_V[2 * hb][:, 0:256], ACT.Gelu_apprx_tanh)
                            nc.scalar.activation(v[:, 2 * hb + 1, 0:256], FIRST_V[2 * hb + 1][:, 0:256], ACT.Gelu_apprx_tanh)\
                                .then_inc(v_gelu_done, 1)
                            continue
                        nc.scalar.activation(v[:, 2 * hb:2 * hb + 2, bass.ds(256 * n + 256 * par, 256)],
                                             G[2 * par + hb][:, :].rearrange("p (t n) -> p t n", t=2),
                                             ACT.Gelu_apprx_tanh).then_inc(v_gelu_done, 1)

            v_pair(0)
            with act.Fori(1, W_UZ // 2) as u:
                v_pair(u)
            act.preload_act_table_set("natural_log_exp_and_others")
            act.wait_ge(v_stat_dve, 1)
            nc.scalar.activation(v_stat[:, 1, :], v_stat[:, 0, :], ACT.Ln, scale=1.0 / AW, bias=eps_col).then_inc(v_stat_act, 1)
            act.wait_ge(v_stat_act, 1)
            nc.scalar.activation(v_stat[:, 2, :], v_stat[:, 1, :], ACT.Exp, scale=-0.5).then_inc(v_stat_act, 1)
            act.wait_ge(v_stat_act, 2)
            nc.scalar.activation(v_stat[:, 3, :], v_stat[:, 2, :], ACT.Square, scale=math.sqrt(0.5 / AW)).then_inc(v_stat_act, 1)

            def uz_pair(u):
                j = 2 * u - W_UZ
                for par in range(2):
                    to_hi(*next_chunk(u, par))
                    act.wait_ge(mm_done, 4 * u + 2 * par + 1)
                    ge(act, uz_done, j + par - 1)
                    nc.scalar.activation(gelu_u[par][:, :], G[2 * par][:, :], ACT.Gelu_apprx_tanh).then_inc(gelu_done, 1)
                    act.wait_ge(mm_done, 4 * u + 2 * par + 2)
                    ge(act, uz_done, j + par)
                    nc.scalar.activation(tanh_z[:, :], G[2 * par + 1][:, :], ACT.Tanh, scale=0.5).then_inc(tanh_done, 1)
                    act.wait_ge(y_done, j + par + 1)
                    nc.scalar.activation(y_hi[:, j + par, :], mixed[par][:, :], ACT.Copy).then_inc(yhi_done, 1)

            uz_pair(W_UZ // 2)
            with act.Fori(W_UZ // 2 + 1, W_OUTA // 2) as u:
                uz_pair(u)

            act.preload_act_table_set("natural_log_exp_and_others")
            act.wait_ge(mix_freed, AT)
            act.dma_start(blocks[:, :, :], d["blocks"].rearrange("p (b n) -> p b n", n=P)).then_inc(blocks_loaded, 16)
            for m in range(KT):
                to_hi(*divmod(W_OUTA + m + 1, 2))
                square_x(0, m, 2 * (W_OUTA + m) - 14)
            rstd_start(N_X1, NB[:, :], DM)
            h_round(1, SHIFT_KV, True, h=hk_hi)

            for c in range(NKV // 2):
                u = W_KV // 2 + c
                for par in range(2):
                    to_hi(*next_chunk(u, par))
                    if c < 2:
                        h_round(2, SHIFT_B, True, (4 * c + 2 * par, 4 * c + 2 * par + 1))
                    if par == 0:
                        for half in range(2):
                            act.wait_ge(mm_done, 4 * u + half + 1)
                            nc.scalar.activation(sq[half][:, :], G[half][:, :], ACT.Square).then_inc(qsq_ready, 1)
                    rstd_start(N_K + 2 * c + par, NB[:, :], P)

            def head(n, p, mho, attend, project):
                m = n - 1
                w0 = 2 * n + W_B
                k = 3 * n + N_Q
                u0 = n + W_B // 2

                def z_start():
                    act.wait_ge(mm_done, 2 * w0)
                    act.wait_ge(acc_freed, 2 * w0 - 17)
                    nc.scalar.activation(z_t[:, :], G[1][:, :], ACT.Exp, scale=-1.0).then_inc(z_exp, 1)

                def exps(r):
                    act.wait_ge(max_done, 4 * m + r + 1)
                    nc.scalar.activation(s_b[:, :], s_b[:, :], ACT.Exp, bias=row_stat[:, 0, r:r + 1],
                                         accum_out=row_stat[:, 1, r:r + 1]).then_inc(exp_done, 1)

                def turn_copy(r):
                    act.wait_ge(turn_done, 4 * m + r + 1)
                    nc.scalar.activation(p_t[:, 0:TOK], T0[:, :], ACT.Copy).then_inc(pt_act, 1)

                def squares(mi):
                    act.wait_ge(mm_done, 2 * w0 + mi + 1)
                    act.wait_ge(sum_done, k + mi - 1)
                    nc.scalar.activation(sq[(mi + p) % 2][:, :], G[mi % 2][:, :], ACT.Square).then_inc(qsq_ready, 1)

                if attend:
                    z_start()
                    exps(0)
                if project:
                    to_hi(u0, 1)
                    squares(0)
                if attend:
                    turn_copy(0)
                    if mho is not None:
                        out_round(n, p, mho)
                if project:
                    rstd_start(k, NB[:, :], P)
                if attend:
                    exps(1)
                if project:
                    squares(1)
                if attend:
                    turn_copy(1)
                if project:
                    rstd_start(k + 1, NB[:, :], P)
                if attend:
                    exps(2)
                if project:
                    to_hi(u0 + 1, 0)
                    squares(2)
                if attend:
                    turn_copy(2)
                if project:
                    rstd_start(k + 2, NB[:, :], P)
                if attend:
                    exps(3)
                    turn_copy(3)

            def out_round(n, p, mho):
                act.wait_ge(head_out, n - 1)
                nc.scalar.activation(yb_hi[:, mho + 4 * p, :], yb[:, :], ACT.Copy).then_inc(ybhi_done, 1)

            head(0, 0, None, False, True)
            head(1, 1, None, True, True)
            head(2, 0, 0, True, True)
            with act.Fori(2, QH // 2) as i:
                head(2 * i - 1, 1, i - 2, True, True)
                head(2 * i, 0, i - 1, True, True)
            head(QH - 1, 1, QH // 2 - 2, True, True)
            head(QH, 0, QH // 2 - 1, True, False)
            out_round(QH + 1, 1, QH // 2 - 1)

            for c in range(4):
                to_hi(*divmod(W_OUTB + c + 1, 2))
                for m in (2 * c, 2 * c + 1):
                    square_x(1, m, 2 * W_OUTB - 15 + m)
            rstd_start(N_X2, NB[:, :], DM)
            act.wait_ge(wf_zeroed, 2)
            act.wait_ge(small_loaded, 64)
            nc.scalar.activation(wf_hi[:, :, 0:8], wf_raw[:, :, :], ACT.Copy).then_inc(wfhi_done, 1)
            h_round(3, SHIFT_1, False)
            to_hi(*divmod(W_Q2 + 1, 2))

            act.wait_ge(fg_done, 1)
            nc.scalar.activation(gate_abs[:, :], T0[0:8, :], ACT.Abs, bias=bf_col[:, :]).then_inc(fgate_act, 1)
            act.wait_ge(fgate_act, 1)
            nc.scalar.activation(gate_exp[:, :], gate_abs[:, :], ACT.Exp, scale=-1.0).then_inc(fgate_act, 1)
            act.preload_act_table_set("natural_log")
            act.wait_ge(fgate_act, 2)
            nc.scalar.activation(gate_ln[:, :], gate_exp[:, :], ACT.Ln, bias=ones[0:8, 0:1]).then_inc(fgate_act, 1)
            act.preload_act_table_set("natural_log_exp_and_others")

            def turn2_copy(n):
                act.wait_ge(turn2_done, n + 1)
                width = (UNITS2[n % 12][1] + 1) * P
                nc.scalar.activation(pt_2[n % 2][:, 0:width], T0[:, 0:width], ACT.Copy).then_inc(pt2_done, 1)

            def fox_round(a):
                act.wait_ge(pv2_done, 12 * a + 12)
                nc.scalar.activation(m_hi[:, a, :], AD[:, :], ACT.Copy).then_inc(mhi_done, 1)

            def diff_square(a):
                k = norm_d(a)
                act.wait_ge(sum_done, k - 1)
                nc.scalar.activation(sq[k % 2][:, :], T1[:, :], ACT.Square).then_inc(qsq_ready, 1)

            def diff_round(a):
                act.wait_ge(d_done, a + 1)
                nc.scalar.activation(m_hi[:, 4 + a, :], d_out[:, :], ACT.Copy).then_inc(mhi_done, 1)

            def spread_copy(n):
                act.wait_ge(c_spread, n + 1)
                nc.scalar.activation(c_row[n][:, :], (T0, T1)[n % 2][:, :], ACT.Copy).then_inc(c_row_ready, 1)

            for t in range(5):
                w0 = W_Q2 + 3 * t
                a = t - 1
                attend, project = t >= 1, t < 4
                for u in range(12):
                    n = 12 * a + u
                    if project and u in (0, 4, 8) and (t, u) != (0, 0):
                        to_hi(*divmod(w0 + u // 4 + 1, 2))
                    if attend and n >= 2:
                        turn2_copy(n - 2)
                    if a >= 1 and u == 2:
                        fox_round(a - 1)
                        diff_square(a - 1)
                    if attend:
                        kind, qb = UNITS2[u]
                        width = (qb + 1) * P
                        act.wait_ge(max2_done, n + 1)
                        for e in range(2 if kind == 2 else 1):
                            ex = nc.scalar.activation(s_2[n % 3][:, e, 0:width], s_2[n % 3][:, e, 0:width], ACT.Exp,
                                                      bias=stat2[:, 0, n % 2, e:e + 1], accum_out=stat2[:, 1, n % 2, e:e + 1])
                        ex.then_inc(exp2_done, 1)
                    if project and u in (1, 3, 5, 7):
                        k = norm2(t, u // 2)
                        act.wait_ge(mm_done, 2 * w0 + u // 2 + 1)
                        act.wait_ge(sum_done, k - 1)
                        nc.scalar.activation(sq[k % 2][:, :], G[u // 2 % 2][:, :], ACT.Square).then_inc(qsq_ready, 1)
                    if project and u in (2, 4, 6, 8):
                        rstd_start(norm2(t, u // 2 - 1), NB[:, :], 64)
                    if a >= 1 and u == 3:
                        rstd_start(norm_d(a - 1), NB[:, :], P)
                    if a >= 1 and u == 4:
                        diff_round(a - 1)
                    if t == 0 and u >= 6:
                        spread_copy(u - 6)
                if t == 0:
                    spread_copy(6)
                    spread_copy(7)
            turn2_copy(46)
            turn2_copy(47)
            fox_round(3)
            diff_square(3)
            rstd_start(norm_d(3), NB[:, :], P)
            diff_round(3)

            for c in range(4):
                to_hi(*divmod(W_OUT2 + c + 1, 2))
                for m in (2 * c, 2 * c + 1):
                    square_x(2, m, 2 * W_OUT2 - 15 + m)
            rstd_start(N_X3, NB[:, :], DM)
            h_round(4, SHIFT_2, False)

            def gate_up(u, f, par, first):
                to_hi(*next_chunk(u, par))
                act.wait_ge(mm_done, 4 * u + 2 * par + 1)
                ge(act, gulo_done, f + first - 1)
                nc.scalar.activation(tanh_g[par][:, :], G[2 * par][:, :], ACT.Tanh, scale=0.5).then_inc(tanhg_done, 1)
                act.wait_ge(acc_freed, 4 * u + 2 * par - 14)
                nc.scalar.activation(gu_hi[:, f, :], gu[par][:, :], ACT.Copy).then_inc(guhi_done, 1)

            for par in range(2):
                gate_up(W_GU1 // 2, par, par, 0)
            with act.Fori(W_GU1 // 2 + 1, W_DN1 // 2) as u:
                for par in range(2):
                    gate_up(u, 2 * (u - W_GU1 // 2) + par, par, 0)
            with act.Fori(W_DN1 // 2, W_GU2 // 2) as u:
                for par in range(2):
                    to_hi(*next_chunk(u, par))
            with act.Fori(W_GU2 // 2, W_DN2 // 2) as u:
                for par in range(2):
                    gate_up(u, 2 * (u - W_GU2 // 2) + par, par, FF1)

            for w in range(W_DN2 + 1, W_END):
                to_hi(*divmod(w, 2), FF2 * 256)

        @block.vector
        def _(dve):
            def f32(tile):
                return tile.bitcast(F32)

            def stt(out, in0, scalar, in1, op0, op1, **more):
                return nc.vector.scalar_tensor_tensor(out, in0, scalar, in1, op0, op1, **more)

            def to_lo(u, par, used=2048):
                dve.wait_ge(hi_done, 2 * u + par + 1)
                nc.vector.tensor_tensor(w_lo[par][:, 0:used], w_raw[par][:, 0:used], f32(w_hi[par][:, 0:used]), ALU.subtract)\
                    .then_inc(lo_done, 1)

            def ada_step(done, first, raw, cond):
                nc.vector.tensor_scalar(ada_acc[:, :], raw[:, 0, :], silu_c[:, cond:cond + 1], None, ALU.mult).then_inc(done, 1)
                for kt in range(1, KT):
                    dve.wait_ge(done, first + kt)
                    stt(ada_acc[:, :], raw[:, kt, :], silu_c[:, cond + kt:cond + kt + 1], ada_acc[:, :], ALU.mult, ALU.add)\
                        .then_inc(done, 1)

            def ada_end(r):
                dve.wait_ge(ada_mm_done, r + 1)
                nc.vector.tensor_tensor(mods[:, bass.ds(2 * (r + UP), 2)], AD[:, 0:2], mod_bias[:, bass.ds(2 * (r + UP), 2)], ALU.add)\
                    .then_inc(ada_out, 1)

            def ada(r, cond):
                if not (isinstance(r, int) and r == 0):
                    ada_end(r - 1)
                dve.wait_ge(ada_loaded, 16 * (r + 1))
                ada_step(ada_sum, 8 * r, ada_raw, cond)

            def gain(e, scale, g, have):
                if have > 0:
                    dve.wait_ge(ada_out, have)
                ge(dve, hx_done, 8 * e)
                stt(gscale[:, :], mods[:, scale:scale + 8], 1.0, vecs[:, g:g + 8], ALU.add, ALU.mult).then_inc(gs_done, 1)
                dve.wait_ge(gs_done, e + 1)

            def rstd_end(k, total, count, rstd=rstd):
                dve.wait_ge(half_done, k + 1)
                stt(y0_half[:, :], total, count * EPS, y0_half[:, :], ALU.add, ALU.mult).then_inc(newton_done, 1)
                dve.wait_ge(newton_done, k + 1)
                stt(rstd[:, :], y0_half[:, :], 1.5, y0[:, :], ALU.subtract, ALU.mult, reverse0=True).then_inc(rstd_done, 1)
                dve.wait_ge(rstd_done, k + 1)

            def h_scale(e, kt):
                ge(dve, hlo_done, 8 * e + kt - 1)
                stt(hx[kt % 2][:, :], x[:, kt, :], gscale[:, kt:kt + 1], x_rstd[:, :], ALU.mult, ALU.mult).then_inc(hx_done, 1)

            def h_rest(e, kt, shift, dilate, h=(h_hi, h_lo)):
                dve.wait_ge(hhi_done, 8 * e + kt + 1)
                src, hi, lo = hx[kt % 2][:, :], f32(h[0][:, kt, :]), h[1][:, kt, :]
                if dilate:
                    src, hi, lo = dilated(src), four(hi), four(lo)
                stt(lo, src, mods[:, shift + kt:shift + kt + 1], hi, ALU.add, ALU.subtract).then_inc(hlo_done, 1)

            def h_split(e, shift, dilate, h=(h_hi, h_lo)):
                h_scale(e, 0)
                for kt in range(KT):
                    if kt + 1 < KT:
                        h_scale(e, kt + 1)
                    h_rest(e, kt, shift, dilate, h)

            def update_x(m, acc, gate, mm, n, dilate=False):
                dve.wait_ge(mm_done, mm)
                xm = dilated(x[:, m, :]) if dilate else x[:, m, :]
                stt(xm, four(acc) if dilate else acc, mods[:, bass.ds(m + gate, 1)], xm, ALU.mult, ALU.add).then_inc(acc_freed, n)

            dve.wait_ge(vecs_loaded, 16)
            dve.wait_ge(silu_ready, 1)
            for s in range(0, UP, 2):
                dve.wait_ge(ada_up_loaded[s % 4], 16 * (s // 4 + 1))
                ge(dve, up_summed, s // 2)
                ada_step(up_sum, 4 * s, ada_up[s % 4], 0)
                if s == 0:
                    nc.vector.tensor_scalar(gains[:, 0:1], vecs[:, G_QB:G_QB + 1], P ** -0.5, None, ALU.mult)
                    nc.vector.tensor_scalar(gains[:, 1:2], vecs[:, G_FQ:G_FQ + 1], 0.125, None, ALU.mult)
                    nc.vector.tensor_copy(gains[:, 2:3], vecs[:, G_FK:G_FK + 1])
                    nc.vector.tensor_scalar(gains[:, 3:4], vecs[:, G_DQ:G_DQ + 1], 0.125, None, ALU.mult)
                    nc.vector.tensor_copy(gains[:, 4:5], vecs[:, G_DK:G_DK + 1])
                    nc.vector.tensor_scalar(gains[:, 5:6], vecs[:, G_DN:G_DN + 1], 1.0 - LAM_INIT, None, ALU.mult).then_inc(gains_ready, 1)
                if s == 2:
                    dve.wait_ge(ws_loaded, 16)
                    dve.wait_ge(consts_loaded, 16)
                    tri = consts[:, K_TRI:K_TRI + P].unsqueeze(1).broadcast_to([P, GROUPS, P])
                    nc.vector.tensor_tensor(ws_t[:, :, :], ws_raw[:, :, :], tri, ALU.mult).then_inc(ws_ready, 1)
                    dve.wait_ge(small_loaded, 64)
                    for n in range(2):
                        stt(lam_prod[:, 64 * n:64 * n + 64], lam_rows[:, 128 * n:128 * n + 64], 1.0,
                            lam_rows[:, 128 * n + 64:128 * n + 128], ALU.mult, ALU.mult, accum_out=lam_two[:, n:n + 1]).then_inc(lam_part, 1)
            rstd_end(N_X0, NB[:, :], DM, x_rstd)
            dve.wait_ge(lam_exp, 1)
            stt(neg_lam[:, :], lam_two[:, 1:2], -LAM_INIT, lam_two[:, 0:1], ALU.add, ALU.subtract).then_inc(lam_ready, 1)
            dve.wait_ge(up_summed, UP // 2)
            dve.wait_ge(up_done, UP // 2)
            nc.vector.tensor_tensor(mods[:, 0:2 * UP], AD[:, 0:2 * UP], mod_bias[:, 0:2 * UP], ALU.add).then_inc(up_out, 1)
            dve.wait_ge(up_out, 1)
            gain(0, SCALE_A, G_A, 0)
            to_lo(0, 0)
            h_split(0, SHIFT_A, False)

            def v_pair(u):
                n = 2 * u - W_V
                for par in range(2):
                    to_lo(*next_chunk(u, par))
                    ada(n + par, 0)
                    dve.wait_ge(v_gelu_done, 4 * u + 2 * par + 2)
                    ge(dve, v_sums_done, n + par)
                    for t in range(TB):
                        vt = v[:, t, bass.ds(256 * n + 256 * par, 256)]
                        last = stt(v_sq[:, t, :], vt, 1.0, vt, ALU.mult, ALU.mult, accum_out=v_sums[:, t, bass.ds(n + par, 1)])
                    last.then_inc(v_sums_done, 1)

            v_pair(0)
            with dve.Fori(1, W_UZ // 2) as u:
                v_pair(u)
            dve.wait_ge(v_sums_done, GROUPS)
            nc.vector.tensor_reduce(v_stat[:, 0, :], v_sums[:, :, :], AX, ALU.add).then_inc(v_stat_dve, 1)
            dve.wait_ge(v_stat_act, 3)
            dve.wait_ge(v_stat_dve, 1)
            stt(v_stat[:, 4, :], v_stat[:, 0, :], AW * EPS, v_stat[:, 3, :], ALU.add, ALU.mult).then_inc(v_stat_dve, 1)
            dve.wait_ge(v_stat_dve, 2)
            stt(v_stat[:, 5, :], v_stat[:, 4, :], 1.5, v_stat[:, 2, :], ALU.subtract, ALU.mult, reverse0=True).then_inc(v_stat_dve, 1)

            def uz_pair(u):
                jj = 2 * u - W_UZ
                g = u - W_UZ // 2
                for par in range(2):
                    j = jj + par
                    to_lo(*next_chunk(u, par))
                    ada(j + W_UZ, 0)
                    dve.wait_ge(gelu_done, j + 1)
                    dve.wait_ge(tanh_done, j + 1)
                    stt(tanh_z[:, :], tanh_z[:, :], 1.0, G[2 * par + 1][:, :], ALU.add, ALU.mult).then_inc(acc_freed, 2)
                    dve.wait_ge(acc_freed, 2 * j + 2)
                    stt(gelu_u[par][:, :], tanh_z[:, :], 0.5, gelu_u[par][:, :], ALU.mult, ALU.mult).then_inc(uz_done, 1)
                    dve.wait_ge(mix_done, j + 1)
                    mix = mixed[par][:, :].rearrange("p (c t) -> p c t", c=TB)
                    stt(mix, (T0, T1)[par][:, :].rearrange("p (c t) -> p c t", c=TB), vecs[:, bass.ds(j + G_SGU, 1)],
                        b_sp[:, bass.ds(g, 1), :].broadcast_to([P, TB, P]), ALU.mult, ALU.add).then_inc(mix_freed, 1)
                    dve.wait_ge(mix_freed, j + 1)
                    dve.wait_ge(uz_done, j + 1)
                    nc.vector.tensor_tensor(mixed[par][:, :], mixed[par][:, :], gelu_u[par][:, :], ALU.mult).then_inc(y_done, 1)
                    dve.wait_ge(yhi_done, j + 1)
                    nc.vector.tensor_tensor(y_lo[:, :, bass.ds(j * P, P)], mix,
                                            f32(y_hi[:, j, :]).rearrange("p (c t) -> p c t", c=TB),
                                            ALU.subtract).then_inc(ylo_done, 1)

            dve.wait_ge(small_loaded, 64)
            uz_pair(W_UZ // 2)
            with dve.Fori(W_UZ // 2 + 1, W_OUTA // 2) as u:
                uz_pair(u)

            with dve.Fori(W_OUTA // 2, W_KV // 2) as u:
                for par in range(2):
                    m = 2 * u - W_OUTA + par
                    to_lo(*next_chunk(u, par))
                    ada(m + W_OUTA, 8)
                    dve.wait_ge(ada_out, m + W_OUTA)
                    update_x(m, G[2 * par][:, :], GATE_A, 4 * u + 2 * par + 2, 2)
            gain(1, SCALE_KV, G_KV, 8)
            rstd_end(N_X1, NB[:, :], DM, x_rstd)
            h_split(1, SHIFT_KV, True, (hk_hi, hk_lo))

            gain(2, SCALE_B, G_B, 20)
            for c in range(NKV // 2):
                u = W_KV // 2 + c
                for par in range(2):
                    tiles = (4 * c + 2 * par, 4 * c + 2 * par + 1) if c < 2 else ()
                    to_lo(*next_chunk(u, par))
                    for kt in tiles:
                        h_scale(2, kt)
                    ada(2 * u + par, 8)
                    rstd_end(N_K + 2 * c + par, NB[:, :], P)
                    stt(k_t[:, 2 * c + par, :], G[par][:, :], vecs[:, G_K:G_K + 1], rstd[:, :], ALU.mult, ALU.mult).then_inc(acc_freed, 1)
                    for kt in tiles:
                        h_rest(2, kt, SHIFT_B, True)
                for half in range(2):
                    dve.wait_ge(mm_done, 4 * u + 3 + half)
                    nc.vector.tensor_copy(v_b[:, 2 * half:2 * half + 2, 256 * c:256 * c + 256],
                                          G[2 + half][:, :].rearrange("p (t n) -> p t n", t=2)).then_inc(acc_freed, 1)

            dve.wait_ge(gains_ready, 1)
            dve.wait_ge(blocks_loaded, 16)

            def head_end(n, p, mho):
                dve.wait_ge(pv_done, 4 * (n - 1))
                nc.vector.tensor_tensor(yb[:, :], z_b[p][:, :], AD[:, :], ALU.mult).then_inc(head_out, 1)
                dve.wait_ge(ybhi_done, n - 1)
                nc.vector.tensor_tensor(yb_lo[:, mho + 4 * p, :], yb[:, :], f32(yb_hi[:, mho + 4 * p, :]), ALU.subtract).then_inc(yblo_done, 1)

            def head(n, p, mh, mho, attend, project):
                m, q = n - 1, 1 - p
                u0 = n + W_B // 2
                w0 = 2 * n + W_B
                k = 3 * n + N_Q

                def slope(g):
                    return consts[:, bass.ds(mh + (K_SLOPE + 8 * g + 4 * q), 1)]

                def z_gate():
                    dve.wait_ge(z_exp, n)
                    nc.vector.tensor_scalar(z_t[:, :], z_t[:, :], FAR, 1.0, ALU.min, ALU.add).then_inc(z_part, 1)
                    dve.wait_ge(z_part, 2 * n - 1)
                    nc.vector.reciprocal(z_t[:, :], z_t[:, :]).then_inc(z_part, 1)
                    dve.wait_ge(z_part, 2 * n)
                    nc.vector.tensor_tensor(z_b[q][:, :], z_t[:, :], G[1][:, :], ALU.mult).then_inc(acc_freed, 1)

                def logits(r):
                    dve.wait_ge(qk_done, 4 * m + r + 1)
                    stt(s_b[:, 0:TOK], blocks[:, 3 - r:7 - r, :].rearrange("p b n -> p (b n)"), slope(0), G[2][:, :], ALU.mult, ALU.add)
                    for g in (1, 2):
                        last = stt(s_b[:, TOK + P * (g - 1):TOK + P * g], blocks[:, 6 + g, :], slope(g), G[3][:, P * (g - 1):P * g],
                                   ALU.mult, ALU.add)
                    last.then_inc(s_freed, 1)
                    dve.wait_ge(s_freed, 4 * m + r + 1)
                    nc.vector.tensor_reduce(row_stat[:, 0, r:r + 1], s_b[:, :], AX, ALU.max, negate=True).then_inc(max_done, 1)

                def weights(r):
                    dve.wait_ge(exp_done, 4 * m + r + 1)
                    nc.vector.reciprocal(row_stat[:, 2, r:r + 1], row_stat[:, 1, r:r + 1]).then_inc(inv_done, 1)
                    dve.wait_ge(inv_done, 4 * m + r + 1)
                    nc.vector.tensor_scalar(s_b[:, :], s_b[:, :], row_stat[:, 2, r:r + 1], None, ALU.mult).then_inc(p_ready, 1)

                def turn_copy(r):
                    dve.wait_ge(turn_done, 4 * m + r + 1)
                    nc.vector.tensor_copy(p_t[:, TOK:768], T1[:, 0:256]).then_inc(pt_dve, 1)

                def q_norm(mi):
                    rstd_end(k + mi, NB[:, :], P)
                    stt(q_n[p][:, mi, :], G[mi % 2][:, :], gains[:, 0:1], rstd[:, :], ALU.mult, ALU.mult).then_inc(acc_freed, 1)

                if attend:
                    logits(0)
                    z_gate()
                    weights(0)
                if project:
                    to_lo(u0, 1)
                if attend and mho is not None:
                    head_end(n, p, mho)
                for r in range(4):
                    if attend:
                        turn_copy(r)
                        if r < 3:
                            logits(r + 1)
                    if project and r < 3:
                        q_norm(r)
                    if attend and r < 3:
                        weights(r + 1)
                    if project and r == 2:
                        to_lo(u0 + 1, 0)

            head(0, 0, None, None, False, True)
            head(1, 1, 0, None, True, True)
            head(2, 0, 0, 0, True, True)
            with dve.Fori(2, QH // 2) as i:
                head(2 * i - 1, 1, i - 1, i - 2, True, True)
                head(2 * i, 0, i - 1, i - 1, True, True)
            head(QH - 1, 1, QH // 2 - 1, QH // 2 - 2, True, True)
            head(QH, 0, QH // 2 - 1, QH // 2 - 1, True, False)
            head_end(QH + 1, 1, QH // 2 - 1)

            for c in range(4):
                w = W_OUTB + c
                to_lo(*divmod(w + 1, 2))
                ada(S_OUTB + c + (c + 1) // 2, 8)
                for half in range(2):
                    if half == 1 and c % 2 == 0:
                        ada(S_OUTB + c + c // 2 + 1, 8)
                    update_x(2 * c + half, G[2 * (w % 2) + half][:, :], GATE_B, 2 * w + half + 1, 1, True)
            dve.wait_ge(wfhi_done, 1)
            nc.vector.tensor_tensor(wf_lo[:, :, 0:8], wf_raw[:, :, :], f32(wf_hi[:, :, 0:8]), ALU.subtract).then_inc(wflo_done, 1)
            gain(3, SCALE_1, G_LN1, 32)
            rstd_end(N_X2, NB[:, :], DM, x_rstd)
            h_split(3, SHIFT_1, False)
            to_lo(*divmod(W_Q2 + 1, 2))

            nc.vector.memset(gate_one[:, :], 1.0).then_inc(fgate_dve, 1)
            dve.wait_ge(fgate_act, 1)
            nc.vector.tensor_scalar(gate_min[:, :], T0[0:8, :], bf_col[:, :], 0.0, ALU.add, ALU.min).then_inc(fgate_dve, 1)
            dve.wait_ge(fgate_act, 3)
            dve.wait_ge(fgate_dve, 2)
            nc.vector.tensor_tensor(gate_log[:, :], gate_min[:, :], gate_ln[:, :], ALU.subtract).then_inc(fgate_dve, 1)
            dve.wait_ge(fgate_dve, 3)
            nc.vector.tensor_tensor_scan(cum[:, :], gate_one[:, :], gate_log[:, :], 0.0, ALU.mult, ALU.add).then_inc(fgate_dve, 1)

            def fox_rest(a):
                dve.wait_ge(mhi_done, 2 * a + 1)
                nc.vector.tensor_tensor(m_lo[:, a, :], AD[:, :], f32(m_hi[:, a, :]), ALU.subtract).then_inc(mlo_done, 1)

            def diff_norm(a):
                rstd_end(norm_d(a), NB[:, :], P)
                stt(d_out[:, :], T1[:, :], gains[:, 5:6], rstd[:, :], ALU.mult, ALU.mult).then_inc(d_done, 1)

            def diff_rest(a):
                dve.wait_ge(mhi_done, 2 * a + 2)
                nc.vector.tensor_tensor(m_lo[:, 4 + a, :], d_out[:, :], f32(m_hi[:, 4 + a, :]), ALU.subtract).then_inc(mlo_done, 1)

            def logits2(n):
                a, u = divmod(n, 12)
                kind, qb = UNITS2[u]
                width = (qb + 1) * P
                before, first = s_reads(u)
                sets = 2 if kind == 2 else 1
                dve.wait_ge(qk2_done, n + 1)
                for e in range(sets):
                    s, score = s_2[n % 3][:, e, 0:width], G[2 + (first + e) % 2][:, 0:width]
                    if kind == 2:
                        biased = stt(s, consts[:, K_DIST + TOK - width:K_DIST + TOK], -SLOPES_D[a], score, ALU.mult, ALU.add)
                    else:
                        biased = stt(s, score, c_col[:, qb, 2 * a + kind:2 * a + kind + 1], c_row[2 * a + kind][:, 0:width],
                                     ALU.add, ALU.subtract)
                    biased.then_inc(s2_freed, 1)
                dve.wait_ge(s2_freed, 16 * a + before + sets)
                if kind < 2:
                    s = s_2[n % 3][:, 0, width - P:width]
                    nc.vector.tensor_tensor(s, s, consts[:, K_MASK:K_MASK + P], ALU.add).then_inc(bias2_done, 1)
                    dve.wait_ge(bias2_done, 8 * a + sum(1 for e in UNITS2[:u + 1] if e[0] < 2))
                nc.vector.tensor_reduce(stat2[:, 0, n % 2, 0:sets], s_2[n % 3][:, 0:sets, 0:width], AX, ALU.max, negate=True)\
                    .then_inc(max2_done, 1)

            def weights2(n):
                a, u = divmod(n, 12)
                kind, qb = UNITS2[u]
                width = (qb + 1) * P
                sets = 2 if kind == 2 else 1
                dve.wait_ge(exp2_done, n + 1)
                i0 = 20 * a + u + sum(2 for e in UNITS2[:u] if e[0] == 2)
                nc.vector.reciprocal(stat2[:, 2, n % 2, 0:sets], stat2[:, 1, n % 2, 0:sets]).then_inc(inv2_done, 1)
                dve.wait_ge(inv2_done, i0 + 1)
                p1 = s_2[n % 3][:, 0, 0:width]
                if kind < 2:
                    nc.vector.tensor_scalar(p1, p1, stat2[:, 2, n % 2, 0:1], None, ALU.mult).then_inc(p2_ready, 1)
                else:
                    nc.vector.tensor_scalar(p1, p1, stat2[:, 2, n % 2, 0:1], None, ALU.mult).then_inc(inv2_done, 1)
                    nc.vector.tensor_tensor(lam_inv[:, 0:1], stat2[:, 2, n % 2, 1:2], neg_lam[:, :], ALU.mult).then_inc(inv2_done, 1)
                    dve.wait_ge(inv2_done, i0 + 3)
                    stt(p1, s_2[n % 3][:, 1, 0:width], lam_inv[:, 0:1], p1, ALU.mult, ALU.add).then_inc(p2_ready, 1)

            for t in range(5):
                w0 = W_Q2 + 3 * t
                a = t - 1
                attend, project = t >= 1, t < 4
                for u in range(13):
                    n = 12 * a + u
                    if attend and u < 12:
                        logits2(n)
                    if a >= 1 and u == 2:
                        fox_rest(a - 1)
                    if a >= 1 and u == 4:
                        diff_rest(a - 1)
                    if project and u in (0, 4, 8) and (t, u) != (0, 0):
                        to_lo(*divmod(w0 + u // 4 + 1, 2))
                    if attend and u < 12:
                        weights2(n)
                    if t == 0 and u == 4:
                        dve.wait_ge(c_turned, 1)
                        nc.vector.tensor_copy(c_col[:, :, :], T1[:, 0:32].rearrange("p (t h) -> p t h", t=TB)).then_inc(c_col_ready, 1)
                    if project and u in (2, 4, 6, 8):
                        mi = u // 2 - 1
                        rstd_end(norm2(t, mi), NB[:, :], 64)
                        stt(qk[t % 2][mi][:, :], G[mi % 2][:, :], gains[:, 1 + mi:2 + mi], rstd[:, :], ALU.mult, ALU.mult).then_inc(acc_freed, 1)
                    if a >= 1 and u == 3:
                        diff_norm(a - 1)
                    if project and u in (10, 12):
                        half = u // 2 - 5
                        dve.wait_ge(mm_done, 2 * w0 + half + 5)
                        nc.vector.tensor_copy(v_2[t % 2][:, 2 * half:2 * half + 2, :], G[half][:, :].rearrange("p (t n) -> p t n", t=2))\
                            .then_inc(acc_freed, 1)
                if t == 0:
                    dve.wait_ge(c_col_ready, 1)
                    dve.wait_ge(c_row_ready, GROUPS)
            fox_rest(3)
            diff_norm(3)
            diff_rest(3)

            for c in range(4):
                w = W_OUT2 + c
                to_lo(*divmod(w + 1, 2))
                ada(S_OUT2 + c, 8)
                for half in range(2):
                    update_x(2 * c + half, G[2 * (w % 2) + half][:, :], GATE_1, 2 * w + half + 1, 1)
            gain(4, SCALE_2, G_LN2, S_OUT2)
            rstd_end(N_X3, NB[:, :], DM, x_rstd)
            h_split(4, SHIFT_2, False)
            ada_end(S_END - 1)
            dve.wait_ge(ada_out, S_END)

            def gate_up(u, f, par, first):
                to_lo(*next_chunk(u, par))
                dve.wait_ge(tanhg_done, f + first + 1)
                stt(tanh_g[par][:, :], tanh_g[par][:, :], 1.0, G[2 * par][:, :], ALU.add, ALU.mult).then_inc(acc_freed, 1)
                dve.wait_ge(mm_done, 4 * u + 2 * par + 2)
                dve.wait_ge(acc_freed, 4 * u + 2 * par - 15)
                stt(gu[par][:, :], tanh_g[par][:, :], 0.5, G[2 * par + 1][:, :], ALU.mult, ALU.mult).then_inc(acc_freed, 1)
                dve.wait_ge(guhi_done, f + first + 1)
                nc.vector.tensor_tensor(gu_lo[:, f, :], gu[par][:, :], f32(gu_hi[:, f, :]), ALU.subtract).then_inc(gulo_done, 1)

            with dve.Fori(W_GU1 // 2, W_DN1 // 2) as u:
                for par in range(2):
                    gate_up(u, 2 * (u - W_GU1 // 2) + par, par, 0)
            with dve.Fori(W_DN1 // 2, W_GU2 // 2) as u:
                for par in range(2):
                    to_lo(*next_chunk(u, par))
                    update_x(2 * (u - W_DN1 // 2) + par, G[2 * par][:, :], GATE_2, 4 * u + 2 * par + 2, 2)
            with dve.Fori(W_GU2 // 2, W_DN2 // 2) as u:
                for par in range(2):
                    gate_up(u, 2 * (u - W_GU2 // 2) + par, par, FF1)
            for c in range(4):
                w = W_DN2 + c
                if c < 3:
                    to_lo(*divmod(w + 1, 2), FF2 * 256)
                for half in range(2):
                    update_x(2 * c + half, G[2 * (w % 2) + half][:, :], GATE_2, 2 * w + half + 1, 1)

        @block.tensor
        def _(pe):
            def mm(out, lhsT, rhs, start, stop):
                return nc.tensor.matmul(out, lhsT, rhs, start=start, stop=stop)

            def split(out, parts, n, pieces):
                for kt in pieces:
                    a_hi, a_lo, b_hi, b_lo = parts(kt)
                    mm(out, a_hi, b_hi, kt == 0, False)
                    mm(out, a_hi, b_lo, False, False)
                    last = mm(out, a_lo, b_hi, False, kt == n - 1)
                return last

            def columns(out, par, half, kts, hi, lo_kt, pieces=None):
                n = 256 if kts <= KT else P
                wh = w_hi[par][:, 0:kts * n].rearrange("p (k n) -> p k n", k=kts)
                wl = w_lo[par][:, 0:kts * n].rearrange("p (k n) -> p k n", k=kts)
                for kt in pieces or range(kts):
                    a_hi, a_lo = wh[:, kt, P * half:P * half + P], wl[:, kt, P * half:P * half + P]
                    mm(out, a_hi, hi[:, kt, :], kt == 0, False)
                    mm(out, a_hi, lo_kt(kt), False, False)
                    last = mm(out, a_lo, hi[:, kt, :], False, kt == kts - 1)
                return last

            def h_lo_of(kt):
                return h_lo[:, kt, :]

            def rows(out, par, t, lo, n, pieces=range(KT), h=(h_hi, h_lo)):
                wh = w_hi[par][:, :].rearrange("p (k n) -> p k n", k=KT)
                wl = w_lo[par][:, :].rearrange("p (k n) -> p k n", k=KT)
                s = slice(P * t, P * t + P)
                return split(out, lambda kt: (h[0][:, kt, s], h[1][:, kt, s], wh[:, kt, lo:lo + n], wl[:, kt, lo:lo + n]), KT, pieces)

            def chunk_ready(u, par):
                pe.wait_ge(lo_done, 2 * u + par + 1)

            def ada_sum_up(r):
                pe.wait_ge(ada_sum, 8 * r + 8)
                ge(pe, ada_out, r)
                mm(AD[:, 0:1], ada_acc[:, 0:P], ones[:, 0:1], True, True)
                mm(AD[:, 1:2], ada_acc[:, P:2 * P], ones[:, 0:1], True, True).then_inc(ada_mm_done, 1)

            def h_ready(e, kt):
                pe.wait_ge(hlo_done, 8 * e + kt + 1)

            def first_chunk(e, w, outs, hi, lo_kt, freed):
                chunk_ready(*divmod(w, 2))
                for half in range(2):
                    pe.wait_ge(acc_freed, freed + half)
                for kt in range(KT):
                    h_ready(e, kt)
                    for half in range(2):
                        last = columns(outs[half][:, :], w % 2, half, KT, hi, lo_kt, (kt,))
                        if kt == KT - 1:
                            last.then_inc(mm_done, 1)

            def add_squares(k, norm):
                pe.wait_ge(sq_added, 6 * k + 6)
                pe.wait_ge(newton_done, norm)
                mm(NB[:, :], ones, sq_sum[:, :], True, False)
                pe.wait_ge(sq_ready, 8 * k + 16)
                mm(NB[:, :], ones, sq[1][:, :], False, True).then_inc(sum_done, 1)

            pe.wait_ge(silu_ready, 1)
            for s in range(0, UP, 2):
                pe.wait_ge(ada_up_loaded[(s + 1) % 4], 16 * (s // 4 + 1))
                for c in (2 * s + 2, 2 * s + 3):
                    for kt in range(KT):
                        last = mm(AD[:, c:c + 1], ada_up[(s + 1) % 4][:, kt, P * (c % 2):P * (c % 2) + P], silu_c[:, kt:kt + 1],
                                  kt == 0, kt == KT - 1)
                last.then_inc(up_done, 1)
                if s == 0:
                    pe.wait_ge(consts_loaded, 16)
                pe.wait_ge(up_sum, 4 * s + 8)
                for c in (2 * s, 2 * s + 1):
                    summed = mm(AD[:, c:c + 1], ada_acc[:, P * (c % 2):P * (c % 2) + P], ones[:, 0:1], True, True)
                summed.then_inc(up_summed, 1)
                if s == 2:
                    for kt in range(KT):
                        pe.wait_ge(sq_ready, kt + 1)
                        summed = mm(NB[:, :], ones, sq_first[kt][:, :], kt == 0, kt == KT - 1)
                    summed.then_inc(sum_done, 1)

            def v_pair(u):
                n = 2 * u - W_V
                for par in range(2):
                    chunk_ready(u, par)
                    for hb in range(2):
                        ge(pe, v_gelu_done, 4 * u + 2 * par + hb - 3)
                        for t in range(2):
                            last = rows(G[2 * par + hb][:, 256 * t:256 * t + 256], par, 2 * hb + t, 0, 256)
                        last.then_inc(mm_done, 1)
                        if hb == 0:
                            ada_sum_up(n + par - 1)

            chunk_ready(0, 0)
            for kt in range(KT):
                h_ready(0, kt)
                for t in range(TB):
                    last = rows(FIRST_V[t][:, 0:256], 0, t, 0, 256, (kt,))
                    if kt == KT - 1 and t % 2 == 1:
                        last.then_inc(mm_done, 1)
            chunk_ready(0, 1)
            for hb in range(2):
                for t in range(2):
                    last = rows(G[2 + hb][:, 256 * t:256 * t + 256], 1, 2 * hb + t, 0, 256)
                last.then_inc(mm_done, 1)
                if hb == 0:
                    ada_sum_up(0)
            with pe.Fori(1, W_UZ // 2) as u:
                v_pair(u)

            def uz_pair(u):
                jj = 2 * u - W_UZ
                for par in range(2):
                    j = jj + par
                    chunk_ready(u, par)
                    if isinstance(u, int):
                        pe.wait_ge(v_gelu_done, 2 * (W_UZ - 2 + par) + 2)
                    else:
                        pe.wait_ge(acc_freed, 2 * j - 2)
                    for half in range(2):
                        columns(G[2 * par + half][:, :], par, half, KT, h_hi, h_lo_of).then_inc(mm_done, 1)
                        if half == 0:
                            ada_sum_up(j + W_UZ - 1)
                    pe.wait_ge(v_staged, j + 1)
                    ge(pe, mix_freed, j - 1)
                    for c in range(TB):
                        mixed_c = mm((T0, T1)[par][:, P * c:P * c + P], v_stage[par][:, c, :], ws_t[:, u - W_UZ // 2, :], True, True)
                    mixed_c.then_inc(mix_done, 1)

            pe.wait_ge(ws_ready, 1)
            uz_pair(W_UZ // 2)
            with pe.Fori(W_UZ // 2 + 1, W_OUTA // 2) as u:
                uz_pair(u)

            pe.wait_ge(ylo_done, AT)
            with pe.Fori(W_OUTA // 2, W_KV // 2) as u:
                for par in range(2):
                    m = 2 * u - W_OUTA + par
                    chunk_ready(u, par)
                    pe.wait_ge(acc_freed, 4 * u + 2 * par - 18)
                    for piece in (range(KT), range(KT, AT)):
                        last = columns(G[2 * par][:, :], par, 0, AT, y_hi, lambda kt: y_lo[:, :, P * kt:P * kt + P], piece)
                        if piece[0] == 0:
                            ada_sum_up(m + W_OUTA - 1)
                    last.then_inc(mm_done, 2)
            add_squares(0, N_X1)

            def hk_lo_of(kt):
                return hk_lo[:, kt, :]

            def k_squares(c, half):
                pe.wait_ge(qsq_ready, 2 * c + half + 1)
                pe.wait_ge(newton_done, N_K + 2 * c + half)
                mm(NB[:, :], ones, sq[half][:, :], True, True).then_inc(sum_done, 1)

            for c in range(NKV // 2):
                w = W_KV + 2 * c
                if c == 0:
                    first_chunk(1, w, G, hk_hi, hk_lo_of, 2 * w - 19)
                    ada_sum_up(w - 1)
                else:
                    chunk_ready(w // 2, 0)
                    for half in range(2):
                        pe.wait_ge(acc_freed, 2 * w + half - 19)
                        columns(G[half][:, :], 0, half, KT, hk_hi, hk_lo_of).then_inc(mm_done, 1)
                        if half == 0:
                            ada_sum_up(w - 1)
                k_squares(c, 0)
                chunk_ready(w // 2, 1)
                for half in range(2):
                    if c > 0:
                        pe.wait_ge(acc_freed, 2 * w + half - 17)
                    for t in range(2):
                        last = rows(G[2 + half][:, 256 * t:256 * t + 256], 1, 2 * half + t, 0, 256, h=(hk_hi, hk_lo))
                    last.then_inc(mm_done, 1)
                    if half == 0:
                        k_squares(c, 1)
                        ada_sum_up(w)

            for kt in range(KT):
                h_ready(2, kt)

            def head(n, p, attend, project, prior):
                m, q = n - 1, 1 - p
                u0 = n + W_B // 2
                w0 = 2 * n + W_B
                k = 3 * n + N_Q

                def piece(mi):
                    if mi % 2 == 0:
                        chunk_ready(u0, mi // 2)
                    pe.wait_ge(acc_freed, 2 * w0 + mi - 17)
                    columns(G[mi % 2][:, :], mi // 2, mi % 2, KT, h_hi, h_lo_of).then_inc(mm_done, 1)

                def squares(mi):
                    pe.wait_ge(qsq_ready, k + mi - N_Q + NKV + 1)
                    pe.wait_ge(newton_done, k + mi)
                    mm(NB[:, :], ones, sq[(mi + p) % 2][:, :], True, True).then_inc(sum_done, 1)

                def scores(r):
                    if r == 0:
                        pe.wait_ge(acc_freed, 2 * w0 - 17)
                    if not (isinstance(n, int) and n == 1 and r == 0):
                        pe.wait_ge(s_freed, 4 * m + r)
                    s = slice(P * r, P * r + P)
                    mm(G[2][:, :], q_n[q][:, 0, s], k_t[:, q, :], True, True)
                    mm(G[3][:, 0:P], q_n[q][:, 1, s], k_t[:, 2 + q, s], True, True)
                    mm(G[3][:, P:2 * P], q_n[q][:, 2, s], k_t[:, 4 + q, s], True, True).then_inc(qk_done, 1)

                def turn(r):
                    pe.wait_ge(p_ready, 4 * m + r + 1)
                    for b in range(6):
                        bank = T0[:, P * b:P * b + P] if b < 4 else T1[:, P * (b - 4):P * (b - 3)]
                        turned = nc.tensor.transpose(bank, s_b[:, P * b:P * b + P], ident)
                    turned.then_inc(turn_done, 1)

                if attend:
                    scores(0)
                if project:
                    piece(0)
                elif attend:
                    early_output(0, (0, 4, 1, 5, 2, 6), 6)
                if prior:
                    values(m - 1, p, 3)
                for r in range(4):
                    if attend:
                        turn(r)
                        if r < 3:
                            scores(r + 1)
                    if project and r < 3:
                        squares(r)
                        piece(r + 1)
                    elif attend and r == 0:
                        early_output(1, (0, 4, 1, 5, 2, 6), 6)
                    if attend and r < 3:
                        if r == 0 and prior:
                            pe.wait_ge(head_out, m)
                        values(m, q, r)

            def values(m, q, r):
                pe.wait_ge(pt_act, 4 * m + r + 1)
                pe.wait_ge(pt_dve, 4 * m + r + 1)
                for b in range(6):
                    block_v, g = (b, 0) if b < 4 else (r, b - 3)
                    last = mm(AD[:, P * r:P * r + P], v_b[:, block_v, P * (2 * g + q):P * (2 * g + q + 1)], p_t[:, P * b:P * b + P],
                              b == 0, b == 5)
                last.then_inc(pv_done, 1)

            def yb_lo_of(kt):
                return yb_lo[:, kt, :]

            def early_output(half, kts, heads):
                chunk_ready(*divmod(W_OUTB, 2))
                pe.wait_ge(acc_freed, 2 * W_OUTB + half - 17)
                pe.wait_ge(yblo_done, heads)
                columns(G[half][:, :], W_OUTB % 2, half, KT, yb_hi, yb_lo_of, kts)

            head(0, 0, False, True, False)
            head(1, 1, True, True, False)
            head(2, 0, True, True, True)
            with pe.Fori(2, QH // 2) as i:
                head(2 * i - 1, 1, True, True, True)
                head(2 * i, 0, True, True, True)
            head(QH - 1, 1, True, True, True)
            head(QH, 0, True, False, True)
            values(QH - 1, 1, 3)

            def output(w0, hi, lo_kt, rest, steps):
                for c in range(4):
                    w = w0 + c
                    chunk_ready(*divmod(w, 2))
                    for half in range(2):
                        if c >= 2:
                            pe.wait_ge(acc_freed, 2 * w + half - 19)
                        columns(G[2 * (w % 2) + half][:, :], w % 2, half, KT, hi, lo_kt, rest if c == 0 else None).then_inc(mm_done, 1)
                        if (c, half) in steps:
                            ada_sum_up(steps[c, half])

            pe.wait_ge(yblo_done, QH)
            pe.wait_ge(s_freed, 4 * QH)
            output(W_OUTB, yb_hi, yb_lo_of, (3, 7), {(0, 0): 37, (0, 1): 38, (1, 0): 39, (2, 0): 40, (2, 1): 41, (3, 0): 42})
            add_squares(1, N_X2)

            pe.wait_ge(wflo_done, 1)
            chunk_ready(*divmod(W_Q2, 2))
            pe.wait_ge(acc_freed, 2 * W_Q2 - 17)
            for kt in range(KT):
                h_ready(3, kt)
                gates = split(T0[:, :], lambda kt: (wf_hi[:, kt, :], wf_lo[:, kt, :], h_hi[:, kt, :], h_lo[:, kt, :]), KT, (kt,))
                last = columns(G[0][:, :], W_Q2 % 2, 0, KT, h_hi, h_lo_of, (kt,))
            gates.then_inc(fg_done, 1)
            last.then_inc(mm_done, 1)

            def scores2(n):
                a, u = divmod(n, 12)
                kind, qb = UNITS2[u]
                before, first = s_reads(u)
                for e in range(2 if kind == 2 else 1):
                    if 16 * a + before + e >= 2:
                        pe.wait_ge(s2_freed, 16 * a + before + e - 1)
                    half = slice(64 * e, 64 * e + 64) if kind == 2 else slice(64 * kind, 64 * kind + 64)
                    qt, kt_ = (qk[a % 2][2], qk[a % 2][3]) if kind == 2 else (qk[a % 2][0], qk[a % 2][1])
                    score = mm(G[2 + (first + e) % 2][:, 0:(qb + 1) * P], qt[half, P * qb:P * qb + P], kt_[half, 0:(qb + 1) * P], True, True)
                score.then_inc(qk2_done, 1)

            def turn2(n):
                pe.wait_ge(p2_ready, n + 1)
                ge(pe, pt2_done, n)
                for b in range(UNITS2[n % 12][1] + 1):
                    turned = nc.tensor.transpose(T0[:, P * b:P * b + P], s_2[n % 3][:, 0, P * b:P * b + P], ident)
                turned.then_inc(turn2_done, 1)

            def values2(n):
                a, u = divmod(n, 12)
                kind, qb = UNITS2[u]
                pe.wait_ge(pt2_done, n + 1)
                if u == 0:
                    pe.wait_ge(mlo_done, 2 * a - 1) if a >= 1 else pe.wait_ge(ada_out, S_OUT2 - 1)
                if u == 2:
                    ge(pe, d_done, a)
                for b in range(qb + 1):
                    pt = pt_2[n % 2][:, P * b:P * b + P]
                    if kind == 2:
                        out, vt = T1[:, P * qb:P * qb + P], v_2[a % 2][:, b, P:2 * P]
                    else:
                        out, vt = AD[64 * kind:64 * kind + 64, P * qb:P * qb + P], v_2[a % 2][:, b, 64 * kind:64 * kind + 64]
                    last = mm(out, vt, pt, b == 0, b == qb)
                last.then_inc(pv2_done, 1)

            def head_squares(k, lhs):
                pe.wait_ge(qsq_ready, k - N_2 + 31)
                pe.wait_ge(newton_done, k)
                mm(NB[:, :], lhs, sq[k % 2][:, :], True, True).then_inc(sum_done, 1)

            def spread(n):
                ge(pe, c_row_ready, n - 1)
                mm((T0, T1)[n % 2][:, :], ident[0:8, n:n + 1].broadcast_to([8, P]), cum[:, :], True, True).then_inc(c_spread, 1)

            def m_lo_of(kt):
                return m_lo[:, kt, :]

            for t in range(5):
                w0 = W_Q2 + 3 * t
                a = t - 1
                attend, project = t >= 1, t < 4
                for u in range(12):
                    n = 12 * a + u
                    if attend:
                        if u == 0:
                            pe.wait_ge(acc_freed, 2 * w0 - 16)
                        scores2(n)
                        if n == 2:
                            pe.wait_ge(c_row_ready, GROUPS)
                        if n >= 2:
                            turn2(n - 2)
                        if n >= 3:
                            values2(n - 3)
                    if t == 0 and u == 4:
                        pe.wait_ge(fgate_dve, 4)
                        for b in range(TB):
                            turned = nc.tensor.transpose(T1[:, 8 * b:8 * b + 8], cum[:, P * b:P * b + P], ident[0:8, 0:8])
                        turned.then_inc(c_turned, 1)
                    if t == 0 and u >= 5:
                        if u == 5:
                            pe.wait_ge(c_col_ready, 1)
                        spread(u - 5)
                    if project and (t > 0 or u >= 2):
                        mi, w = u // 2, w0 + u // 4
                        par = w % 2
                        if u % 4 == 0:
                            pe.wait_ge(lo_done, w + 1)
                        if u == 10 or (u % 2 == 0 and mi < 5):
                            pe.wait_ge(acc_freed, 2 * w0 + mi - 17)
                        if mi < 4:
                            last = columns(G[mi % 2][:, :], par, mi % 2, KT, h_hi, h_lo_of, range(4 * (u % 2), 4 * (u % 2) + 4))
                        else:
                            last = rows(G[mi % 2][:, 256 * (u % 2):256 * (u % 2) + 256], par, u - 8, 0, 256)
                        if u % 2 == 1:
                            last.then_inc(mm_done, 1)
                    if project and u in (2, 4, 6, 8):
                        head_squares(norm2(t, u // 2 - 1), half_ones)
                    if a >= 1 and u == 3:
                        head_squares(norm_d(a - 1), ones)
                    if t == 4 and u in (6, 9):
                        half = (u - 6) // 3
                        pe.wait_ge(lo_done, W_OUT2 + 1)
                        pe.wait_ge(mlo_done, 6)
                        columns(G[half][:, :], W_OUT2 % 2, half, KT, m_hi, m_lo_of, (0, 1, 2, 4, 5, 6))
                if t == 0:
                    spread(7)
            turn2(46)
            values2(45)
            turn2(47)
            values2(46)
            values2(47)
            head_squares(norm_d(3), ones)

            pe.wait_ge(mlo_done, KT)
            output(W_OUT2, m_hi, m_lo_of, (3, 7), {(c, 0): S_OUT2 - 1 + c for c in range(4)})
            ada_sum_up(S_END - 1)
            add_squares(2, N_X3)

            def gate_up(u, pars=range(2)):
                for par in pars:
                    chunk_ready(u, par)
                    for half in range(2):
                        pe.wait_ge(acc_freed, 4 * u + 2 * par + half - 19)
                        columns(G[2 * par + half][:, :], par, half, KT, h_hi, h_lo_of).then_inc(mm_done, 1)

            def gu_lo_of(kt):
                return gu_lo[:, kt, :]

            first_chunk(4, W_GU1, G, h_hi, h_lo_of, 2 * W_GU1 - 19)
            gate_up(W_GU1 // 2, (1,))
            with pe.Fori(W_GU1 // 2 + 1, W_DN1 // 2) as u:
                gate_up(u)
            pe.wait_ge(gulo_done, FF1)
            with pe.Fori(W_DN1 // 2, W_GU2 // 2) as u:
                for par in range(2):
                    chunk_ready(u, par)
                    pe.wait_ge(acc_freed, 4 * u + 2 * par - 18)
                    columns(G[2 * par][:, :], par, 0, FF1, gu_hi, gu_lo_of).then_inc(mm_done, 2)
            with pe.Fori(W_GU2 // 2, W_DN2 // 2) as u:
                gate_up(u)
            pe.wait_ge(gulo_done, FF1 + FF2)
            for w in range(W_DN2, W_END):
                chunk_ready(*divmod(w, 2))
                for half in range(2):
                    pe.wait_ge(acc_freed, 2 * w + half - 19)
                    columns(G[2 * (w % 2) + half][:, :], w % 2, half, FF2, gu_hi, gu_lo_of).then_inc(mm_done, 1)


INPUTS = ["a_b_spatial", "diff_lam_2", "b_f_2"]


def layout(inputs):
    src = {name: np.asarray(a) for name, a in inputs.items()}

    def kn(w):
        return w.reshape(-1, P, w.shape[1]).transpose(1, 0, 2)

    w_in_a, w_out_a, w_kv = kn(src["a_w_in"][0]), kn(src["a_w_out"][0]), kn(src["w_kv"])
    w_in_b, w_out_b = kn(src["b_w_in"][0]), kn(src["b_w_out"][0])
    w_in_2, w_out_2 = kn(src["w_in_2"][0]), kn(src["w_out_2"][0])
    w_gate, w_up, w_down = kn(src["w_gate_2"][0]), kn(src["w_up_2"][0]), kn(src["w_down_2"][0])
    chunks = []

    def span(w, lo, n=256):
        chunks.append([w[:, :, lo:lo + n]])

    def pair(wa, a, wb, b):
        chunks.append([wa[:, :, a:a + P], wb[:, :, b:b + P]])

    def gate_up(first, n):
        for f in range(first, first + n):
            pair(w_gate, P * f, w_up, P * f)

    for n in range(8):
        span(w_in_a, AW + 256 * n)
    for j in range(AT):
        pair(w_in_a, P * j, w_in_a, 2 * AW + P * j)
    for m in range(KT):
        span(w_out_a, P * m, P)
    for c in range(NKV // 2):
        span(w_kv, 256 * c)
        span(w_kv, NKV * P + 256 * c)
    for n in range(QH):
        col = P * (n // 2) + 4 * P * (n % 2)
        pair(w_in_b, col, w_in_b, col + DM)
        pair(w_in_b, col + 2 * DM, w_in_b, col + 3 * DM)
    for c in range(4):
        span(w_out_b, 256 * c)
    for t in range(4):
        fox, dif = P * t, 1544 + P * t
        pair(w_in_2, fox, w_in_2, fox + 512)
        pair(w_in_2, dif, w_in_2, dif + 512)
        pair(w_in_2, fox + 1024, w_in_2, dif + 1024)
    for c in range(4):
        span(w_out_2, 256 * c)
    gate_up(0, FF1)
    for m in range(KT):
        span(w_down[:, 0:FF1], P * m, P)
    gate_up(FF1, FF2)
    for c in range(4):
        span(w_down[:, FF1:], 256 * c)
    weights = np.zeros((W_END, P, 2048), np.float32)
    for w, parts in enumerate(chunks):
        tile = np.concatenate(parts, axis=2)
        weights[w, :, 0:tile.shape[1] * tile.shape[2]] = tile.reshape(P, -1)

    mod_weights = {"a": kn(src["a_ada_w"][0]), "kv": kn(src["kv_ada_w"]), "b": kn(src["b_ada_w"][0]), "2": kn(src["w_ada_2"][0])}
    mod_biases = {"a": src["a_ada_b"][0], "kv": src["kv_ada_b"], "b": src["b_ada_b"][0], "2": src["b_ada_2"][0]}
    ada = [mod_weights[name][:, :, 256 * s:256 * s + 256].reshape(P, 2048) for name, lo, n in MODS for s in range(lo, lo + n)]
    rows = [src[name].reshape(-1, P) for name in ("c", "c_2", "a_norm_g", "kv_norm_g", "b_norm_g", "ln1_g_2", "ln2_g_2", "a_sgu_g",
                                                  "k_norm_g", "b_q_norm_g", "diff_norm_g_2")]
    rows += [np.concatenate([src[name][0]] * 2, axis=1) for name in ("fox_qk_g_2", "diff_qk_g_2")]
    rows += [mod_biases[name].reshape(-1, P)[2 * lo:2 * lo + 2 * n] for name, lo, n in MODS]
    tiles, blocks = constants()
    arrays = {name: src[name] for name in INPUTS}
    arrays.update(weights=weights, ada=np.stack(ada), vecs=np.concatenate(rows, axis=0).T, tiles=tiles, blocks=blocks,
                  x=src["x"][0].T.reshape(KT, P, TOK).transpose(1, 0, 2),
                  spatial=src["a_w_spatial"][0].transpose(2, 0, 1), forget=w_in_2[:, :, 1536:1544])
    return {f"in_{name}": np.ascontiguousarray(a) for name, a in arrays.items()}


def kernel(**inputs):
    from concourse import bacc
    from concourse.bass_utils import run_bass_kernel_spmd

    nc = bacc.Bacc("TRN2", target_bir_lowering=False, num_devices=1)
    arrays = layout(inputs)
    d = {n[3:]: nc.dram_tensor(n, a.shape, mybir.dt.from_np(a.dtype), kind="ExternalInput").ap() for n, a in arrays.items()}
    d["out"] = nc.dram_tensor("out", (P, KT, TOK), F32, kind="ExternalOutput").ap()
    program(nc, d)
    run = run_bass_kernel_spmd(nc, [arrays], core_ids=[0])
    return np.ascontiguousarray(run.results[0]["out"].transpose(2, 1, 0)).reshape(1, TOK, DM)
```

```python
import math

import numpy as np

import concourse.bass as bass
from concourse import mybir
from concourse.alu_op_type import AluOpType as ALU

F32 = mybir.dt.float32
F32R = mybir.dt.float32r
ACT = mybir.ActivationFunctionType
AX = mybir.AxisListType.X

P = 128
TOK = 512
TB = TOK // P
DM = 1024
KT = DM // P
EPS = 1e-6
AW = 2 * DM
AT = AW // P
GROUPS = 8
QH = DM // P
NKV = 6
SLOPES_B = [2.0 ** (-8.0 * h / 24) for h in range(1, 25)]
SLOPES_D = [2.0 ** (-8.0 * h / 4) for h in range(1, 5)]
FF = 2816
FF1, FF2 = 16, 6
LAM_INIT = 0.8 - 0.6 * math.exp(0.0)
FAR = 1e30

W_V = 0
W_UZ = W_V + 8
W_OUTA = W_UZ + 16
W_KV = W_OUTA + 8
W_B = W_KV + 6
W_OUTB = W_B + 16
W_Q2 = W_OUTB + 4
W_OUT2 = W_Q2 + 12
W_GU1 = W_OUT2 + 4
W_DN1 = W_GU1 + FF1
W_GU2 = W_DN1 + 8
W_DN2 = W_GU2 + FF2
W_END = W_DN2 + 4

MODS = [("a", 0, 8), ("kv", 0, 8), ("b", 0, 12), ("a", 8, 4), ("2", 0, 24)]
UP = 8
UP_TENSOR, UP_VECTOR = (0, 2, 3, 6), (1, 4, 5, 7)
S_B, S_OUTB, S_END = 38, 46, 48
SHIFT_A, SCALE_A, SHIFT_KV, SCALE_KV = 0, 8, 16, 24
SHIFT_B, SCALE_B, GATE_B, GATE_A = 32, 40, 48, 56
SHIFT_1, SCALE_1, GATE_1, SHIFT_2, SCALE_2, GATE_2 = 64, 72, 80, 88, 96, 104
NMOD = 112

C_1, C_2, G_A, G_KV, G_B, G_LN1, G_LN2, G_SGU = 0, 8, 16, 24, 32, 40, 48, 56
G_K, G_QB, G_DN, G_FQ, G_FK, G_DQ, G_DK = 72, 73, 74, 75, 76, 77, 78
NVEC = 79


def constants():
    i, j = np.arange(P)[:, None], np.arange(P)[None, :]
    ident = np.eye(P)
    ones = np.ones((P, P))
    half = np.kron(np.eye(2), np.ones((64, 64)))
    causal_t = (i <= j) * 1.0
    blocks = []
    for shift in range(3, -4, -1):
        d = 4 * (i - j) + shift
        blocks.append(np.where((d >= 0) & (d <= P), d, FAR))
    d4 = 4 * (i - j)
    blocks.append(np.where(d4 >= 0, d4, FAR))
    blocks.append(np.where((d4 >= 0) & (d4 % 16 == 0), d4, FAR))
    x = np.arange(TOK)[None, :]
    d = i + TOK - P - x
    slopes = np.broadcast_to(-np.array(SLOPES_B, np.float32), (P, 24))
    last = np.broadcast_to(np.array([EPS, 0.0, 0.0, 0.0]), (P, 4))
    tiles = [ident, ones, half, causal_t, np.where(d >= 0, d, FAR), np.where(i >= j, 0.0, -FAR), slopes, last]
    return [np.concatenate(part, axis=1).astype(np.float32) for part in (tiles, blocks)]


K_ID, K_ONE, K_HALF, K_TRI, K_DIST, K_MASK = 0, P, 2 * P, 3 * P, 4 * P, 4 * P + TOK
K_SLOPE = K_MASK + P
K_EPS = K_SLOPE + 24
NCONST = K_EPS + 4


def program(nc, d):
    base = 16512
    top = [base]

    def at(name, shape, off, dt=F32):
        return nc.alloc_sbuf_tensor_at(name, shape, dt, offset=off)

    def take(nbytes):
        off = top[0]
        top[0] += (nbytes + 63) // 64 * 64
        return off

    KB = 1024
    x = at("x", [P, KT, TOK], take(16 * KB))
    off_h = take(32 * KB)
    h_hi = at("h_hi", [P, KT, TOK], off_h, F32R)
    h_lo = at("h_lo", [P, KT, TOK], off_h + 16 * KB, F32R)
    w_raw = [at(f"w_raw{s}", [P, 2048], take(8 * KB)) for s in range(2)]
    w_hi = [at(f"w_hi{s}", [P, 2048], take(8 * KB), F32R) for s in range(2)]
    w_lo = [at(f"w_lo{s}", [P, 2048], take(8 * KB), F32R) for s in range(2)]
    off_ada = take(8 * KB)
    ada_raw = at("ada_raw", [P, KT, 256], off_ada)
    consts = at("consts", [P, NCONST], take(4 * NCONST))
    vecs = at("vecs", [P, NVEC + NMOD], take(4 * (NVEC + NMOD)))
    mod_bias = vecs[:, NVEC:NVEC + NMOD]
    mods = at("mods", [P, NMOD], take(4 * NMOD))
    silu_c = at("silu_c", [P, 16], take(64))
    gains = at("gains", [P, 8], take(32))
    gscale = at("gscale", [P, 8], take(32))
    ada_acc = at("ada_acc", [P, 256], take(KB))
    off_rstd = take(2 * KB)
    x_rstd = at("x_rstd", [P, TOK], off_rstd)
    v_sums = at("v_sums", [P, TB, GROUPS], take(128))
    v_stat = at("v_stat", [P, 8, TB], take(128))
    row_stat = at("row_stat", [P, 3, 4], take(64))
    stat2 = at("stat2", [P, 3, 2, 2], take(64))
    lam_inv = at("lam_inv", [P, 2], take(8))
    lam_two = at("lam_two", [P, 2], take(8))
    neg_lam = at("neg_lam", [P, 1], take(4))
    c_col = at("c_col", [P, TB, 8], take(128))
    bf_col = at("bf_col", [8, 1], take(4))
    wf_raw = at("wf_raw", [P, KT, 8], take(256))
    ident, ones, half_ones = consts[:, K_ID:K_ID + P], consts[:, K_ONE:K_ONE + P], consts[:, K_HALF:K_HALF + P]
    tmp0 = take(18 * KB)
    T = [tmp0 + 2 * KB * s for s in range(9)]
    sq = [at(f"sq{s}", [P, TOK], T[s]) for s in range(2)]
    sq_first = [at(f"sq_first{s}", [P, TOK], T[s]) for s in range(8)]
    y0 = at("y0", [P, TOK], T[3])
    y0_half = at("y0_half", [P, TOK], T[4])
    sq_sum = at("sq_sum", [P, TOK], T[5])
    rstd = at("rstd", [P, TOK], T[6])
    hx = [at(f"hx{s}", [P, TOK], T[7 + s]) for s in range(2)]
    off_blocks = take(4 * 9 * P)
    big = top[0]

    up_acc = [ada_acc, at("ada_acc1", [P, 256], T[8])]

    v = at("v", [P, TB, AW], big)
    y_lo = at("y_lo", [P, TB, AW], big, F32R)
    y_hi = at("y_hi", [P, AT, TOK], big + 32 * KB, F32R)
    ada_up = [at(f"ada_up{s}", [P, KT, 256], (big + 32 * KB if s < 4 else off_h) + 8 * KB * (s % 4)) for s in range(UP)]
    ws_t = at("ws_t", [P, GROUPS, P], big + 64 * KB)
    b_sp = at("b_sp", [P, GROUPS, P], off_blocks)
    ws_raw = at("ws_raw", [P, GROUPS, P], big + 20 * KB)
    gelu_u = [at(f"gelu_u{s}", [P, TOK], T[2 + s]) for s in range(2)]
    tanh_z = at("tanh_z", [P, TOK], T[4])
    mixed = [at(f"mixed{s}", [P, TOK], T[5 + s]) for s in range(2)]
    v_stage = [at(f"v_stage{s}", [P, TB, P], T[7 + s]) for s in range(2)]
    v_sq = at("v_sq", [P, TB, 256], T[2])

    k_t = at("k_t", [P, NKV, TOK], big)
    v_b = at("v_b", [P, TB, NKV * P], big + 12 * KB)
    hk_hi = at("hk_hi", [P, KT, TOK], big + 24 * KB, F32R)
    hk_lo = at("hk_lo", [P, KT, TOK], big + 40 * KB, F32R)
    yb_hi = at("yb_hi", [P, QH, TOK], big + 24 * KB, F32R)
    yb_lo = at("yb_lo", [P, QH, TOK], big + 40 * KB, F32R)
    q_n = [[at(f"q_n{s}_{n}", [P, TOK], (big + 68 * KB, off_rstd, T[1])[n] if s == 0 else big + (56 + 2 * n) * KB) for n in range(3)]
           for s in range(2)]
    s_b = at("s_b", [P, 768], big + 62 * KB)
    p_t = at("p_t", [P, 768], big + 65 * KB)
    z_b = [at("z_b0", [P, TOK], T[2]), at("z_b1", [P, TOK], T[5])]
    z_t = at("z_t", [P, TOK], T[7])
    yb = at("yb", [P, TOK], T[8])
    blocks = at("blocks", [P, 9, P], off_blocks)

    qk = [[at(f"qk{s}_{n}", [P, TOK], big + (4 * s + n) * 2 * KB) for n in range(4)] for s in range(2)]
    v_2 = [at(f"v2{s}", [P, TB, 2 * P], big + (16 + 4 * s) * KB) for s in range(2)]
    m_hi = at("m_hi", [P, KT, TOK], big + 24 * KB, F32R)
    m_lo = at("m_lo", [P, KT, TOK], big + 40 * KB, F32R)
    c_row = [at(f"c_row{n}", [P, TOK], big + (24 + 16 * (n % 2) + n // 2 * 2) * KB) for n in range(8)]
    s_2 = [at(f"s_2{s}", [P, 2, TOK], off) for s, off in enumerate((big + 56 * KB, big + 60 * KB, off_blocks))]
    pt_2 = [at(f"pt_2{s}", [P, TOK], big + 64 * KB + 2 * KB * s) for s in range(2)]
    lam_rows = at("lam_rows", [P, 256], big + 24 * KB)
    lam_prod = at("lam_prod", [P, 128], big + 25 * KB)
    wf_hi = at("wf_hi", [P, KT, P], big + 56 * KB, F32R)
    wf_lo = at("wf_lo", [P, KT, P], big + 60 * KB, F32R)
    gate_abs = at("gate_abs", [8, TOK], T[5])
    gate_exp = at("gate_exp", [8, TOK], T[5])
    gate_ln = at("gate_ln", [8, TOK], T[5])
    gate_min = at("gate_min", [8, TOK], T[7])
    gate_log = at("gate_log", [8, TOK], T[7])
    gate_one = at("gate_one", [8, TOK], big + 68 * KB)
    cum = at("cum", [8, TOK], T[8])
    d_out = at("d_out", [P, TOK], T[7])
    assert big + 70 * KB <= 229344, big

    gu_hi = at("gu_hi", [P, FF1, TOK], big, F32R)
    gu_lo = at("gu_lo", [P, FF1, TOK], big + 32 * KB, F32R)
    tanh_g = [at(f"tanh_g{s}", [P, TOK], T[2 + s]) for s in range(2)]
    gu = [at(f"gu{s}", [P, TOK], T[4 + s]) for s in range(2)]

    G = [nc.alloc_psum_tensor(f"acc{n}", [P, TOK], F32) for n in range(4)]
    T0 = nc.alloc_psum_tensor("turn0", [P, TOK], F32)
    T1 = nc.alloc_psum_tensor("turn1", [P, TOK], F32)
    NB = nc.alloc_psum_tensor("norm", [P, TOK], F32)
    AD = nc.alloc_psum_tensor("ada", [P, TOK], F32)
    FIRST_V = (G[0], T0, G[1], T1)

    def sem(name):
        return nc.alloc_semaphore(name)

    vecs_loaded, consts_loaded, ws_loaded = sem("vecs_loaded"), sem("consts_loaded"), sem("ws_loaded")
    x_loaded = [sem("x_loaded0"), sem("x_loaded1")]
    small_loaded, blocks_loaded, stored = sem("small_loaded"), sem("blocks_loaded"), sem("stored")
    w_loaded = [sem("w_loaded0"), sem("w_loaded1")]
    ada_loaded, ada_up_loaded = sem("ada_loaded"), [sem(f"ada_up_loaded{s}") for s in range(UP)]
    hi_done, lo_done = sem("hi_done"), sem("lo_done")
    mm_done, acc_freed, v_gelu_done = sem("mm_done"), sem("acc_freed"), sem("v_gelu_done")
    ada_sum, ada_mm_done, ada_out = sem("ada_sum"), sem("ada_mm_done"), sem("ada_out")
    up_sum, up_summed, up_done, up_out = sem("up_sum"), sem("up_summed"), sem("up_done"), sem("up_out")
    silu_ready, gains_ready, ws_ready = sem("silu_ready"), sem("gains_ready"), sem("ws_ready")
    lam_part, lam_exp, lam_ready = sem("lam_part"), sem("lam_exp"), sem("lam_ready")
    sq_ready, sq_added, qsq_ready = sem("sq_ready"), sem("sq_added"), sem("qsq_ready")
    sum_done, ln_done, y0_done, half_done = sem("sum_done"), sem("ln_done"), sem("y0_done"), sem("half_done")
    newton_done, rstd_done = sem("newton_done"), sem("rstd_done")
    gs_done, hx_done, hhi_done, hlo_done = sem("gs_done"), sem("hx_done"), sem("hhi_done"), sem("hlo_done")
    hx_start = sem("hx_start")
    v_sums_done, v_stat_dve, v_stat_act = sem("v_sums_done"), sem("v_stat_dve"), sem("v_stat_act")
    v_staged, mix_done, mix_freed = sem("v_staged"), sem("mix_done"), sem("mix_freed")
    gelu_done, tanh_done, uz_done = sem("gelu_done"), sem("tanh_done"), sem("uz_done")
    y_done, yhi_done, ylo_done = sem("y_done"), sem("yhi_done"), sem("ylo_done")
    qk_done, s_freed, max_done, exp_done = sem("qk_done"), sem("s_freed"), sem("max_done"), sem("exp_done")
    inv_done, p_ready, turn_done = sem("inv_done"), sem("p_ready"), sem("turn_done")
    pt_act, pt_dve, pv_done = sem("pt_act"), sem("pt_dve"), sem("pv_done")
    z_exp, z_part = sem("z_exp"), sem("z_part")
    head_out, ybhi_done, yblo_done = sem("head_out"), sem("ybhi_done"), sem("yblo_done")
    wf_zeroed, wfhi_done, wflo_done, fg_done = sem("wf_zeroed"), sem("wfhi_done"), sem("wflo_done"), sem("fg_done")
    fgate_act, fgate_dve, c_turned, c_col_ready = sem("fgate_act"), sem("fgate_dve"), sem("c_turned"), sem("c_col_ready")
    c_spread, c_row_ready = sem("c_spread"), sem("c_row_ready")
    qk2_done, s2_freed, bias2_done, max2_done, exp2_done = sem("qk2_done"), sem("s2_freed"), sem("bias2_done"), sem("max2_done"), sem("exp2_done")
    inv2_done, p2_ready, turn2_done, pt2_done, pv2_done = sem("inv2_done"), sem("p2_ready"), sem("turn2_done"), sem("pt2_done"), sem("pv2_done")
    d_done, mhi_done, mlo_done = sem("d_done"), sem("mhi_done"), sem("mlo_done")
    tanhg_done, gz_done, guhi_done, gulo_done = sem("tanhg_done"), sem("gz_done"), sem("guhi_done"), sem("gulo_done")

    N_X0, N_X1, N_K, N_Q, N_X2, N_2 = 0, 1, 2, 8, 32, 33
    N_X3 = N_2 + 20

    def norm2(t, mi):
        return N_2 + 4 * t + max(0, t - 1) + mi

    def norm_d(a):
        return N_2 + (8, 13, 18, 19)[a]

    UNITS2 = [(kind, qb) for qb in range(TB) for kind in (2, 0, 1)]

    def ge(eng, semaphore, value):
        if not isinstance(value, int) or value > 0:
            eng.wait_ge(semaphore, value)

    def next_chunk(u, par):
        return (u, 1) if par == 0 else (u + 1, 0)

    def dilated(tile):
        return tile.rearrange("p (i r) -> p r i", r=4)

    def four(tile):
        return tile.rearrange("p (r i) -> p r i", r=4)

    def s_reads(u):
        before = sum(2 if kind == 2 else 1 for kind, qb in UNITS2[:u])
        return before, before % 2

    block = nc.Block()
    with block:

        @block.sync
        def _(sp):
            weights, ada_weights = d["weights"], d["ada"]

            def load(u, par, used=2048):
                src = weights[bass.ds(2 * u + par, 1), :, 0:used].rearrange("a p n -> p (a n)")
                sp.lower_ap_dma(src)
                ge(sp, lo_done, 2 * u + par - 1)
                sp.dma_start(w_raw[par][:, 0:used], src).then_inc(w_loaded[par], 16)

            def ada_load(r):
                src = ada_weights[bass.ds(r + UP, 1), :, :].rearrange("a p n -> p (a n)")
                sp.lower_ap_dma(src)
                ge(sp, ada_sum, 8 * r)
                sp.dma_start(ada_raw[:, :, :].rearrange("p k n -> p (k n)"), src).then_inc(ada_loaded, 16)

            def ada_up_load(s):
                sp.dma_start(ada_up[s][:, :, :].rearrange("p k n -> p (k n)"), ada_weights[s]).then_inc(ada_up_loaded[s], 16)

            sp.dma_start(vecs[:, :], d["vecs"]).then_inc(vecs_loaded, 16)
            for s in range(3):
                ada_up_load(s)
            for half in range(2):
                sp.dma_start(x[:, 4 * half:4 * half + 4, :], d["x"][:, 4 * half:4 * half + 4, :]).then_inc(x_loaded[half], 16)
            for s in range(3, UP):
                ada_up_load(s)
            for par in range(2):
                load(W_V // 2, par)

            for par in range(2):
                load(1, par)
                ada_load(par)
            with sp.Fori(2, W_B // 2 + 1) as u:
                for par in range(2):
                    load(u, par)
                    ada_load(2 * u + par - 2)
            with sp.Fori(W_B // 2 + 1, W_OUTB // 2 + 1) as u:
                for par in range(2):
                    load(u, par)
                ada_load(u + (S_B - W_B // 2 - 1))
            for par in range(2):
                load(W_OUTB // 2 + 1, par)
                ada_load(S_OUTB + par)
            with sp.Fori(W_Q2 // 2, W_DN2 // 2) as u:
                for par in range(2):
                    load(u, par)
            for w in range(W_DN2, W_END):
                load(*divmod(w, 2), FF2 * 256)
            for m in range(KT):
                sp.wait_ge(acc_freed, 2 * W_DN2 - 15 + m)
                sp.dma_start(d["out"][:, m, :], x[:, m, :]).then_inc(stored, 16)
            sp.wait_ge(stored, 16 * KT)

        @block.gpsimd
        def _(pool):
            def to_lo(u, par):
                pool.wait_ge(hi_done, 2 * u + par + 1)
                pool.wait_ge(lo_done, 2 * u + par)
                nc.gpsimd.tensor_tensor(w_lo[par][:, :], w_raw[par][:, :], w_hi[par][:, :].bitcast(F32), ALU.subtract).then_inc(lo_done, 1)

            def stage(j, par):
                ge(pool, mix_done, j - 1)
                nc.gpsimd.tensor_tensor(v_stage[par][:, :, :], v[:, :, bass.ds(j * P, P)],
                                        v_stat[:, 5, :].unsqueeze(2).broadcast_to([P, TB, P]), ALU.mult).then_inc(v_staged, 1)

            def sum_squares(k, total, tile):
                for m in range(1, KT - 1):
                    pool.wait_ge(sq_ready, 8 * k + m + 1)
                    if m > 1:
                        pool.wait_ge(sq_added, 6 * k + m - 1)
                    nc.gpsimd.tensor_tensor(total, tile(0) if m == 1 else total, tile(m), ALU.add).then_inc(sq_added, 1)

            sum_squares(0, sq_first[0][:, :], lambda m: sq_first[m][:, :])
            to_lo(0, 1)
            pool.wait_ge(v_stat_dve, 3)
            stage(0, 0)
            stage(1, 1)
            with pool.Fori(1, AT // 2) as i:
                for par in range(2):
                    stage(2 * i + par, par)

            sum_squares(1, sq_sum[:, :], lambda m: sq[m % 2][:, :])
            to_lo(W_KV // 2, 1)
            with pool.Fori(W_B // 2, W_OUTB // 2) as u:
                to_lo(u, 1)
                to_lo(u + 1, 0)
            to_lo(W_OUTB // 2, 1)
            pool.wait_ge(pv_done, 4 * QH)
            nc.gpsimd.memset(wf_hi[:, :, :].bitcast(F32), 0.0).then_inc(wf_zeroed, 1)
            nc.gpsimd.memset(wf_lo[:, :, :].bitcast(F32), 0.0).then_inc(wf_zeroed, 1)
            sum_squares(2, sq_sum[:, :], lambda m: sq[m % 2][:, :])
            to_lo(W_Q2 // 2, 1)
            with pool.Fori(W_Q2 // 2 + 1, W_OUT2 // 2 + 1) as u:
                for par in range(2):
                    to_lo(u, par)
            sum_squares(3, sq_sum[:, :], lambda m: sq[m % 2][:, :])
            to_lo(W_GU1 // 2, 1)

        @block.scalar
        def _(act):
            eps_col = consts[:, K_EPS:K_EPS + 1]

            def to_hi(u, par, used=2048):
                act.wait_ge(w_loaded[par], 16 * u + 16)
                ge(act, mm_done, 4 * u + 2 * par - 2)
                nc.scalar.activation(w_hi[par][:, 0:used], w_raw[par][:, 0:used], ACT.Copy).then_inc(hi_done, 1)

            def rstd_start(k, total, count):
                act.wait_ge(sum_done, k + 1)
                ge(act, rstd_done, k)
                nc.scalar.activation(y0[:, :], total, ACT.Ln, scale=1.0 / count, bias=eps_col).then_inc(ln_done, 1)
                act.wait_ge(ln_done, k + 1)
                nc.scalar.activation(y0[:, :], y0[:, :], ACT.Exp, scale=-0.5).then_inc(y0_done, 1)
                act.wait_ge(y0_done, k + 1)
                nc.scalar.activation(y0_half[:, :], y0[:, :], ACT.Square, scale=math.sqrt(0.5 / count)).then_inc(half_done, 1)

            def h_round(e, shift, dilate, kts=range(KT), h=h_hi):
                for kt in kts:
                    act.wait_ge(hx_done, 8 * e + kt + 1)
                    src, dst = hx[kt % 2][:, :], h[:, kt, :]
                    nc.scalar.activation(four(dst) if dilate else dst, dilated(src) if dilate else src, ACT.Identity,
                                         bias=mods[:, shift + kt:shift + kt + 1]).then_inc(hhi_done, 1)

            def square_x(k, m, seen):
                act.wait_ge(acc_freed, seen)
                if m >= 2:
                    act.wait_ge(sq_added, 6 * k + max(1, m - 2))
                nc.scalar.activation(sq[m % 2][:, :], x[:, m, :], ACT.Square).then_inc(sq_ready, 1)

            act.dma_start(consts[:, :], d["tiles"]).then_inc(consts_loaded, 16)
            act.dma_start(ws_raw[:, :, :], d["spatial"]).then_inc(ws_loaded, 16)
            act.dma_start(b_sp[:, :, :], d["a_b_spatial"][0].rearrange("g t -> (g t)").partition_broadcast(P)
                          .rearrange("p (g t) -> p g t", g=GROUPS)).then_inc(small_loaded, 16)
            act.dma_start(lam_rows[:, :], d["diff_lam_2"][0].rearrange("a b -> (a b)").partition_broadcast(P)).then_inc(small_loaded, 16)
            act.dma_start(bf_col[:, :], d["b_f_2"].rearrange("a h -> h a")).then_inc(small_loaded, 16)
            act.dma_start(wf_raw[:, :, :], d["forget"]).then_inc(small_loaded, 16)

            act.wait_ge(vecs_loaded, 16)
            nc.scalar.activation(silu_c[:, :], vecs[:, C_1:C_1 + 16], ACT.Silu).then_inc(silu_ready, 1)
            act.preload_act_table_set("natural_log_exp_and_others")
            for kt in range(KT):
                act.wait_ge(x_loaded[kt // 4], 16)
                nc.scalar.activation(sq_first[kt][:, :], x[:, kt, :], ACT.Square).then_inc(sq_ready, 1)
            rstd_start(N_X0, NB[:, :], DM)
            act.wait_ge(lam_part, 2)
            nc.scalar.activation(lam_two[:, :], lam_two[:, :], ACT.Exp).then_inc(lam_exp, 1)
            to_hi(0, 0)
            to_hi(0, 1)
            h_round(0, SHIFT_A, False)

            def v_pair(u):
                n = 2 * u - W_V
                for par in range(2):
                    if not (isinstance(u, int) and par == 0):
                        to_hi(*next_chunk(u, par))
                    for hb in range(2):
                        act.wait_ge(mm_done, 4 * u + 2 * par + hb + 1)
                        if isinstance(u, int) and par == 0:
                            nc.scalar.activation(v[:, 2 * hb, 0:256], FIRST_V[2 * hb][:, 0:256], ACT.Gelu_apprx_tanh)
                            nc.scalar.activation(v[:, 2 * hb + 1, 0:256], FIRST_V[2 * hb + 1][:, 0:256], ACT.Gelu_apprx_tanh)\
                                .then_inc(v_gelu_done, 1)
                            continue
                        nc.scalar.activation(v[:, 2 * hb:2 * hb + 2, bass.ds(256 * n + 256 * par, 256)],
                                             G[2 * par + hb][:, :].rearrange("p (t n) -> p t n", t=2),
                                             ACT.Gelu_apprx_tanh).then_inc(v_gelu_done, 1)

            v_pair(0)
            with act.Fori(1, W_UZ // 2) as u:
                v_pair(u)
            act.preload_act_table_set("natural_log_exp_and_others")
            act.wait_ge(v_stat_dve, 1)
            nc.scalar.activation(v_stat[:, 1, :], v_stat[:, 0, :], ACT.Ln, scale=1.0 / AW, bias=eps_col).then_inc(v_stat_act, 1)
            act.wait_ge(v_stat_act, 1)
            nc.scalar.activation(v_stat[:, 2, :], v_stat[:, 1, :], ACT.Exp, scale=-0.5).then_inc(v_stat_act, 1)
            act.wait_ge(v_stat_act, 2)
            nc.scalar.activation(v_stat[:, 3, :], v_stat[:, 2, :], ACT.Square, scale=math.sqrt(0.5 / AW)).then_inc(v_stat_act, 1)

            def uz_pair(u):
                j = 2 * u - W_UZ
                for par in range(2):
                    to_hi(*next_chunk(u, par))
                    act.wait_ge(mm_done, 4 * u + 2 * par + 1)
                    ge(act, uz_done, j + par - 1)
                    nc.scalar.activation(gelu_u[par][:, :], G[2 * par][:, :], ACT.Gelu_apprx_tanh).then_inc(gelu_done, 1)
                    act.wait_ge(mm_done, 4 * u + 2 * par + 2)
                    ge(act, uz_done, j + par)
                    nc.scalar.activation(tanh_z[:, :], G[2 * par + 1][:, :], ACT.Tanh, scale=0.5).then_inc(tanh_done, 1)
                    act.wait_ge(y_done, j + par + 1)
                    nc.scalar.activation(y_hi[:, j + par, :], mixed[par][:, :], ACT.Copy).then_inc(yhi_done, 1)

            uz_pair(W_UZ // 2)
            with act.Fori(W_UZ // 2 + 1, W_OUTA // 2) as u:
                uz_pair(u)

            act.preload_act_table_set("natural_log_exp_and_others")
            act.wait_ge(mix_freed, AT)
            act.dma_start(blocks[:, :, :], d["blocks"].rearrange("p (b n) -> p b n", n=P)).then_inc(blocks_loaded, 16)
            for m in range(KT):
                to_hi(*divmod(W_OUTA + m + 1, 2))
                square_x(1, m, 2 * (W_OUTA + m) - 14)
            rstd_start(N_X1, NB[:, :], DM)
            h_round(1, SHIFT_KV, True, range(1), hk_hi)
            to_hi(W_KV // 2, 1)
            h_round(1, SHIFT_KV, True, range(1, KT), hk_hi)

            for c in range(NKV // 2):
                u = W_KV // 2 + c
                for par in range(2):
                    if (c, par) != (0, 0):
                        to_hi(*next_chunk(u, par))
                    if par == 0:
                        for half in range(2):
                            act.wait_ge(mm_done, 4 * u + half + 1)
                            nc.scalar.activation(sq[half][:, :], G[half][:, :], ACT.Square).then_inc(qsq_ready, 1)
                    rstd_start(N_K + 2 * c + par, NB[:, :], P)
                    if c < 2:
                        h_round(2, SHIFT_B, True, (4 * c + 2 * par, 4 * c + 2 * par + 1))

            def head(n, p, mho, attend, project):
                m = n - 1
                w0 = 2 * n + W_B
                k = 3 * n + N_Q
                u0 = n + W_B // 2

                def z_start():
                    act.wait_ge(mm_done, 2 * w0)
                    act.wait_ge(acc_freed, 2 * w0 - 17)
                    nc.scalar.activation(z_t[:, :], G[1][:, :], ACT.Exp, scale=-1.0).then_inc(z_exp, 1)

                def exps(r):
                    act.wait_ge(max_done, 4 * m + r + 1)
                    nc.scalar.activation(s_b[:, :], s_b[:, :], ACT.Exp, bias=row_stat[:, 0, r:r + 1],
                                         accum_out=row_stat[:, 1, r:r + 1]).then_inc(exp_done, 1)

                def turn_copy(r):
                    act.wait_ge(turn_done, 4 * m + r + 1)
                    nc.scalar.activation(p_t[:, 0:TOK], T0[:, :], ACT.Copy).then_inc(pt_act, 1)

                def squares(mi):
                    act.wait_ge(mm_done, 2 * w0 + mi + 1)
                    act.wait_ge(sum_done, k + mi)
                    nc.scalar.activation(sq[0][:, :], G[mi % 2][:, :], ACT.Square).then_inc(qsq_ready, 1)

                if attend:
                    z_start()
                    exps(0)
                if project:
                    to_hi(u0, 1)
                    squares(0)
                if attend:
                    turn_copy(0)
                    if mho is not None:
                        out_round(n, p, mho)
                if project:
                    rstd_start(k, NB[:, :], P)
                if attend:
                    exps(1)
                if project:
                    squares(1)
                if attend:
                    turn_copy(1)
                if project:
                    rstd_start(k + 1, NB[:, :], P)
                if attend:
                    exps(2)
                if project:
                    to_hi(u0 + 1, 0)
                    squares(2)
                else:
                    to_hi(*divmod(W_OUTB + 1, 2))
                if attend:
                    turn_copy(2)
                if project:
                    rstd_start(k + 2, NB[:, :], P)
                if attend:
                    exps(3)
                    turn_copy(3)

            def out_round(n, p, mho):
                act.wait_ge(head_out, n - 1)
                nc.scalar.activation(yb_hi[:, mho + 4 * p, :], yb[:, :], ACT.Copy).then_inc(ybhi_done, 1)

            head(0, 0, None, False, True)
            head(1, 1, None, True, True)
            head(2, 0, 0, True, True)
            with act.Fori(2, QH // 2) as i:
                head(2 * i - 1, 1, i - 2, True, True)
                head(2 * i, 0, i - 1, True, True)
            head(QH - 1, 1, QH // 2 - 2, True, True)
            head(QH, 0, QH // 2 - 1, True, False)
            out_round(QH + 1, 1, QH // 2 - 1)

            for c in range(4):
                if c < 3:
                    to_hi(*divmod(W_OUTB + c + 2, 2))
                else:
                    act.wait_ge(wf_zeroed, 2)
                    act.wait_ge(small_loaded, 64)
                    nc.scalar.activation(wf_hi[:, :, 0:8], wf_raw[:, :, :], ACT.Copy).then_inc(wfhi_done, 1)
                for m in (2 * c, 2 * c + 1):
                    square_x(2, m, 2 * W_OUTB - 15 + m)
            rstd_start(N_X2, NB[:, :], DM)
            h_round(3, SHIFT_1, False, range(1))
            to_hi(*divmod(W_Q2 + 1, 2))
            h_round(3, SHIFT_1, False, range(1, KT))

            act.wait_ge(fg_done, 1)
            nc.scalar.activation(gate_abs[:, :], T0[0:8, :], ACT.Abs, bias=bf_col[:, :]).then_inc(fgate_act, 1)
            act.wait_ge(fgate_act, 1)
            nc.scalar.activation(gate_exp[:, :], gate_abs[:, :], ACT.Exp, scale=-1.0).then_inc(fgate_act, 1)
            act.preload_act_table_set("natural_log")
            act.wait_ge(fgate_act, 2)
            nc.scalar.activation(gate_ln[:, :], gate_exp[:, :], ACT.Ln, bias=ones[0:8, 0:1]).then_inc(fgate_act, 1)
            act.preload_act_table_set("natural_log_exp_and_others")

            def turn2_copy(n):
                act.wait_ge(turn2_done, n + 1)
                width = (UNITS2[n % 12][1] + 1) * P
                nc.scalar.activation(pt_2[n % 2][:, 0:width], T0[:, 0:width], ACT.Copy).then_inc(pt2_done, 1)

            def fox_round(a):
                act.wait_ge(pv2_done, 12 * a + 12)
                nc.scalar.activation(m_hi[:, a, :], AD[:, :], ACT.Copy).then_inc(mhi_done, 1)

            def diff_square(a):
                k = norm_d(a)
                act.wait_ge(pv2_done, 12 * a + 10)
                act.wait_ge(sum_done, k - 1)
                nc.scalar.activation(sq[k % 2][:, :], T1[:, :], ACT.Square).then_inc(qsq_ready, 1)

            def diff_round(a):
                act.wait_ge(d_done, a + 1)
                nc.scalar.activation(m_hi[:, 4 + a, :], d_out[:, :], ACT.Copy).then_inc(mhi_done, 1)

            def spread_copy(n):
                act.wait_ge(c_spread, n + 1)
                nc.scalar.activation(c_row[n][:, :], (T0, T1)[n % 2][:, :], ACT.Copy).then_inc(c_row_ready, 1)

            for t in range(5):
                w0 = W_Q2 + 3 * t
                a = t - 1
                attend, project = t >= 1, t < 4
                for u in range(12):
                    n = 12 * a + u
                    if t == 0 and u >= 6:
                        spread_copy(u - 6)
                    if attend and n >= 2:
                        turn2_copy(n - 2)
                    if attend:
                        kind, qb = UNITS2[u]
                        width = (qb + 1) * P
                        act.wait_ge(max2_done, n + 1)
                        for e in range(2 if kind == 2 else 1):
                            ex = nc.scalar.activation(s_2[n % 3][:, e, 0:width], s_2[n % 3][:, e, 0:width], ACT.Exp,
                                                      bias=stat2[:, 0, n % 2, e:e + 1], accum_out=stat2[:, 1, n % 2, e:e + 1])
                        ex.then_inc(exp2_done, 1)
                    if a >= 1 and u == 0:
                        diff_square(a - 1)
                    if a >= 1 and u == 2:
                        fox_round(a - 1)
                    if a >= 1 and u == 3:
                        diff_round(a - 1)
                    if t == 4 and u == 5:
                        to_hi(*divmod(W_OUT2 + 1, 2))
                    if project and u in (1, 4, 8) and (t, u) != (0, 1):
                        to_hi(*divmod(w0 + u // 4 + 1, 2))
                    if project and u in (1, 3, 5, 7):
                        k = norm2(t, u // 2)
                        act.wait_ge(mm_done, 2 * w0 + u // 2 + 1)
                        act.wait_ge(sum_done, k - 1)
                        nc.scalar.activation(sq[k % 2][:, :], G[u // 2 % 2][:, :], ACT.Square).then_inc(qsq_ready, 1)
                    if a >= 1 and u == 0:
                        rstd_start(norm_d(a - 1), NB[:, :], P)
                    if project and u in (2, 4, 6, 8):
                        rstd_start(norm2(t, u // 2 - 1), NB[:, :], 64)
                if t == 0:
                    spread_copy(6)
                    spread_copy(7)
            turn2_copy(46)
            diff_square(3)
            turn2_copy(47)
            rstd_start(norm_d(3), NB[:, :], P)
            fox_round(3)
            diff_round(3)

            for c in range(4):
                if c < 3:
                    to_hi(*divmod(W_OUT2 + c + 2, 2))
                for m in (2 * c, 2 * c + 1):
                    square_x(3, m, 2 * W_OUT2 - 15 + m)
            rstd_start(N_X3, NB[:, :], DM)
            h_round(4, SHIFT_2, False, range(1))
            to_hi(W_GU1 // 2, 1)
            h_round(4, SHIFT_2, False, range(1, KT))

            def gate_up(u, f, par, first):
                if not (isinstance(u, int) and par == 0):
                    to_hi(*next_chunk(u, par))
                act.wait_ge(mm_done, 4 * u + 2 * par + 1)
                ge(act, gulo_done, f + first - 1)
                nc.scalar.activation(tanh_g[par][:, :], G[2 * par][:, :], ACT.Tanh, scale=0.5).then_inc(tanhg_done, 1)
                act.wait_ge(acc_freed, 4 * u + 2 * par - 14)
                nc.scalar.activation(gu_hi[:, f, :], gu[par][:, :], ACT.Copy).then_inc(guhi_done, 1)

            for par in range(2):
                gate_up(W_GU1 // 2, par, par, 0)
            with act.Fori(W_GU1 // 2 + 1, W_DN1 // 2) as u:
                for par in range(2):
                    gate_up(u, 2 * (u - W_GU1 // 2) + par, par, 0)
            with act.Fori(W_DN1 // 2, W_GU2 // 2) as u:
                for par in range(2):
                    to_hi(*next_chunk(u, par))
            with act.Fori(W_GU2 // 2, W_DN2 // 2) as u:
                for par in range(2):
                    gate_up(u, 2 * (u - W_GU2 // 2) + par, par, FF1)

            for w in range(W_DN2 + 1, W_END):
                to_hi(*divmod(w, 2), FF2 * 256)

        @block.vector
        def _(dve):
            def f32(tile):
                return tile.bitcast(F32)

            def stt(out, in0, scalar, in1, op0, op1, **more):
                return nc.vector.scalar_tensor_tensor(out, in0, scalar, in1, op0, op1, **more)

            def to_lo(u, par, used=2048):
                dve.wait_ge(hi_done, 2 * u + par + 1)
                ge(dve, lo_done, 2 * u + par)
                nc.vector.tensor_tensor(w_lo[par][:, 0:used], w_raw[par][:, 0:used], f32(w_hi[par][:, 0:used]), ALU.subtract)\
                    .then_inc(lo_done, 1)

            def ada_step(done, first, raw, cond, acc=ada_acc):
                nc.vector.tensor_scalar(acc[:, :], raw[:, 0, :], silu_c[:, cond:cond + 1], None, ALU.mult).then_inc(done, 1)
                for kt in range(1, KT):
                    dve.wait_ge(done, first + kt)
                    stt(acc[:, :], raw[:, kt, :], silu_c[:, cond + kt:cond + kt + 1], acc[:, :], ALU.mult, ALU.add)\
                        .then_inc(done, 1)

            def ada_end(r, columns=AD[:, 0:2]):
                dve.wait_ge(ada_mm_done, r + 1)
                nc.vector.tensor_tensor(mods[:, bass.ds(2 * (r + UP), 2)], columns, mod_bias[:, bass.ds(2 * (r + UP), 2)], ALU.add)\
                    .then_inc(ada_out, 1)

            def ada(r, cond, columns=AD[:, 0:2]):
                if not (isinstance(r, int) and r == 0):
                    ada_end(r - 1, columns)
                dve.wait_ge(ada_loaded, 16 * (r + 1))
                ada_step(ada_sum, 8 * r, ada_raw, cond)

            def gain(e, scale, g, have):
                if have > 0:
                    dve.wait_ge(ada_out, have)
                ge(dve, hx_done, 8 * e)
                stt(gscale[:, :], mods[:, scale:scale + 8], 1.0, vecs[:, g:g + 8], ALU.add, ALU.mult).then_inc(gs_done, 1)
                dve.wait_ge(gs_done, e + 1)

            def rstd_end(k, total, count, rstd=rstd):
                dve.wait_ge(half_done, k + 1)
                stt(y0_half[:, :], total, count * EPS, y0_half[:, :], ALU.add, ALU.mult).then_inc(newton_done, 1)
                dve.wait_ge(newton_done, k + 1)
                stt(rstd[:, :], y0_half[:, :], 1.5, y0[:, :], ALU.subtract, ALU.mult, reverse0=True).then_inc(rstd_done, 1)
                dve.wait_ge(rstd_done, k + 1)

            def h_scale(e, kt):
                ge(dve, hlo_done, 8 * e + kt - 1)
                stt(hx[kt % 2][:, :], x[:, kt, :], gscale[:, kt:kt + 1], x_rstd[:, :], ALU.mult, ALU.mult).then_inc(hx_done, 1)

            def x_norm(k, e, first):
                dve.wait_ge(y0_done, k + 1)
                dve.wait_ge(hlo_done, 8 * e - 1)
                stt(hx[0][:, :], x[:, 0, :], gscale[:, 0:1], y0[:, :], ALU.mult, ALU.mult).then_inc(hx_start, 1)
                dve.wait_ge(half_done, k + 1)
                stt(y0_half[:, :], NB[:, :], DM * EPS, y0_half[:, :], ALU.add, ALU.mult).then_inc(newton_done, 1)
                dve.wait_ge(newton_done, k + 1)
                dve.wait_ge(hx_start, first + 1)
                stt(hx[0][:, :], y0_half[:, :], 1.5, hx[0][:, :], ALU.subtract, ALU.mult, reverse0=True).then_inc(hx_done, 1)
                stt(x_rstd[:, :], y0_half[:, :], 1.5, y0[:, :], ALU.subtract, ALU.mult, reverse0=True).then_inc(rstd_done, 1)
                dve.wait_ge(rstd_done, k + 1)

            def h_rest(e, kt, shift, dilate, h=(h_hi, h_lo)):
                dve.wait_ge(hhi_done, 8 * e + kt + 1)
                src, hi, lo = hx[kt % 2][:, :], f32(h[0][:, kt, :]), h[1][:, kt, :]
                if dilate:
                    src, hi, lo = dilated(src), four(hi), four(lo)
                stt(lo, src, mods[:, shift + kt:shift + kt + 1], hi, ALU.add, ALU.subtract).then_inc(hlo_done, 1)

            def h_split(e, shift, dilate, h=(h_hi, h_lo)):
                if e == 0:
                    h_scale(e, 0)
                h_rest(e, 0, shift, dilate, h)
                h_scale(e, 1)
                for kt in range(1, KT):
                    if kt + 1 < KT:
                        h_scale(e, kt + 1)
                    h_rest(e, kt, shift, dilate, h)

            def update_x(m, acc, gate, mm, n, dilate=False):
                dve.wait_ge(mm_done, mm)
                xm = dilated(x[:, m, :]) if dilate else x[:, m, :]
                stt(xm, four(acc) if dilate else acc, mods[:, bass.ds(m + gate, 1)], xm, ALU.mult, ALU.add).then_inc(acc_freed, n)

            dve.wait_ge(vecs_loaded, 16)
            dve.wait_ge(silu_ready, 1)
            for i, s in enumerate(UP_VECTOR):
                dve.wait_ge(ada_up_loaded[s], 16)
                ge(dve, up_summed, i - 1)
                ada_step(up_sum, 8 * i, ada_up[s], 0, up_acc[i % 2])
                if i == 0:
                    nc.vector.tensor_scalar(gains[:, 0:1], vecs[:, G_QB:G_QB + 1], P ** -0.5, None, ALU.mult)
                    nc.vector.tensor_scalar(gains[:, 1:2], vecs[:, G_FQ:G_FQ + 1], 0.125, None, ALU.mult)
                    nc.vector.tensor_copy(gains[:, 2:3], vecs[:, G_FK:G_FK + 1])
                    nc.vector.tensor_scalar(gains[:, 3:4], vecs[:, G_DQ:G_DQ + 1], 0.125, None, ALU.mult)
                    nc.vector.tensor_copy(gains[:, 4:5], vecs[:, G_DK:G_DK + 1])
                    nc.vector.tensor_scalar(gains[:, 5:6], vecs[:, G_DN:G_DN + 1], 1.0 - LAM_INIT, None, ALU.mult).then_inc(gains_ready, 1)
                    dve.wait_ge(ws_loaded, 16)
                    dve.wait_ge(consts_loaded, 16)
                    tri = consts[:, K_TRI:K_TRI + P].unsqueeze(1).broadcast_to([P, GROUPS, P])
                    nc.vector.tensor_tensor(ws_t[:, :, :], ws_raw[:, :, :], tri, ALU.mult).then_inc(ws_ready, 1)
                    dve.wait_ge(small_loaded, 64)
                    for n in range(2):
                        stt(lam_prod[:, 64 * n:64 * n + 64], lam_rows[:, 128 * n:128 * n + 64], 1.0,
                            lam_rows[:, 128 * n + 64:128 * n + 128], ALU.mult, ALU.mult, accum_out=lam_two[:, n:n + 1]).then_inc(lam_part, 1)
            rstd_end(N_X0, NB[:, :], DM, x_rstd)
            dve.wait_ge(lam_exp, 1)
            stt(neg_lam[:, :], lam_two[:, 1:2], -LAM_INIT, lam_two[:, 0:1], ALU.add, ALU.subtract).then_inc(lam_ready, 1)
            to_lo(0, 0)
            dve.wait_ge(up_summed, len(UP_VECTOR))
            dve.wait_ge(up_done, len(UP_TENSOR))
            nc.vector.tensor_tensor(mods[:, 0:2 * UP], AD[:, 0:2 * UP], mod_bias[:, 0:2 * UP], ALU.add).then_inc(up_out, 1)
            dve.wait_ge(up_out, 1)
            gain(0, SCALE_A, G_A, 0)
            h_split(0, SHIFT_A, False)

            def v_pair(u):
                n = 2 * u - W_V
                for par in range(2):
                    if not (isinstance(u, int) and par == 0):
                        to_lo(*next_chunk(u, par))
                    ada(n + par, 0)
                    dve.wait_ge(v_gelu_done, 4 * u + 2 * par + 2)
                    ge(dve, v_sums_done, n + par)
                    for t in range(TB):
                        vt = v[:, t, bass.ds(256 * n + 256 * par, 256)]
                        last = stt(v_sq[:, t, :], vt, 1.0, vt, ALU.mult, ALU.mult, accum_out=v_sums[:, t, bass.ds(n + par, 1)])
                    last.then_inc(v_sums_done, 1)

            v_pair(0)
            with dve.Fori(1, W_UZ // 2) as u:
                v_pair(u)
            dve.wait_ge(v_sums_done, GROUPS)
            nc.vector.tensor_reduce(v_stat[:, 0, :], v_sums[:, :, :], AX, ALU.add).then_inc(v_stat_dve, 1)
            dve.wait_ge(v_stat_act, 3)
            dve.wait_ge(v_stat_dve, 1)
            stt(v_stat[:, 4, :], v_stat[:, 0, :], AW * EPS, v_stat[:, 3, :], ALU.add, ALU.mult).then_inc(v_stat_dve, 1)
            dve.wait_ge(v_stat_dve, 2)
            stt(v_stat[:, 5, :], v_stat[:, 4, :], 1.5, v_stat[:, 2, :], ALU.subtract, ALU.mult, reverse0=True).then_inc(v_stat_dve, 1)

            def uz_pair(u):
                jj = 2 * u - W_UZ
                g = u - W_UZ // 2
                for par in range(2):
                    j = jj + par
                    to_lo(*next_chunk(u, par))
                    ada(j + W_UZ, 0)
                    dve.wait_ge(gelu_done, j + 1)
                    dve.wait_ge(tanh_done, j + 1)
                    stt(tanh_z[:, :], tanh_z[:, :], 1.0, G[2 * par + 1][:, :], ALU.add, ALU.mult).then_inc(acc_freed, 2)
                    dve.wait_ge(acc_freed, 2 * j + 2)
                    stt(gelu_u[par][:, :], tanh_z[:, :], 0.5, gelu_u[par][:, :], ALU.mult, ALU.mult).then_inc(uz_done, 1)
                    dve.wait_ge(mix_done, j + 1)
                    mix = mixed[par][:, :].rearrange("p (c t) -> p c t", c=TB)
                    stt(mix, (T0, T1)[par][:, :].rearrange("p (c t) -> p c t", c=TB), vecs[:, bass.ds(j + G_SGU, 1)],
                        b_sp[:, bass.ds(g, 1), :].broadcast_to([P, TB, P]), ALU.mult, ALU.add).then_inc(mix_freed, 1)
                    dve.wait_ge(mix_freed, j + 1)
                    dve.wait_ge(uz_done, j + 1)
                    nc.vector.tensor_tensor(mixed[par][:, :], mixed[par][:, :], gelu_u[par][:, :], ALU.mult).then_inc(y_done, 1)
                    dve.wait_ge(yhi_done, j + 1)
                    nc.vector.tensor_tensor(y_lo[:, :, bass.ds(j * P, P)], mix,
                                            f32(y_hi[:, j, :]).rearrange("p (c t) -> p c t", c=TB),
                                            ALU.subtract).then_inc(ylo_done, 1)

            dve.wait_ge(small_loaded, 64)
            uz_pair(W_UZ // 2)
            with dve.Fori(W_UZ // 2 + 1, W_OUTA // 2) as u:
                uz_pair(u)

            with dve.Fori(W_OUTA // 2, W_KV // 2) as u:
                for par in range(2):
                    m = 2 * u - W_OUTA + par
                    to_lo(*next_chunk(u, par))
                    ada(m + W_OUTA, 8)
                    dve.wait_ge(ada_out, m + W_OUTA)
                    update_x(m, G[2 * par][:, :], GATE_A, 4 * u + 2 * par + 2, 2)
            gain(1, SCALE_KV, G_KV, 8)
            x_norm(N_X1, 1, 0)
            h_split(1, SHIFT_KV, True, (hk_hi, hk_lo))

            gain(2, SCALE_B, G_B, 20)
            for c in range(NKV // 2):
                u = W_KV // 2 + c
                for par in range(2):
                    tiles = (4 * c + 2 * par, 4 * c + 2 * par + 1) if c < 2 else ()
                    if (c, par) != (0, 0):
                        to_lo(*next_chunk(u, par))
                    for kt in tiles:
                        h_scale(2, kt)
                    ada(2 * u + par, 8)
                    rstd_end(N_K + 2 * c + par, NB[:, :], P)
                    stt(k_t[:, 2 * c + par, :], G[par][:, :], vecs[:, G_K:G_K + 1], rstd[:, :], ALU.mult, ALU.mult).then_inc(acc_freed, 1)
                    for kt in tiles:
                        h_rest(2, kt, SHIFT_B, True)
                for half in range(2):
                    dve.wait_ge(mm_done, 4 * u + 3 + half)
                    nc.vector.tensor_copy(v_b[:, 2 * half:2 * half + 2, 256 * c:256 * c + 256],
                                          G[2 + half][:, :].rearrange("p (t n) -> p t n", t=2)).then_inc(acc_freed, 1)

            dve.wait_ge(gains_ready, 1)
            dve.wait_ge(blocks_loaded, 16)

            def head_output(n, p):
                dve.wait_ge(pv_done, 4 * (n - 1))
                nc.vector.tensor_tensor(yb[:, :], z_b[p][:, :], AD[:, :], ALU.mult).then_inc(head_out, 1)

            def head_rest(n, p, mho):
                dve.wait_ge(ybhi_done, n - 1)
                nc.vector.tensor_tensor(yb_lo[:, mho + 4 * p, :], yb[:, :], f32(yb_hi[:, mho + 4 * p, :]), ALU.subtract).then_inc(yblo_done, 1)

            def head(n, p, mh, mho, attend, project):
                m, q = n - 1, 1 - p
                k = 3 * n + N_Q

                def slope(g):
                    return consts[:, bass.ds(mh + (K_SLOPE + 8 * g + 4 * q), 1)]

                def z_bound():
                    dve.wait_ge(z_exp, n)
                    nc.vector.tensor_scalar(z_t[:, :], z_t[:, :], FAR, 1.0, ALU.min, ALU.add).then_inc(z_part, 1)

                def z_divide(part, parts):
                    dve.wait_ge(z_part, 2 * n - 1)
                    s = slice(TOK // parts * part, TOK // parts * (part + 1))
                    nc.vector.reciprocal(z_t[:, s], z_t[:, s]).then_inc(z_part, 1)

                def z_gate(parts):
                    dve.wait_ge(z_part, 2 * n - 1 + parts)
                    nc.vector.tensor_tensor(z_b[q][:, :], z_t[:, :], G[1][:, :], ALU.mult).then_inc(acc_freed, 1)

                def logits(r):
                    dve.wait_ge(qk_done, 4 * m + r + 1)
                    stt(s_b[:, 0:TOK], blocks[:, 3 - r:7 - r, :].rearrange("p b n -> p (b n)"), slope(0), G[2][:, :], ALU.mult, ALU.add)
                    for g in (1, 2):
                        last = stt(s_b[:, TOK + P * (g - 1):TOK + P * g], blocks[:, 6 + g, :], slope(g), G[3][:, P * (g - 1):P * g],
                                   ALU.mult, ALU.add)
                    last.then_inc(s_freed, 1)
                    dve.wait_ge(s_freed, 4 * m + r + 1)
                    nc.vector.tensor_reduce(row_stat[:, 0, r:r + 1], s_b[:, :], AX, ALU.max, negate=True).then_inc(max_done, 1)

                def weights(r):
                    dve.wait_ge(exp_done, 4 * m + r + 1)
                    nc.vector.reciprocal(row_stat[:, 2, r:r + 1], row_stat[:, 1, r:r + 1]).then_inc(inv_done, 1)
                    dve.wait_ge(inv_done, 4 * m + r + 1)
                    nc.vector.tensor_scalar(s_b[:, :], s_b[:, :], row_stat[:, 2, r:r + 1], None, ALU.mult).then_inc(p_ready, 1)

                def turn_copy(r):
                    dve.wait_ge(turn_done, 4 * m + r + 1)
                    nc.vector.tensor_copy(p_t[:, TOK:768], T1[:, 0:256]).then_inc(pt_dve, 1)

                def q_norm(mi):
                    rstd_end(k + mi, NB[:, :], P)
                    stt(q_n[p][mi][:, :], G[mi % 2][:, :], gains[:, 0:1], rstd[:, :], ALU.mult, ALU.mult).then_inc(acc_freed, 1)

                if attend:
                    logits(0)
                    z_bound()
                    if project:
                        weights(0)
                        z_divide(0, 1)
                        z_gate(1)
                        if mho is not None:
                            head_output(n, p)
                            head_rest(n, p, mho)
                    else:
                        z_divide(0, 2)
                        weights(0)
                        head_output(n, p)
                for r in range(4):
                    if attend:
                        turn_copy(r)
                        if r < 3:
                            logits(r + 1)
                        if r == 0 and not project:
                            head_rest(n, p, mho)
                    if project and r < 3:
                        q_norm(r)
                    if attend and r < 3:
                        weights(r + 1)
                    if r == 0 and not project:
                        z_divide(1, 2)
                        z_gate(2)
                    if project and r == 1:
                        ada(n + S_B, 8, T1[:, 256:258])

            head(0, 0, None, None, False, True)
            head(1, 1, 0, None, True, True)
            head(2, 0, 0, 0, True, True)
            with dve.Fori(2, QH // 2) as i:
                head(2 * i - 1, 1, i - 1, i - 2, True, True)
                head(2 * i, 0, i - 1, i - 1, True, True)
            head(QH - 1, 1, QH // 2 - 1, QH // 2 - 2, True, True)
            head(QH, 0, QH // 2 - 1, QH // 2 - 1, True, False)
            head_output(QH + 1, 1)
            head_rest(QH + 1, 1, QH // 2 - 1)

            for c in range(4):
                w = W_OUTB + c
                if c == 3:
                    dve.wait_ge(wfhi_done, 1)
                    nc.vector.tensor_tensor(wf_lo[:, :, 0:8], wf_raw[:, :, :], f32(wf_hi[:, :, 0:8]), ALU.subtract).then_inc(wflo_done, 1)
                for half in range(2):
                    update_x(2 * c + half, G[2 * (w % 2) + half][:, :], GATE_B, 2 * w + half + 1, 1, True)
                if c < 3:
                    to_lo(*divmod(w + 2, 2))
                if c % 2 == 0:
                    ada(S_OUTB + c // 2, 8)
            gain(3, SCALE_1, G_LN1, 32)
            x_norm(N_X2, 3, 1)
            h_split(3, SHIFT_1, False)
            ada_end(S_END - 1)

            nc.vector.memset(gate_one[:, :], 1.0).then_inc(fgate_dve, 1)
            dve.wait_ge(fgate_act, 1)
            nc.vector.tensor_scalar(gate_min[:, :], T0[0:8, :], bf_col[:, :], 0.0, ALU.add, ALU.min).then_inc(fgate_dve, 1)
            dve.wait_ge(fgate_act, 3)
            dve.wait_ge(fgate_dve, 2)
            nc.vector.tensor_tensor(gate_log[:, :], gate_min[:, :], gate_ln[:, :], ALU.subtract).then_inc(fgate_dve, 1)
            dve.wait_ge(fgate_dve, 3)
            nc.vector.tensor_tensor_scan(cum[:, :], gate_one[:, :], gate_log[:, :], 0.0, ALU.mult, ALU.add).then_inc(fgate_dve, 1)

            def fox_rest(a):
                dve.wait_ge(mhi_done, 2 * a + 1)
                nc.vector.tensor_tensor(m_lo[:, a, :], AD[:, :], f32(m_hi[:, a, :]), ALU.subtract).then_inc(mlo_done, 1)

            def diff_norm(a):
                rstd_end(norm_d(a), NB[:, :], P)
                stt(d_out[:, :], T1[:, :], gains[:, 5:6], rstd[:, :], ALU.mult, ALU.mult).then_inc(d_done, 1)

            def diff_rest(a):
                dve.wait_ge(mhi_done, 2 * a + 2)
                nc.vector.tensor_tensor(m_lo[:, 4 + a, :], d_out[:, :], f32(m_hi[:, 4 + a, :]), ALU.subtract).then_inc(mlo_done, 1)

            def logits2(n):
                a, u = divmod(n, 12)
                kind, qb = UNITS2[u]
                width = (qb + 1) * P
                before, first = s_reads(u)
                sets = 2 if kind == 2 else 1
                dve.wait_ge(qk2_done, n + 1)
                for e in range(sets):
                    s, score = s_2[n % 3][:, e, 0:width], G[2 + (first + e) % 2][:, 0:width]
                    if kind == 2:
                        biased = stt(s, consts[:, K_DIST + TOK - width:K_DIST + TOK], -SLOPES_D[a], score, ALU.mult, ALU.add)
                    else:
                        biased = stt(s, score, c_col[:, qb, 2 * a + kind:2 * a + kind + 1], c_row[2 * a + kind][:, 0:width],
                                     ALU.add, ALU.subtract)
                    biased.then_inc(s2_freed, 1)
                dve.wait_ge(s2_freed, 16 * a + before + sets)
                if kind < 2:
                    s = s_2[n % 3][:, 0, width - P:width]
                    nc.vector.tensor_tensor(s, s, consts[:, K_MASK:K_MASK + P], ALU.add).then_inc(bias2_done, 1)
                    dve.wait_ge(bias2_done, 8 * a + sum(1 for e in UNITS2[:u + 1] if e[0] < 2))
                nc.vector.tensor_reduce(stat2[:, 0, n % 2, 0:sets], s_2[n % 3][:, 0:sets, 0:width], AX, ALU.max, negate=True)\
                    .then_inc(max2_done, 1)

            def weights2(n):
                a, u = divmod(n, 12)
                kind, qb = UNITS2[u]
                width = (qb + 1) * P
                sets = 2 if kind == 2 else 1
                dve.wait_ge(exp2_done, n + 1)
                i0 = 20 * a + u + sum(2 for e in UNITS2[:u] if e[0] == 2)
                nc.vector.reciprocal(stat2[:, 2, n % 2, 0:sets], stat2[:, 1, n % 2, 0:sets]).then_inc(inv2_done, 1)
                dve.wait_ge(inv2_done, i0 + 1)
                p1 = s_2[n % 3][:, 0, 0:width]
                if kind < 2:
                    nc.vector.tensor_scalar(p1, p1, stat2[:, 2, n % 2, 0:1], None, ALU.mult).then_inc(p2_ready, 1)
                else:
                    nc.vector.tensor_scalar(p1, p1, stat2[:, 2, n % 2, 0:1], None, ALU.mult).then_inc(inv2_done, 1)
                    nc.vector.tensor_tensor(lam_inv[:, 0:1], stat2[:, 2, n % 2, 1:2], neg_lam[:, :], ALU.mult).then_inc(inv2_done, 1)
                    dve.wait_ge(inv2_done, i0 + 3)
                    stt(p1, s_2[n % 3][:, 1, 0:width], lam_inv[:, 0:1], p1, ALU.mult, ALU.add).then_inc(p2_ready, 1)

            for t in range(5):
                w0 = W_Q2 + 3 * t
                a = t - 1
                attend, project = t >= 1, t < 4
                for u in range(13):
                    n = 12 * a + u
                    if attend and u < 12:
                        logits2(n)
                    if attend and n >= 1 and u < 12:
                        weights2(n - 1)
                    if t == 0 and u == 4:
                        dve.wait_ge(c_turned, 1)
                        nc.vector.tensor_copy(c_col[:, :, :], T1[:, 0:32].rearrange("p (t h) -> p t h", t=TB)).then_inc(c_col_ready, 1)
                    if a >= 1 and u == 1:
                        diff_norm(a - 1)
                    if a >= 1 and u == 3:
                        fox_rest(a - 1)
                    if a >= 1 and u == 4:
                        diff_rest(a - 1)
                    if project and u in (3, 5, 7, 9):
                        mi = u // 2 - 1
                        rstd_end(norm2(t, mi), NB[:, :], 64)
                        stt(qk[t % 2][mi][:, :], G[mi % 2][:, :], gains[:, 1 + mi:2 + mi], rstd[:, :], ALU.mult, ALU.mult).then_inc(acc_freed, 1)
                    if project and u in (10, 12):
                        half = u // 2 - 5
                        dve.wait_ge(mm_done, 2 * w0 + half + 5)
                        nc.vector.tensor_copy(v_2[t % 2][:, 2 * half:2 * half + 2, :], G[half][:, :].rearrange("p (t n) -> p t n", t=2))\
                            .then_inc(acc_freed, 1)
                if t == 0:
                    dve.wait_ge(c_col_ready, 1)
                    dve.wait_ge(c_row_ready, GROUPS)
            weights2(47)
            diff_norm(3)
            fox_rest(3)
            diff_rest(3)

            for c in range(4):
                w = W_OUT2 + c
                for half in range(2):
                    update_x(2 * c + half, G[2 * (w % 2) + half][:, :], GATE_1, 2 * w + half + 1, 1)
                if c < 3:
                    to_lo(*divmod(w + 2, 2))
            gain(4, SCALE_2, G_LN2, S_END)
            x_norm(N_X3, 4, 2)
            h_split(4, SHIFT_2, False)

            def gate_up(u, f, par, first):
                if not (isinstance(u, int) and par == 0):
                    to_lo(*next_chunk(u, par))
                dve.wait_ge(tanhg_done, f + first + 1)
                stt(tanh_g[par][:, :], tanh_g[par][:, :], 1.0, G[2 * par][:, :], ALU.add, ALU.mult).then_inc(acc_freed, 1)
                dve.wait_ge(mm_done, 4 * u + 2 * par + 2)
                dve.wait_ge(acc_freed, 4 * u + 2 * par - 15)
                stt(gu[par][:, :], tanh_g[par][:, :], 0.5, G[2 * par + 1][:, :], ALU.mult, ALU.mult).then_inc(acc_freed, 1)
                dve.wait_ge(guhi_done, f + first + 1)
                nc.vector.tensor_tensor(gu_lo[:, f, :], gu[par][:, :], f32(gu_hi[:, f, :]), ALU.subtract).then_inc(gulo_done, 1)

            for par in range(2):
                gate_up(W_GU1 // 2, par, par, 0)
            with dve.Fori(W_GU1 // 2 + 1, W_DN1 // 2) as u:
                for par in range(2):
                    gate_up(u, 2 * (u - W_GU1 // 2) + par, par, 0)
            with dve.Fori(W_DN1 // 2, W_GU2 // 2) as u:
                for par in range(2):
                    to_lo(*next_chunk(u, par))
                    update_x(2 * (u - W_DN1 // 2) + par, G[2 * par][:, :], GATE_2, 4 * u + 2 * par + 2, 2)
            with dve.Fori(W_GU2 // 2, W_DN2 // 2) as u:
                for par in range(2):
                    gate_up(u, 2 * (u - W_GU2 // 2) + par, par, FF1)
            for c in range(4):
                w = W_DN2 + c
                if c < 3:
                    to_lo(*divmod(w + 1, 2), FF2 * 256)
                for half in range(2):
                    update_x(2 * c + half, G[2 * (w % 2) + half][:, :], GATE_2, 2 * w + half + 1, 1)

        @block.tensor
        def _(pe):
            def mm(out, lhsT, rhs, start, stop):
                return nc.tensor.matmul(out, lhsT, rhs, start=start, stop=stop)

            def split(out, parts, n, pieces):
                for kt in pieces:
                    a_hi, a_lo, b_hi, b_lo = parts(kt)
                    mm(out, a_hi, b_hi, kt == 0, False)
                    mm(out, a_hi, b_lo, False, False)
                    last = mm(out, a_lo, b_hi, False, kt == n - 1)
                return last

            def columns(out, par, half, kts, hi, lo_kt, pieces=None):
                n = 256 if kts <= KT else P
                wh = w_hi[par][:, 0:kts * n].rearrange("p (k n) -> p k n", k=kts)
                wl = w_lo[par][:, 0:kts * n].rearrange("p (k n) -> p k n", k=kts)
                for kt in pieces or range(kts):
                    a_hi, a_lo = wh[:, kt, P * half:P * half + P], wl[:, kt, P * half:P * half + P]
                    mm(out, a_hi, hi[:, kt, :], kt == 0, False)
                    mm(out, a_hi, lo_kt(kt), False, False)
                    last = mm(out, a_lo, hi[:, kt, :], False, kt == kts - 1)
                return last

            def h_lo_of(kt):
                return h_lo[:, kt, :]

            def rows(out, par, t, lo, n, pieces=range(KT), h=(h_hi, h_lo)):
                wh = w_hi[par][:, :].rearrange("p (k n) -> p k n", k=KT)
                wl = w_lo[par][:, :].rearrange("p (k n) -> p k n", k=KT)
                s = slice(P * t, P * t + P)
                return split(out, lambda kt: (h[0][:, kt, s], h[1][:, kt, s], wh[:, kt, lo:lo + n], wl[:, kt, lo:lo + n]), KT, pieces)

            def chunk_ready(u, par):
                pe.wait_ge(lo_done, 2 * u + par + 1)

            def ada_sum_up(r, columns=AD[:, 0:2]):
                pe.wait_ge(ada_sum, 8 * r + 8)
                ge(pe, ada_out, r)
                mm(columns[:, 0:1], ada_acc[:, 0:P], ones[:, 0:1], True, True)
                mm(columns[:, 1:2], ada_acc[:, P:2 * P], ones[:, 0:1], True, True).then_inc(ada_mm_done, 1)

            def h_ready(e, kt):
                pe.wait_ge(hlo_done, 8 * e + kt + 1)

            def first_chunk(e, w, outs, hi, lo_kt, freed):
                chunk_ready(*divmod(w, 2))
                for half in range(2):
                    pe.wait_ge(acc_freed, freed + half)
                for kt in range(KT):
                    h_ready(e, kt)
                    for half in range(2):
                        last = columns(outs[half][:, :], w % 2, half, KT, hi, lo_kt, (kt,))
                        if kt == KT - 1:
                            last.then_inc(mm_done, 1)

            def add_squares(k, norm):
                pe.wait_ge(sq_added, 6 * k + 6)
                pe.wait_ge(newton_done, norm)
                mm(NB[:, :], ones, sq_sum[:, :], True, False)
                pe.wait_ge(sq_ready, 8 * k + 8)
                mm(NB[:, :], ones, sq[1][:, :], False, True).then_inc(sum_done, 1)

            pe.wait_ge(silu_ready, 1)
            def column_pair(s, weights_of, vector_of, kts):
                for c in (2 * s, 2 * s + 1):
                    for kt in range(kts):
                        last = mm(AD[:, c:c + 1], weights_of(kt)[:, P * (c % 2):P * (c % 2) + P], vector_of(kt), kt == 0, kt == kts - 1)
                return last

            def up_step(s):
                pe.wait_ge(ada_up_loaded[s], 16)
                column_pair(s, lambda kt: ada_up[s][:, kt, :], lambda kt: silu_c[:, kt:kt + 1], KT).then_inc(up_done, 1)

            def up_sum_up(i):
                pe.wait_ge(up_sum, 8 * i + 8)
                column_pair(UP_VECTOR[i], lambda kt: up_acc[i % 2], lambda kt: ones[:, 0:1], 1).then_inc(up_summed, 1)

            up_step(UP_TENSOR[0])
            pe.wait_ge(consts_loaded, 16)
            up_sum_up(0)
            up_step(UP_TENSOR[1])
            up_step(UP_TENSOR[2])
            pe.wait_ge(sq_added, KT - 2)
            mm(NB[:, :], ones, sq_first[0][:, :], True, False)
            pe.wait_ge(sq_ready, KT)
            mm(NB[:, :], ones, sq_first[KT - 1][:, :], False, True).then_inc(sum_done, 1)
            up_sum_up(1)
            up_sum_up(2)
            up_step(UP_TENSOR[3])
            up_sum_up(3)

            def v_pair(u):
                n = 2 * u - W_V
                for par in range(2):
                    chunk_ready(u, par)
                    for hb in range(2):
                        ge(pe, v_gelu_done, 4 * u + 2 * par + hb - 3)
                        for t in range(2):
                            last = rows(G[2 * par + hb][:, 256 * t:256 * t + 256], par, 2 * hb + t, 0, 256)
                        last.then_inc(mm_done, 1)
                        if hb == 0:
                            ada_sum_up(n + par - 1)

            chunk_ready(0, 0)
            for kt in range(KT):
                h_ready(0, kt)
                for t in range(TB):
                    last = rows(FIRST_V[t][:, 0:256], 0, t, 0, 256, (kt,))
                    if kt == KT - 1 and t % 2 == 1:
                        last.then_inc(mm_done, 1)
            chunk_ready(0, 1)
            for hb in range(2):
                for t in range(2):
                    last = rows(G[2 + hb][:, 256 * t:256 * t + 256], 1, 2 * hb + t, 0, 256)
                last.then_inc(mm_done, 1)
                if hb == 0:
                    ada_sum_up(0)
            with pe.Fori(1, W_UZ // 2) as u:
                v_pair(u)

            def uz_pair(u):
                jj = 2 * u - W_UZ
                for par in range(2):
                    j = jj + par
                    chunk_ready(u, par)
                    if isinstance(u, int):
                        pe.wait_ge(v_gelu_done, 2 * (W_UZ - 2 + par) + 2)
                    else:
                        pe.wait_ge(acc_freed, 2 * j - 2)
                    for half in range(2):
                        columns(G[2 * par + half][:, :], par, half, KT, h_hi, h_lo_of).then_inc(mm_done, 1)
                        if half == 0:
                            ada_sum_up(j + W_UZ - 1)
                    pe.wait_ge(v_staged, j + 1)
                    ge(pe, mix_freed, j - 1)
                    for c in range(TB):
                        mixed_c = mm((T0, T1)[par][:, P * c:P * c + P], v_stage[par][:, c, :], ws_t[:, u - W_UZ // 2, :], True, True)
                    mixed_c.then_inc(mix_done, 1)

            pe.wait_ge(ws_ready, 1)
            uz_pair(W_UZ // 2)
            with pe.Fori(W_UZ // 2 + 1, W_OUTA // 2) as u:
                uz_pair(u)

            def out_a(u, first=False):
                for par in range(2):
                    m = 2 * u - W_OUTA + par
                    chunk_ready(u, par)
                    pe.wait_ge(acc_freed, 4 * u + 2 * par - 18)
                    for piece in (range(KT), range(KT, AT - 2), range(AT - 2, AT)):
                        if first and par == 0:
                            pe.wait_ge(ylo_done, piece[-1] + 1)
                        last = columns(G[2 * par][:, :], par, 0, AT, y_hi, lambda kt: y_lo[:, :, P * kt:P * kt + P], piece)
                        if piece[0] == 0:
                            ada_sum_up(m + W_OUTA - 1)
                    last.then_inc(mm_done, 2)

            out_a(W_OUTA // 2, True)
            with pe.Fori(W_OUTA // 2 + 1, W_KV // 2) as u:
                out_a(u)
            add_squares(1, N_X1)

            def hk_lo_of(kt):
                return hk_lo[:, kt, :]

            def k_squares(c, half):
                pe.wait_ge(qsq_ready, 2 * c + half + 1)
                pe.wait_ge(newton_done, N_K + 2 * c + half)
                mm(NB[:, :], ones, sq[half][:, :], True, True).then_inc(sum_done, 1)

            for c in range(NKV // 2):
                w = W_KV + 2 * c
                if c == 0:
                    first_chunk(1, w, G, hk_hi, hk_lo_of, 2 * w - 19)
                    ada_sum_up(w - 1)
                else:
                    chunk_ready(w // 2, 0)
                    for half in range(2):
                        pe.wait_ge(acc_freed, 2 * w + half - 19)
                        columns(G[half][:, :], 0, half, KT, hk_hi, hk_lo_of).then_inc(mm_done, 1)
                        if half == 0:
                            ada_sum_up(w - 1)
                k_squares(c, 0)
                chunk_ready(w // 2, 1)
                for half in range(2):
                    if c > 0:
                        pe.wait_ge(acc_freed, 2 * w + half - 17)
                    for t in range(2):
                        last = rows(G[2 + half][:, 256 * t:256 * t + 256], 1, 2 * half + t, 0, 256, h=(hk_hi, hk_lo))
                    last.then_inc(mm_done, 1)
                    if half == 0:
                        k_squares(c, 1)
                        ada_sum_up(w)

            for kt in range(KT):
                h_ready(2, kt)

            def head(n, p, attend, project, prior):
                m, q = n - 1, 1 - p
                u0 = n + W_B // 2
                w0 = 2 * n + W_B
                k = 3 * n + N_Q

                def piece(mi):
                    if mi % 2 == 0:
                        chunk_ready(u0, mi // 2)
                    pe.wait_ge(acc_freed, 2 * w0 + mi - 17)
                    columns(G[mi % 2][:, :], mi // 2, mi % 2, KT, h_hi, h_lo_of).then_inc(mm_done, 1)

                def squares(mi):
                    pe.wait_ge(qsq_ready, k + mi - N_Q + NKV + 1)
                    pe.wait_ge(newton_done, k + mi)
                    mm(NB[:, :], ones, sq[0][:, :], True, True).then_inc(sum_done, 1)

                def scores(r):
                    if r == 0:
                        pe.wait_ge(acc_freed, 2 * w0 - 17)
                    if not (isinstance(n, int) and n == 1 and r == 0):
                        pe.wait_ge(s_freed, 4 * m + r)
                    s = slice(P * r, P * r + P)
                    mm(G[2][:, :], q_n[q][0][:, s], k_t[:, q, :], True, True)
                    mm(G[3][:, 0:P], q_n[q][1][:, s], k_t[:, 2 + q, s], True, True)
                    mm(G[3][:, P:2 * P], q_n[q][2][:, s], k_t[:, 4 + q, s], True, True).then_inc(qk_done, 1)

                def turn(r):
                    pe.wait_ge(p_ready, 4 * m + r + 1)
                    if r == 2 and project:
                        pe.wait_ge(ada_out, n + S_B)
                    for b in range(6):
                        bank = T0[:, P * b:P * b + P] if b < 4 else T1[:, P * (b - 4):P * (b - 3)]
                        turned = nc.tensor.transpose(bank, s_b[:, P * b:P * b + P], ident)
                    turned.then_inc(turn_done, 1)

                if attend:
                    scores(0)
                if project:
                    piece(0)
                elif attend:
                    early_output(0, (0, 4, 1, 5), 6)
                if prior:
                    values(m - 1, p, 3)
                for r in range(4):
                    if attend:
                        turn(r)
                        if r < 3:
                            scores(r + 1)
                    if project and r < 3:
                        squares(r)
                        piece(r + 1)
                    if project and r == 1:
                        if attend:
                            pe.wait_ge(pt_dve, 4 * m + 2)
                        ada_sum_up(n + (S_B - 1), T1[:, 256:258])
                    if attend and r < 3:
                        if r == 0 and prior:
                            pe.wait_ge(head_out, m)
                        values(m, q, r)
                    if not project and r == 0:
                        early_output(0, (2, 6), 6)
                    if not project and r == 1:
                        early_output(1, (0, 4, 1, 5), 6)
                    if not project and r == 2:
                        early_output(1, (2, 6, 3), 7)
                        early_output(0, (3,), 7)

            def values(m, q, r):
                pe.wait_ge(pt_act, 4 * m + r + 1)
                pe.wait_ge(pt_dve, 4 * m + r + 1)
                for b in range(6):
                    block_v, g = (b, 0) if b < 4 else (r, b - 3)
                    last = mm(AD[:, P * r:P * r + P], v_b[:, block_v, P * (2 * g + q):P * (2 * g + q + 1)], p_t[:, P * b:P * b + P],
                              b == 0, b == 5)
                last.then_inc(pv_done, 1)

            def yb_lo_of(kt):
                return yb_lo[:, kt, :]

            def early_output(half, kts, heads):
                chunk_ready(*divmod(W_OUTB, 2))
                pe.wait_ge(acc_freed, 2 * W_OUTB + half - 17)
                pe.wait_ge(yblo_done, heads)
                columns(G[half][:, :], W_OUTB % 2, half, KT, yb_hi, yb_lo_of, kts)

            head(0, 0, False, True, False)
            head(1, 1, True, True, False)
            head(2, 0, True, True, True)
            with pe.Fori(2, QH // 2) as i:
                head(2 * i - 1, 1, True, True, True)
                head(2 * i, 0, True, True, True)
            head(QH - 1, 1, True, True, True)
            head(QH, 0, True, False, True)
            values(QH - 1, 1, 3)

            def output(w0, hi, lo_kt, lo_made, rest, early, steps):
                late = tuple(kt for kt in range(KT) if kt not in early)
                for c, kts in ((1, early), (0, rest), (1, late), (2, range(KT)), (3, range(KT))):
                    w = w0 + c
                    chunk_ready(*divmod(w, 2))
                    if c == 0:
                        pe.wait_ge(lo_made, KT)
                    for half in range(2):
                        if c >= 2:
                            pe.wait_ge(acc_freed, 2 * w + half - 19)
                        last = columns(G[2 * (w % 2) + half][:, :], w % 2, half, KT, hi, lo_kt, kts)
                        if kts is not early:
                            last.then_inc(mm_done, 1)
                            if (c, half) in steps:
                                ada_sum_up(steps[c, half])

            pe.wait_ge(s_freed, 4 * QH)
            output(W_OUTB, yb_hi, yb_lo_of, yblo_done, (7,), (0, 4), {(0, 0): S_OUTB - 1, (2, 0): S_OUTB})
            ada_sum_up(S_END - 1)
            add_squares(2, N_X2)

            pe.wait_ge(wflo_done, 1)
            chunk_ready(*divmod(W_Q2, 2))
            pe.wait_ge(acc_freed, 2 * W_Q2 - 17)
            for kt in range(KT):
                h_ready(3, kt)
                gates = split(T0[:, :], lambda kt: (wf_hi[:, kt, :], wf_lo[:, kt, :], h_hi[:, kt, :], h_lo[:, kt, :]), KT, (kt,))
                last = columns(G[0][:, :], W_Q2 % 2, 0, KT, h_hi, h_lo_of, (kt,))
            gates.then_inc(fg_done, 1)
            last.then_inc(mm_done, 1)

            def scores2(n):
                a, u = divmod(n, 12)
                kind, qb = UNITS2[u]
                before, first = s_reads(u)
                for e in range(2 if kind == 2 else 1):
                    if 16 * a + before + e >= 2:
                        pe.wait_ge(s2_freed, 16 * a + before + e - 1)
                    half = slice(64 * e, 64 * e + 64) if kind == 2 else slice(64 * kind, 64 * kind + 64)
                    qt, kt_ = (qk[a % 2][2], qk[a % 2][3]) if kind == 2 else (qk[a % 2][0], qk[a % 2][1])
                    score = mm(G[2 + (first + e) % 2][:, 0:(qb + 1) * P], qt[half, P * qb:P * qb + P], kt_[half, 0:(qb + 1) * P], True, True)
                score.then_inc(qk2_done, 1)

            def turn2(n):
                pe.wait_ge(p2_ready, n + 1)
                ge(pe, pt2_done, n)
                for b in range(UNITS2[n % 12][1] + 1):
                    turned = nc.tensor.transpose(T0[:, P * b:P * b + P], s_2[n % 3][:, 0, P * b:P * b + P], ident)
                turned.then_inc(turn2_done, 1)

            def values2(n):
                a, u = divmod(n, 12)
                kind, qb = UNITS2[u]
                pe.wait_ge(pt2_done, n + 1)
                if u == 1:
                    pe.wait_ge(mlo_done, 2 * a - 1) if a >= 1 else pe.wait_ge(ada_out, S_END)
                if u == 0:
                    pe.wait_ge(acc_freed, 2 * (W_Q2 + 3 * a) - 10)
                    ge(pe, d_done, a)
                for b in range(qb + 1):
                    pt = pt_2[n % 2][:, P * b:P * b + P]
                    if kind == 2:
                        out, vt = T1[:, P * qb:P * qb + P], v_2[a % 2][:, b, P:2 * P]
                    else:
                        out, vt = AD[64 * kind:64 * kind + 64, P * qb:P * qb + P], v_2[a % 2][:, b, 64 * kind:64 * kind + 64]
                    last = mm(out, vt, pt, b == 0, b == qb)
                last.then_inc(pv2_done, 1)

            def head_squares(k, lhs):
                pe.wait_ge(qsq_ready, k - N_2 + 31)
                pe.wait_ge(newton_done, k)
                mm(NB[:, :], lhs, sq[k % 2][:, :], True, True).then_inc(sum_done, 1)

            def spread(n):
                ge(pe, c_row_ready, n - 1)
                mm((T0, T1)[n % 2][:, :], ident[0:8, n:n + 1].broadcast_to([8, P]), cum[:, :], True, True).then_inc(c_spread, 1)

            def m_lo_of(kt):
                return m_lo[:, kt, :]

            for t in range(5):
                w0 = W_Q2 + 3 * t
                a = t - 1
                attend, project = t >= 1, t < 4
                for u in range(12):
                    n = 12 * a + u
                    if attend:
                        if u == 0:
                            pe.wait_ge(acc_freed, 2 * w0 - 18)
                        scores2(n)
                        if n == 2:
                            pe.wait_ge(c_row_ready, GROUPS)
                        if n >= 2:
                            turn2(n - 2)
                        if n >= 3:
                            values2(n - 3)
                    if t == 0 and u == 4:
                        pe.wait_ge(fgate_dve, 4)
                        for b in range(TB):
                            turned = nc.tensor.transpose(T1[:, 8 * b:8 * b + 8], cum[:, P * b:P * b + P], ident[0:8, 0:8])
                        turned.then_inc(c_turned, 1)
                    if t == 0 and u >= 5:
                        if u == 5:
                            pe.wait_ge(c_col_ready, 1)
                        spread(u - 5)
                    if t > 0 and project and u in (2, 4, 6, 8):
                        head_squares(norm2(t, u // 2 - 1), half_ones)
                    if project and (t > 0 or u >= 2):
                        mi, w = u // 2, w0 + u // 4
                        par = w % 2
                        if u % 4 == 0:
                            pe.wait_ge(lo_done, w + 1)
                        if u == 10 or (u % 2 == 0 and mi < 5):
                            pe.wait_ge(acc_freed, 2 * w0 + mi - 17)
                        if mi < 4:
                            last = columns(G[mi % 2][:, :], par, mi % 2, KT, h_hi, h_lo_of, range(4 * (u % 2), 4 * (u % 2) + 4))
                        else:
                            last = rows(G[mi % 2][:, 256 * (u % 2):256 * (u % 2) + 256], par, u - 8, 0, 256)
                        if u % 2 == 1:
                            last.then_inc(mm_done, 1)
                    if t == 0 and u in (2, 4, 6, 8):
                        head_squares(norm2(t, u // 2 - 1), half_ones)
                    if t == 4:
                        half = u % 2
                        if u < 2:
                            pe.wait_ge(lo_done, W_OUT2 + 1)
                            pe.wait_ge(acc_freed, 2 * W_OUT2 + half - 17)
                        pe.wait_ge(mlo_done, 4 if u < 8 else 6)
                        columns(G[half][:, :], W_OUT2 % 2, half, KT, m_hi, m_lo_of, ((0, 4, 1, 5, 2, 6)[u // 2],))
                    if a >= 1 and u == 0:
                        head_squares(norm_d(a - 1), ones)
                if t == 0:
                    spread(7)
            turn2(46)
            values2(45)
            turn2(47)
            head_squares(norm_d(3), ones)
            values2(46)
            values2(47)

            pe.wait_ge(s2_freed, 64)
            output(W_OUT2, m_hi, m_lo_of, mlo_done, (3, 7), (0, 4, 1, 5), {})
            add_squares(3, N_X3)

            def gate_up(u, pars=range(2)):
                for par in pars:
                    chunk_ready(u, par)
                    for half in range(2):
                        pe.wait_ge(acc_freed, 4 * u + 2 * par + half - 19)
                        columns(G[2 * par + half][:, :], par, half, KT, h_hi, h_lo_of).then_inc(mm_done, 1)

            def gu_lo_of(kt):
                return gu_lo[:, kt, :]

            first_chunk(4, W_GU1, G, h_hi, h_lo_of, 2 * W_GU1 - 19)
            gate_up(W_GU1 // 2, (1,))
            with pe.Fori(W_GU1 // 2 + 1, W_DN1 // 2) as u:
                gate_up(u)

            def down(u, first=False):
                for par in range(2):
                    chunk_ready(u, par)
                    pe.wait_ge(acc_freed, 4 * u + 2 * par - 18)
                    for piece in (range(FF1 - 2), range(FF1 - 2, FF1)):
                        if first and par == 0:
                            pe.wait_ge(gulo_done, piece[-1] + 1)
                        last = columns(G[2 * par][:, :], par, 0, FF1, gu_hi, gu_lo_of, piece)
                    last.then_inc(mm_done, 2)

            down(W_DN1 // 2, True)
            with pe.Fori(W_DN1 // 2 + 1, W_GU2 // 2) as u:
                down(u)
            with pe.Fori(W_GU2 // 2, W_DN2 // 2) as u:
                gate_up(u)
            for w in range(W_DN2, W_END):
                chunk_ready(*divmod(w, 2))
                for half in range(2):
                    pe.wait_ge(acc_freed, 2 * w + half - 19)
                for piece in (range(FF2 - 2), range(FF2 - 2, FF2)) if w == W_DN2 else (range(FF2),):
                    if w == W_DN2:
                        pe.wait_ge(gulo_done, FF1 + piece[-1] + 1)
                    for half in range(2):
                        last = columns(G[2 * (w % 2) + half][:, :], w % 2, half, FF2, gu_hi, gu_lo_of, piece)
                        if piece[-1] == FF2 - 1:
                            last.then_inc(mm_done, 1)


INPUTS = ["a_b_spatial", "diff_lam_2", "b_f_2"]


def layout(inputs):
    src = {name: np.asarray(a) for name, a in inputs.items()}

    def kn(w):
        return w.reshape(-1, P, w.shape[1]).transpose(1, 0, 2)

    w_in_a, w_out_a, w_kv = kn(src["a_w_in"][0]), kn(src["a_w_out"][0]), kn(src["w_kv"])
    w_in_b, w_out_b = kn(src["b_w_in"][0]), kn(src["b_w_out"][0])
    w_in_2, w_out_2 = kn(src["w_in_2"][0]), kn(src["w_out_2"][0])
    w_gate, w_up, w_down = kn(src["w_gate_2"][0]), kn(src["w_up_2"][0]), kn(src["w_down_2"][0])
    chunks = []

    def span(w, lo, n=256):
        chunks.append([w[:, :, lo:lo + n]])

    def pair(wa, a, wb, b):
        chunks.append([wa[:, :, a:a + P], wb[:, :, b:b + P]])

    def gate_up(first, n):
        for f in range(first, first + n):
            pair(w_gate, P * f, w_up, P * f)

    for n in range(8):
        span(w_in_a, AW + 256 * n)
    for j in range(AT):
        pair(w_in_a, P * j, w_in_a, 2 * AW + P * j)
    for m in range(KT):
        span(w_out_a, P * m, P)
    for c in range(NKV // 2):
        span(w_kv, 256 * c)
        span(w_kv, NKV * P + 256 * c)
    for n in range(QH):
        col = P * (n // 2) + 4 * P * (n % 2)
        pair(w_in_b, col, w_in_b, col + DM)
        pair(w_in_b, col + 2 * DM, w_in_b, col + 3 * DM)
    for c in range(4):
        span(w_out_b, 256 * c)
    for t in range(4):
        fox, dif = P * t, 1544 + P * t
        pair(w_in_2, fox, w_in_2, fox + 512)
        pair(w_in_2, dif, w_in_2, dif + 512)
        pair(w_in_2, fox + 1024, w_in_2, dif + 1024)
    for c in range(4):
        span(w_out_2, 256 * c)
    gate_up(0, FF1)
    for m in range(KT):
        span(w_down[:, 0:FF1], P * m, P)
    gate_up(FF1, FF2)
    for c in range(4):
        span(w_down[:, FF1:], 256 * c)
    weights = np.zeros((W_END, P, 2048), np.float32)
    for w, parts in enumerate(chunks):
        tile = np.concatenate(parts, axis=2)
        weights[w, :, 0:tile.shape[1] * tile.shape[2]] = tile.reshape(P, -1)

    mod_weights = {"a": kn(src["a_ada_w"][0]), "kv": kn(src["kv_ada_w"]), "b": kn(src["b_ada_w"][0]), "2": kn(src["w_ada_2"][0])}
    mod_biases = {"a": src["a_ada_b"][0], "kv": src["kv_ada_b"], "b": src["b_ada_b"][0], "2": src["b_ada_2"][0]}
    ada = [mod_weights[name][:, :, 256 * s:256 * s + 256].reshape(P, 2048) for name, lo, n in MODS for s in range(lo, lo + n)]
    rows = [src[name].reshape(-1, P) for name in ("c", "c_2", "a_norm_g", "kv_norm_g", "b_norm_g", "ln1_g_2", "ln2_g_2", "a_sgu_g",
                                                  "k_norm_g", "b_q_norm_g", "diff_norm_g_2")]
    rows += [np.concatenate([src[name][0]] * 2, axis=1) for name in ("fox_qk_g_2", "diff_qk_g_2")]
    rows += [mod_biases[name].reshape(-1, P)[2 * lo:2 * lo + 2 * n] for name, lo, n in MODS]
    tiles, blocks = constants()
    arrays = {name: src[name] for name in INPUTS}
    arrays.update(weights=weights, ada=np.stack(ada), vecs=np.concatenate(rows, axis=0).T, tiles=tiles, blocks=blocks,
                  x=src["x"][0].T.reshape(KT, P, TOK).transpose(1, 0, 2),
                  spatial=src["a_w_spatial"][0].transpose(2, 0, 1), forget=w_in_2[:, :, 1536:1544])
    return {f"in_{name}": np.ascontiguousarray(a) for name, a in arrays.items()}


def kernel(**inputs):
    from concourse import bacc
    from concourse.bass_utils import run_bass_kernel_spmd

    nc = bacc.Bacc("TRN2", target_bir_lowering=False, num_devices=1)
    arrays = layout(inputs)
    d = {n[3:]: nc.dram_tensor(n, a.shape, mybir.dt.from_np(a.dtype), kind="ExternalInput").ap() for n, a in arrays.items()}
    d["out"] = nc.dram_tensor("out", (P, KT, TOK), F32, kind="ExternalOutput").ap()
    program(nc, d)
    run = run_bass_kernel_spmd(nc, [arrays], core_ids=[0])
    return np.ascontiguousarray(run.results[0]["out"].transpose(2, 1, 0)).reshape(1, TOK, DM)
```
